# Optimizing a Trainium2 kernel written in Bass

```python
import jax, jax.numpy as jnp
from jax import lax
import numpy as np

D_MODEL = 1024
BATCH = 1
SEQ = 1024
DEPTH = 1

GRID_W = 64
CTX_LEN = 256
HGRN_HEADS = 4
HGRN_KEY = 128
HGRN_VAL = 128
HGRN_KDIM = HGRN_HEADS * HGRN_KEY
HGRN_WIDTH = HGRN_HEADS * HGRN_VAL
CONV_WIDTH = D_MODEL - HGRN_WIDTH
CONV_KERNEL = 31
CONV_PAD = CONV_KERNEL // 2
CHUNK = 64
D_FF = (((8 * D_MODEL + 2) // 3 + 255) // 256) * 256
N_MOD = 6
EPS = 1e-6
F_MIN = 1e-30
PROJ_SIZES = (HGRN_KDIM, HGRN_KDIM, HGRN_KDIM, HGRN_WIDTH, HGRN_WIDTH, CONV_WIDTH, CONV_WIDTH)
D_IN = sum(PROJ_SIZES)

kernel_name = "hybrid_hgrn2_conformer_dit_block"

def rms_norm(x, g):
    xf = x.astype(jnp.float32)
    y = xf * lax.rsqrt(jnp.mean(xf * xf, axis=-1, keepdims=True) + EPS)
    return (y * g.astype(jnp.float32)).astype(x.dtype)

def layer_norm(x, g, b):
    xf = x.astype(jnp.float32)
    mu = jnp.mean(xf, axis=-1, keepdims=True)
    var = jnp.mean(jnp.square(xf - mu), axis=-1, keepdims=True)
    y = (xf - mu) * lax.rsqrt(var + EPS)
    return (y * g.astype(jnp.float32) + b.astype(jnp.float32)).astype(x.dtype)

def modulate(x, gain, shift, scale):
    return rms_norm(x, gain) * (1 + scale) + shift

def split_proj(p):
    return jnp.split(p, list(np.cumsum(PROJ_SIZES)[:-1]), axis=-1)

def lower_bound(P, l):
    p = jax.nn.softmax(P.astype(jnp.float32), axis=0)
    return (jnp.cumsum(p, axis=0) - p[0])[l]

def forget_gate(pre, lb):
    s = jax.nn.sigmoid(pre.astype(jnp.float32))
    f = lb + (1 - lb) * s
    one_minus_f = (1 - lb) * (1 - s)
    return one_minus_f, jnp.log(jnp.maximum(f, F_MIN))

def hgrn_inputs(p, lb_f, lb_b):
    B, L = p[0].shape[:2]
    heads = lambda t, d: t.astype(jnp.float32).reshape(B, L, HGRN_HEADS, d)
    q = heads(p[0], HGRN_KEY) * (HGRN_KEY ** -0.5)
    k_f, lf_f = forget_gate(p[1], lb_f)
    k_b, lf_b = forget_gate(p[2], lb_b)
    v = heads(p[3], HGRN_VAL)
    return (q, heads(k_f, HGRN_KEY), heads(k_b, HGRN_KEY), v,
            heads(lf_f, HGRN_KEY), heads(lf_b, HGRN_KEY))

def gla_scan(q, k, v, logf, s0):
    B, L, H, _ = q.shape
    V = v.shape[-1]
    n = L // CHUNK
    to_chunks = lambda t: t.reshape(B, n, CHUNK, H, t.shape[-1]).transpose(1, 0, 3, 2, 4)
    mask = jnp.tril(jnp.ones((CHUNK, CHUNK), bool))[:, :, None]

    def step(S, inp):
        qc, kc, vc, gc = inp
        b = jnp.cumsum(gc, axis=2)
        o_inter = jnp.einsum('bhtk,bhkv->bhtv', qc * jnp.exp(b), S)
        diff = b[:, :, :, None, :] - b[:, :, None, :, :]
        decay = jnp.where(mask, jnp.exp(jnp.where(mask, diff, 0.0)), 0.0)
        A = jnp.einsum('bhtk,bhtsk,bhsk->bhts', qc, decay, kc)
        o = o_inter + jnp.einsum('bhts,bhsv->bhtv', A, vc)
        b_last = b[:, :, -1:, :]
        S_new = (jnp.exp(b_last[:, :, 0, :])[..., None] * S
                 + jnp.einsum('bhsk,bhsv->bhkv', kc * jnp.exp(b_last - b), vc))
        return S_new, o

    S, o = lax.scan(step, s0, (to_chunks(q), to_chunks(k), to_chunks(v), to_chunks(logf)))
    o = o.transpose(1, 0, 3, 2, 4).reshape(B, L, H, V)
    return o, S

def hgrn_bidir(q, k_f, k_b, v, lf_f, lf_b, s0_f, s0_b):
    flip = lambda t: jnp.flip(t, axis=1)
    o_f, s_f = gla_scan(q, k_f, v, lf_f, s0_f)
    o_b, s_b = gla_scan(flip(q), flip(k_b), flip(v), flip(lf_b), s0_b)
    return o_f + flip(o_b), s_f, s_b

def hgrn_readout(o, p_g, onorm_g):
    B, L = o.shape[:2]
    y = o * lax.rsqrt(jnp.mean(o * o, axis=-1, keepdims=True) + EPS) * onorm_g.astype(jnp.float32)
    y = y.reshape(B, L, HGRN_WIDTH) * jax.nn.silu(p_g.astype(jnp.float32))
    return y.astype(p_g.dtype)

def conv_branch(p_a, p_b, dw_w, dw_b, ln_g, ln_b, rows):
    u = p_a * jax.nn.sigmoid(p_b)
    B, L, C = u.shape
    seqs = u.reshape(B * rows, L // rows, C)
    y = lax.conv_general_dilated(seqs, dw_w.reshape(CONV_KERNEL, 1, C).astype(u.dtype),
                                 window_strides=(1,), padding=[(CONV_PAD, CONV_PAD)],
                                 dimension_numbers=('NWC', 'WIO', 'NWC'),
                                 feature_group_count=C)
    y = y.reshape(B, L, C) + dw_b
    return jax.nn.silu(layer_norm(y, ln_g, ln_b))

def mixer_output(o, p, rows, w_out, onorm_g, dw_w, dw_b, ln_g, ln_b):
    a = hgrn_readout(o, p[4], onorm_g)
    b = conv_branch(p[5], p[6], dw_w, dw_b, ln_g, ln_b, rows)
    return jnp.concatenate([a, b], axis=-1) @ w_out

def swiglu(h, wg, wu, wd):
    return (jax.nn.silu(h @ wg) * (h @ wu)) @ wd

def setup_inputs(seed: int = 0) -> dict:
    key = jax.random.key(seed)
    ks = jax.random.split(key, 24)
    f32 = jnp.float32
    nrm = lambda k, shape, s: jax.random.normal(k, shape, f32) * s
    gain = lambda k, shape: 1.0 + 0.05 * jax.random.normal(k, shape, f32)
    return {
        "x": nrm(ks[0], (BATCH, SEQ, D_MODEL), 1.0),
        "c": nrm(ks[1], (BATCH, D_MODEL), 1.0),
        "ctx": nrm(ks[2], (BATCH, CTX_LEN, D_MODEL), 1.0),
        "c_ctx": nrm(ks[3], (D_MODEL,), 1.0),
        "w_mod": nrm(ks[4], (DEPTH, D_MODEL, N_MOD * D_MODEL), 0.5 * D_MODEL ** -0.5),
        "b_mod": nrm(ks[5], (DEPTH, N_MOD * D_MODEL), 0.02),
        "pre_mix_g": gain(ks[6], (DEPTH, D_MODEL)),
        "post_mix_g": gain(ks[7], (DEPTH, D_MODEL)),
        "pre_ffn_g": gain(ks[8], (DEPTH, D_MODEL)),
        "post_ffn_g": gain(ks[9], (DEPTH, D_MODEL)),
        "w_in": nrm(ks[10], (DEPTH, D_MODEL, D_IN), D_MODEL ** -0.5),
        "w_out": nrm(ks[11], (DEPTH, D_MODEL, D_MODEL), D_MODEL ** -0.5),
        "hgrn_lb_fwd": nrm(ks[12], (DEPTH, HGRN_KDIM), 1.0),
        "hgrn_lb_bwd": nrm(ks[13], (DEPTH, HGRN_KDIM), 1.0),
        "hgrn_onorm_g": gain(ks[14], (DEPTH, HGRN_VAL)),
        "conv_dw_w": nrm(ks[15], (DEPTH, CONV_KERNEL, CONV_WIDTH), CONV_KERNEL ** -0.5),
        "conv_dw_b": nrm(ks[16], (DEPTH, CONV_WIDTH), 0.02),
        "conv_ln_g": gain(ks[17], (DEPTH, CONV_WIDTH)),
        "conv_ln_b": nrm(ks[18], (DEPTH, CONV_WIDTH), 0.02),
        "ffn_w_gate": nrm(ks[19], (DEPTH, D_MODEL, D_FF), D_MODEL ** -0.5),
        "ffn_w_up": nrm(ks[20], (DEPTH, D_MODEL, D_FF), D_MODEL ** -0.5),
        "ffn_w_down": nrm(ks[21], (DEPTH, D_FF, D_MODEL), D_FF ** -0.5),
    }

def reference(x, c, ctx, c_ctx, w_mod, b_mod, pre_mix_g, post_mix_g, pre_ffn_g, post_ffn_g,
              w_in, w_out, hgrn_lb_fwd, hgrn_lb_bwd, hgrn_onorm_g, conv_dw_w, conv_dw_b,
              conv_ln_g, conv_ln_b, ffn_w_gate, ffn_w_up, ffn_w_down):
    B, L, _ = x.shape
    rows = L // GRID_W
    zero_state = jnp.zeros((B, HGRN_HEADS, HGRN_KEY, HGRN_VAL), jnp.float32)
    sc = jax.nn.silu(c)
    scc = jax.nn.silu(c_ctx)[None]
    xc = ctx
    for l in range(DEPTH):
        last = l == DEPTH - 1
        mx = jnp.split((sc @ w_mod[l] + b_mod[l])[:, None, :], N_MOD, axis=-1)
        mc = jnp.split((scc @ w_mod[l] + b_mod[l])[:, None, :], N_MOD, axis=-1)
        lb_f = lower_bound(hgrn_lb_fwd, l)
        lb_b = lower_bound(hgrn_lb_bwd, l)

        px = split_proj(modulate(x, pre_mix_g[l], mx[0], mx[1]) @ w_in[l])
        pc = split_proj(modulate(xc, pre_mix_g[l], mc[0], mc[1]) @ w_in[l])
        oc, s_f, s_b = hgrn_bidir(*hgrn_inputs(pc, lb_f, lb_b), zero_state, zero_state)
        ox, _, _ = hgrn_bidir(*hgrn_inputs(px, lb_f, lb_b), s_f, s_b)
        mix_x = mixer_output(ox, px, rows, w_out[l], hgrn_onorm_g[l], conv_dw_w[l],
                             conv_dw_b[l], conv_ln_g[l], conv_ln_b[l])
        x = x + mx[2] * rms_norm(mix_x, post_mix_g[l])

        hx = swiglu(modulate(x, pre_ffn_g[l], mx[3], mx[4]), ffn_w_gate[l], ffn_w_up[l], ffn_w_down[l])
        x = x + mx[5] * rms_norm(hx, post_ffn_g[l])

        if not last:
            mix_c = mixer_output(oc, pc, 1, w_out[l], hgrn_onorm_g[l], conv_dw_w[l],
                                 conv_dw_b[l], conv_ln_g[l], conv_ln_b[l])
            xc = xc + mc[2] * rms_norm(mix_c, post_mix_g[l])
            hc = swiglu(modulate(xc, pre_ffn_g[l], mc[3], mc[4]), ffn_w_gate[l], ffn_w_up[l], ffn_w_down[l])
            xc = xc + mc[5] * rms_norm(hc, post_ffn_g[l])
    return x


_drawn_inputs = setup_inputs


def setup_inputs(seed=0):
    import zlib

    import numpy as np

    out = dict(_drawn_inputs(seed))
    spreads = {}
    factors = {'ctx': 8.0,
     'c_ctx': 8.0,
     'post_mix_g': 3.716,
     'pre_ffn_g': 2.999,
     'post_ffn_g': 3.787,
     'hgrn_onorm_g': 5.134,
     'conv_dw_b': 7.192,
     'conv_ln_g': 4.607,
     'conv_ln_b': 21.7}
    for name, (base, spread) in spreads.items():
        noise = np.random.default_rng([zlib.crc32(name.encode()), seed]).standard_normal(out[name].shape)
        drawn = base * np.exp(spread * noise) if base else spread * noise
        out[name] = __import__('jax').numpy.asarray(drawn.astype(out[name].dtype))
    for name, factor in factors.items():
        out[name] = (out[name] * factor).astype(out[name].dtype)
    return out
```

```python
from contextlib import ExitStack

import numpy as np

import concourse.bass as bass
from concourse import mybir

F32 = mybir.dt.float32
F32R = mybir.dt.float32r
U8 = mybir.dt.uint8
ALU = mybir.AluOpType
ACT = mybir.ActivationFunctionType

P = 128
DM = 1024
KT = DM // P
SEQ = 1024
CTX = 256
TOK = CTX + SEQ
XT, CT = SEQ // P, CTX // P
NT = XT + CT
HEADS = 4
GRID = 64
ROWS = SEQ // GRID
TAPS = 31
PAD = TAPS // 2
DFF = 2816
FT = DFF // P
EPS = 1e-6
F_MIN = 1e-30
BANK = 512
LEVELS = 7

R_C, R_CC, R_BM, R_PREM, R_PREF, R_POSTM, R_POSTF, R_LBF, R_LBB, R_DWB, R_LNG, R_LNB, R_ON = (
    0, 8, 16, 64, 72, 80, 88, 96, 100, 104, 108, 112, 116)
NVEC = 117

TILES = [("ff", 512), ("fb", 1024), ("q", 0), ("g", 2048), ("b", 3072), ("a", 2560), ("v", 1536)]
NTILE = len(TILES)
UNITS = [(p, kind, n) for p, (kind, _) in enumerate(TILES)
         for n in range(3 if kind in ("ff", "fb", "v") else 2)]
NUNIT = len(UNITS)
GRING = 3
GEMM_BY = ["dve" if k in ("g", "a") else "act" for _, k, _ in UNITS]

SCAN = 3
USES = [("level", l, hf) for l in range(LEVELS + 1) for hf in range(2)]
_scan = [[("turn", g, d) for d in range(2)] for g in range(SCAN)], [[("outer", g, d) for d in range(2)] for g in range(SCAN)]
USES += _scan[0][0]
for _g in range(SCAN):
    USES += _scan[1][_g]
    if _g + 1 < SCAN:
        USES += _scan[0][_g + 1]
USES += [("o", 0, 0), ("o", 1, 0), ("ssq", 0, 0), ("rb", 0, 0), ("rb", 1, 0)]
NUSE = len(USES)
LRING, LBASE = 5, 3
USE_BY = ["act" if u[0] in ("turn", "ssq") or u[:2] == ("level", 0) else "dve" for u in USES]


def ordinal(by, i):
    return by[:i].count(by[i])


def ring_wait(by, ring, i):
    n = len(by)
    j = i - ring if i >= ring else max(k for k in range(n) if k % ring == i % ring)
    return by[j], ordinal(by, j), 0 if i >= ring else 1


PE_STEPS = [[] for _ in UNITS]
for _i, _u in enumerate(USES):
    _at = {"level": _u[1], "turn": 8 + _u[1], "outer": 9 + _u[1], "o": 12, "ssq": 13, "rb": 14}[_u[0]]
    PE_STEPS[_at].append(_i)

N_GACT, N_GDVE = GEMM_BY.count("act"), GEMM_BY.count("dve")
N_UACT, N_UDVE = USE_BY.count("act"), USE_BY.count("dve")
NK = LEVELS + 1
NSTATE = 2 * 3 * SCAN
LN_STEPS = 18
BODY_STEPS = 40
NGROUP = FT // 2


def scan_chunk(d, n):
    if d == 0:
        return n
    return CT - 1 - n if n < CT else NT - 1 - (n - CT)


def last_unit(p):
    return max(u for u, (q, _, _) in enumerate(UNITS) if q == p)


def kernel_program(nc, x, c, ctx, c_ctx, w_mod, b_mod, pre_mix_g, post_mix_g, pre_ffn_g,
                   post_ffn_g, w_in, w_out, hgrn_lb_fwd, hgrn_lb_bwd, hgrn_onorm_g, conv_dw_w,
                   conv_dw_b, conv_ln_g, conv_ln_b, ffn_w_gate, ffn_w_up, ffn_w_down,
                   ident_in, masks_in, out):
    with ExitStack() as es:
        free = [(nc.sbuf_base + 31) // 32 * 32]
        spot = {}

        def sb(name, shape, dt=F32, offset=None):
            if offset is None:
                offset = free[0]
                free[0] += (int(np.prod(shape[1:])) * (1 if dt == U8 else 4) + 31) // 32 * 32
            spot[name] = offset
            return nc.alloc_sbuf_tensor_at(name, shape, dt, offset=offset)

        RAW = 3
        raw = sb("raw", [P, RAW, DM])
        split = sb("split", [P, 2, 2, DM], F32R)
        ident = sb("ident", [P, P])
        masks = sb("masks", [P, LEVELS, P], U8)
        vec = sb("vec", [P, NVEC])
        taps = sb("taps", [P, 4, TAPS])
        mod = sb("mod", [P, 6, KT, 2])
        gain = sb("gain", [P, KT, 2])
        gain2 = sb("gain2", [P, KT])
        gate = sb("gate", [P, 2, KT])
        silc = sb("silc", [P, KT, 2])
        silt = sb("silt", [P, 2, KT])
        lb = sb("lb", [P, 3, 8])
        lbt = sb("lbt", [P, 3, 8])
        ones = sb("ones", [P, P])
        eps = sb("eps", [P, 1])
        ss = sb("ss", [P, 2, NT])
        rr = sb("rr", [P, 2, NT])
        hss = sb("hss", [P, 2, XT])

        hT = sb("hT", [P, 2, KT, TOK], F32R)
        A0 = spot["hT"]
        cat = sb("cat", [P, 8, SEQ])
        W0 = free[0]
        F = sb("F", [P, 2, TOK])
        K = sb("K", [P, 2, TOK])
        Q = sb("Q", [P, 2, SEQ])
        qraw = sb("qraw", [P, SEQ])
        T = sb("T", [P, 2, TOK // 2])
        V = sb("V", [P, NT, P])
        AT = sb("AT", [P, SEQ])
        S = sb("S", [P, 2, XT, P])
        KC = sb("KC", [P, SEQ], offset=spot["S"])
        KTok = sb("KTok", [P, 2, 3, P])
        U = sb("U", [P, SEQ])
        assert free[0] <= nc.sbuf_usable_end, (free[0], nc.sbuf_usable_end)

        xst = sb("xst", [P, NT, DM], offset=W0)
        xfull = sb("xfull", [P, 2, KT, P], offset=W0 + 40960)
        vrow = sb("vrow", [P, P], offset=W0 + 49152)
        trow = sb("trow", [P, 4 * P], offset=W0 + 49152 + 512)
        junk = sb("junk", [P, DM], offset=W0 + 49152 + 2560)
        mask32 = sb("mask32", [P, LEVELS, P], offset=W0 + 49152 + 2560 + 4096)
        mraw = sb("mraw", [P, 8, DM], offset=spot["cat"])
        XT0 = A0 + 65536
        catS = sb("catS", [P, 2, 2, KT, BANK], F32R, offset=A0)
        Gb = sb("Gb", [P, DM], offset=XT0)
        x1t = sb("x1t", [P, 3, DM], offset=XT0 + 4096)
        rstd = sb("rstd", [P, SEQ], offset=XT0 + 4096)
        lnsg = sb("lnsg", [P, 2, SEQ], offset=XT0 + 8192)
        woA = sb("woA", [P, 6, 2, DM], F32R, offset=W0)
        mixt = sb("mixt", [P, DM], offset=W0 + 49152)
        vtmp = sb("vtmp", [P, 2, BANK], offset=W0 + 49152)
        x2t = sb("x2t", [P, KT, P], offset=W0 + 53248)
        h2f = sb("h2f", [P, KT, P], offset=W0 + 57344)
        h2T = [sb("h2Ta", [P, 2, KT, BANK], F32R, offset=spot["cat"]),
               sb("h2Tb", [P, 2, KT, BANK], F32R, offset=A0)]
        y = sb("y", [P, XT, DM], offset=A0 + 32768)
        sgm = sb("sgm", [P, 2, BANK], offset=XT0 + 4096)
        slotX = sb("slotX", [P, 2, DM], F32R, offset=XT0 + 8192)
        mid = sb("mid", [P, 2, 2, 2, SEQ], F32R, offset=W0)
        more = sb("more", [P, 3, 2, DM], F32R, offset=W0 + 32768)
        mid32 = sb("mid32", [P, 2, BANK], offset=W0 + 57344)
        xres = sb("xres", [P, 2, DM], offset=W0)
        junk2 = sb("junk2", [P, DM], offset=W0 + 8192)

        def wo_part(q, k):
            return woA[:, k, q] if k < 6 else split[:, k - 6, q]

        def ffn_part(q, j):
            return split[:, j, q] if j < 2 else (more[:, j - 2, q] if j < 5 else slotX[:, q])

        bank = [es.enter_context(nc.psum_tensor(f"bank{i}", [P, BANK], F32)) for i in range(8)]
        x1_dram = nc.dram_tensor("x1_scratch", [SEQ, DM], F32, kind="Internal").ap()

        def sem(name):
            return es.enter_context(nc.semaphore(name))

        small_in = sem("small_in")
        x_in = [sem(f"x_in{i}") for i in range(4)]
        mod_in = [sem(f"mod_in{i}") for i in range(8)]
        raw_in = [sem(f"raw_in{i}") for i in range(RAW)]
        x1_in = [sem(f"x1_in{i}") for i in range(3)]
        x1_store = [sem(f"x1_store{i}") for i in range(3)]
        res_in = [sem(f"res_in{i}") for i in range(2)]
        out_done = [sem(f"out_done{i}") for i in range(2)]
        pe_cols, cols_done, sil_sig, lb_exp = sem("pe_cols"), sem("cols_done"), sem("sil_sig"), sem("lb_exp")
        mod_full, mod_done = sem("mod_full"), sem("mod_done")
        x_root, xn_ready, xp_full, xp_free = sem("x_root"), sem("xn_ready"), sem("xp_full"), sem("xp_free")
        h_hi, h_lo = sem("h_hi"), sem("h_lo")
        w_hi, w_lo = sem("w_hi"), sem("w_lo")
        gemm_full, gemm_act, gemm_dve, g_sig = sem("gemm_full"), sem("gemm_act"), sem("gemm_dve"), sem("g_sig")
        use_full, use_act, use_dve = sem("use_full"), sem("use_act"), sem("use_dve")
        k_ready, kc_ready, q_ready = sem("k_ready"), sem("kc_ready"), sem("q_ready")
        state_done, sq_ready, rs_ready, conv_done = sem("state_done"), sem("sq_ready"), sem("rs_ready"), sem("conv_done")
        ln_pe, ln_act, ln_dve = sem("ln_pe"), sem("ln_act"), sem("ln_dve")
        cat_hi, cat_lo, o_hi, o_lo = sem("cat_hi"), sem("cat_lo"), sem("o_hi"), sem("o_lo")
        g_full, g_done = sem("g_full"), sem("g_done")
        mix_full, mix_root, mix_done, x1_root = sem("mix_full"), sem("mix_root"), sem("mix_done"), sem("x1_root")
        x2_ready, h2_full, h2_free, h2_hi, h2_lo = (sem("x2_ready"), sem("h2_full"), sem("h2_free"),
                                                    sem("h2_hi"), sem("h2_lo"))
        f_hi, f_lo = sem("f_hi"), sem("f_lo")
        gu_full, gu_sig, gu_free, mid_hi, mid_lo = (sem("gu_full"), sem("gu_sig"), sem("gu_free"),
                                                    sem("mid_hi"), sem("mid_lo"))
        down_full, down_free, gu_part = sem("down_full"), sem("down_free"), sem("gu_part")
        y_root, y_done = sem("y_root"), sem("y_done")
        dve_step, act_step = sem("dve_step"), sem("act_step")

        class Steps:

            def __init__(self, eng, s):
                self.eng, self.s, self.base, self.n = eng, s, 0, 0

            def __call__(self, ins):
                self.n += 1
                ins.then_inc(self.s, 1)
                return self.n

            def wait(self, n=None):
                self.eng.wait_ge(self.s, self.base + (self.n if n is None else n))

        def view(t, offset, dims):
            a = t[:]
            return bass.AP(a.tensor, a.offset + offset, [list(a.ap[0])] + [list(d) for d in dims])

        def first(s):
            return isinstance(s, int) and s == 0

        def cat_tile(i):
            return cat[:, bass.ds(i, 1), :].rearrange("p o n -> p (o n)")

        xf = x.rearrange("b (t p) d -> (b t) p d", p=P)
        cf = ctx.rearrange("b (t p) d -> (b t) p d", p=P)
        outf = out.rearrange("b (t p) d -> (b t) p d", p=P)
        wm = w_mod.rearrange("l (k p) (m n) -> (l m) k p n", p=P, m=6)
        win = w_in.rearrange("l (k p) n -> (l p) k n", p=P)
        wo = w_out.rearrange("l (k p) n -> (l k) p n", p=P)
        wg = ffn_w_gate.rearrange("l (k p) n -> (l p) k n", p=P)
        wu = ffn_w_up.rearrange("l (k p) n -> (l p) k n", p=P)
        wd = ffn_w_down.rearrange("l (k p) n -> (l k) p n", p=P)

        def rows(a):
            return a.rearrange("l (r n) -> (l r) n", n=P)

        small = [(R_C, rows(c)), (R_CC, c_ctx.rearrange("(r n) -> r n", n=P)), (R_BM, rows(b_mod)),
                 (R_PREM, rows(pre_mix_g)), (R_PREF, rows(pre_ffn_g)), (R_POSTM, rows(post_mix_g)),
                 (R_POSTF, rows(post_ffn_g)), (R_LBF, rows(hgrn_lb_fwd)), (R_LBB, rows(hgrn_lb_bwd)),
                 (R_DWB, rows(conv_dw_b)), (R_LNG, rows(conv_ln_g)), (R_LNB, rows(conv_ln_b)),
                 (R_ON, rows(hgrn_onorm_g))]
        n_small = len(small) + 3

        MODS = [1, 0, 2, 3, 4, 5]
        MOD_AT = [3, 6, 9, 12]

        def mod_slot(i):
            if i < 2 * KT:
                return i % 8, i // 8, i - 8
            j = (i - 2 * KT) % 4
            return 4 + j, 2 + (i - 2 * KT) // 4, (i - 4 if i >= 2 * KT + 4 else 2 * KT - 4 + j)

        SLOT_TILES = [[p for p in range(NTILE) if p % RAW == r] for r in range(RAW)]

        def head_fill(s, p):
            mine = SLOT_TILES[p % RAW]
            return s * len(mine) + (mine.index(p) + 1)

        def late_fill(i):
            return HEADS * len(SLOT_TILES[i % RAW]) + i // RAW + 1

        def ffn_rounds(eng, body):
            body(0, 0)
            body(1, 1)
            with eng.Fori(0, (NGROUP - 3) // 2) as r:
                body(r * 2 + 2, 0)
                body(r * 2 + 3, 1)
            body(NGROUP - 1, (NGROUP - 1) % 2)

        def gu_no(n, j):
            return j if first(n) else n * 6 + (j - 2)

        def down_no(n, j):
            if isinstance(n, int) and n == NGROUP - 1:
                return 6 * NGROUP - 2 + j
            return n * 6 + (8 + j)

        block = es.enter_context(nc.Block())

        @block.sync
        def _(sp):
            for r0, src in small:
                sp.dma_start(vrow[r0:r0 + src.shape[0], :], src).then_inc(small_in, 16)
            sp.dma_start(trow[0:TAPS, :], conv_dw_w.rearrange("l t n -> (l t) n")).then_inc(small_in, 16)
            sp.dma_start(ident[:], ident_in).then_inc(small_in, 16)
            sp.dma_start(mask32[:], masks_in).then_inc(small_in, 16)
            for t in range(NT):
                src = cf[t] if t < CT else xf[t - CT]
                sp.dma_start(xst[:, t, :], src).then_inc(x_in[0 if t < CT else 1 + (t - CT) // 3], 16)

            def load_mod(i):
                slot, _, before = mod_slot(i)
                if before >= 0:
                    sp.wait_ge(mod_full, before + 1)
                sp.dma_start(mraw[:, slot, :], wm[MODS[i // KT], i % KT]).then_inc(mod_in[slot], 16)

            def load_tile(s, p):
                col = (s - 1) * P + (P + TILES[p][1])
                if p >= RAW:
                    sp.wait_ge(w_lo, s * NTILE + (p - RAW + 1))
                elif not first(s):
                    sp.wait_ge(w_lo, s * NTILE + (SLOT_TILES[p][-1] + 1 - NTILE))
                sp.dma_start(raw[:, p % RAW, :].rearrange("p (k n) -> p k n", k=KT),
                             win[:, :, bass.ds(col, P)]).then_inc(raw_in[p % RAW], 16)

            for i in range(2 * KT):
                load_mod(i)
            for p in range(RAW):
                load_tile(0, p)
            for p in range(RAW, NTILE):
                for i in range(KT):
                    load_mod((p - RAW + 2) * KT + i)
                load_tile(0, p)
            with sp.Fori(1, HEADS) as s:
                for p in range(NTILE):
                    load_tile(s, p)

            for i in range(KT):
                if i < RAW:
                    sp.wait_ge(w_lo, (HEADS - 1) * NTILE + SLOT_TILES[i][-1] + 1)
                else:
                    sp.wait_ge(o_lo, i - RAW + 1)
                sp.dma_start(raw[:, i % RAW, :], wo[i]).then_inc(raw_in[i % RAW], 16)

            def load_ffn(n, no, r, kind):
                row = n * 2 + int(kind[1])
                at = row if kind[0] == "d" else row * P
                at = at if isinstance(at, int) else sp.snap(at)
                if isinstance(no, int) and no < RAW:
                    sp.wait_ge(o_lo, KT + no - RAW + 1)
                else:
                    sp.wait_ge(f_lo, no - (RAW - 1))
                if kind[0] == "d":
                    sp.dma_start(raw[:, r, :].rearrange("p (o n) -> p o n", o=1),
                                 wd[bass.ds(at, 1)].rearrange("o p n -> p o n")).then_inc(raw_in[r], 16)
                else:
                    w = wg if kind[0] == "g" else wu
                    sp.dma_start(raw[:, r, :].rearrange("p (k n) -> p k n", k=KT),
                                 w[:, :, bass.ds(at, P)]).then_inc(raw_in[r], 16)

            GU = ["g0", "u0", "g1", "u1"]
            for j in range(RAW):
                load_ffn(0, j, (KT + j) % RAW, GU[j])

            for t in range(XT + 2):
                if t < XT:
                    if t == 0:
                        sp.wait_ge(cat_lo, 2 * KT)
                    if t >= 3:
                        sp.wait_ge(x1_store[t % 3], 16 * (t // 3))
                        sp.wait_ge(x2_ready, t - 2)
                    sp.dma_start(x1t[:, t % 3, :], xf[t]).then_inc(x1_in[t % 3], 16)
                if t >= 2:
                    sp.wait_ge(mix_done, t - 1)
                    sp.dma_start(x1_dram[(t - 2) * P:(t - 1) * P, :],
                                 x1t[:, (t - 2) % 3, :]).then_inc(x1_store[(t - 2) % 3], 16)

            load_ffn(0, RAW, (KT + RAW) % RAW, GU[RAW])

            def round_loads(n, par):
                if not first(n):
                    for j in range(2):
                        load_ffn(n - 1, down_no(n - 1, j), (KT + 2 + j) % RAW, f"d{j}")
                if not (isinstance(n, int) and n == NGROUP - 1):
                    for j in range(4):
                        load_ffn(n + 1, gu_no(n + 1, j), (KT + 4 + j) % RAW, GU[j])

            ffn_rounds(sp, round_loads)
            for j in range(2):
                no = down_no(NGROUP - 1, j)
                load_ffn(NGROUP - 1, no, (KT + no) % RAW, f"d{j}")

            for t in range(3):
                sp.wait_ge(x1_store[t], 16 * len(range(t, XT, 3)))
            sp.wait_ge(down_full, 16 * NGROUP)
            for t in range(XT + 2):
                if t >= 2:
                    sp.wait_ge(y_done, t - 1)
                    sp.dma_start(outf[t - 2], xres[:, t % 2, :]).then_inc(out_done[t % 2], 16)
                if t < XT:
                    if t >= 2:
                        sp.wait_ge(out_done[t % 2], 16 * (t // 2))
                    sp.dma_start(xres[:, t % 2, :], x1_dram[t * P:(t + 1) * P, :]).then_inc(res_in[t % 2], 16)
            for q in range(2):
                sp.wait_ge(out_done[q], 16 * (XT // 2))

        @block.tensor
        def _(pe):
            def mm(o, l, r, start, stop):
                return pe.matmul(o, l, r, start=start, stop=stop, skip_group_check=True)

            def product(o, a, b, start, stop):
                mm(o, a[0], b[0], start, False)
                mm(o, a[0], b[1], False, False)
                return mm(o, a[1], b[0], False, stop)

            pe.wait_ge(small_in, 16 * n_small)
            pe.transpose(bank[0][:, 0:NVEC], vrow[0:NVEC, :], ident[0:NVEC, 0:NVEC]).then_inc(pe_cols, 1)
            for j in range(4):
                ins = pe.transpose(bank[1][:, j * TAPS:(j + 1) * TAPS], trow[0:TAPS, j * P:(j + 1) * P],
                                   ident[0:TAPS, 0:TAPS])
            ins.then_inc(pe_cols, 1)

            def mod_vector(n):
                if n == 5:
                    pe.wait_ge(mod_done, 1)
                b = bank[LBASE + n % 5]
                for k in range(KT):
                    slot, before, _ = mod_slot(n * KT + k)
                    pe.wait_ge(mod_in[slot], 16 * (before + 1))
                    for j in range(KT):
                        ins = mm(b[:, 2 * j:2 * j + 2], mraw[:, slot, j * P:(j + 1) * P], silc[:, k, :],
                                 k == 0 and j == 0, k == KT - 1)
                    ins.then_inc(mod_full, 1)

            pe.wait_ge(cols_done, 2)
            mod_vector(0)
            mod_vector(1)

            for t in range(NT):
                pe.wait_ge(xn_ready, t + 1)
                for half in range(2):
                    n = 2 * t + half
                    if n >= 3:
                        pe.wait_ge(xp_free, n - 2)
                    for k in range(4):
                        kk = half * 4 + k
                        ins = pe.transpose(bank[n % 3][:, k * P:(k + 1) * P], xst[:, t, kk * P:(kk + 1) * P],
                                           ident[:])
                    ins.then_inc(xp_full, 1)

            def wait_bank(by, ring, i, s, act_sem, dve_sem):
                who, k, ago = ring_wait(by, ring, i)
                n = by.count(who)
                pe.wait_ge(act_sem if who == "act" else dve_sem, s * n + ((1 - ago) * n + k + 1))

            def project(s, u):
                p, kind, n = UNITS[u]
                b = bank[u % GRING]
                if n == 0:
                    pe.wait_ge(w_lo, s * NTILE + (p + 1))
                wait_bank(GEMM_BY, GRING, u, s, gemm_act, gemm_dve)

                def w(k):
                    return [split[:, p % 2, q, k * P:(k + 1) * P] for q in range(2)]

                if kind == "v":
                    for t in range(4 * n, min(4 * n + 4, NT)):
                        for k in range(KT):
                            ins = product(b[:, (t % 4) * P:(t % 4 + 1) * P],
                                          [hT[:, q, k, t * P:(t + 1) * P] for q in range(2)], w(k),
                                          k == 0, k == KT - 1)
                else:
                    t0 = n * BANK if kind in ("ff", "fb") else CTX + n * BANK
                    wd_ = min(BANK, TOK - t0)
                    for k in range(KT):
                        ins = product(b[:, 0:wd_], w(k), [hT[:, q, k, t0:t0 + wd_] for q in range(2)],
                                      k == 0, k == KT - 1)
                ins.then_inc(gemm_full, 1)

            def use(h, i):
                kind, a1, a2 = USES[i]
                b = bank[LBASE + i % LRING]
                wait_bank(USE_BY, LRING, i, h, use_act, use_dve)
                if kind == "level":
                    l, hf = a1, a2
                    if hf == 0 and l == 0:
                        pe.wait_ge(k_ready, h * NK + 1)
                    elif hf == 0:
                        pe.wait_ge(kc_ready, h * LEVELS + l)
                        pe.wait_ge(q_ready, h * NK + l)
                    for cc in range(4):
                        ch = hf * 4 + cc
                        o = b[:, cc * P:(cc + 1) * P]
                        if l == 0:
                            tk = CTX + ch * P
                            mm(o, K[:, 0, tk:tk + P], qraw[:, ch * P:(ch + 1) * P], True, False)
                            ins = mm(o, K[:, 1, tk:tk + P], qraw[:, ch * P:(ch + 1) * P], False, True)
                        else:
                            bs = 1 << (l - 1)
                            q = view(Q, ch * P, [(2 * bs, P // (2 * bs)), (SEQ + bs, 2), (1, bs)])
                            ins = mm(o, KC[:, ch * P:(ch + 1) * P], q, True, True)
                elif kind == "turn":
                    if a1 == 0 and a2 == 0:
                        pe.wait_ge(k_ready, h * NK + NK)
                    for j in range(3):
                        ch = scan_chunk(a2, 3 * a1 + j)
                        ins = pe.transpose(b[:, j * P:(j + 1) * P], K[:, a2, ch * P:(ch + 1) * P], ident[:])
                elif kind == "outer":
                    if a2 == 0:
                        if a1 == 0:
                            pe.wait_ge(gemm_act, h * N_GACT + 2 * N_GACT)
                        pe.wait_ge(use_act, h * N_UACT + (N_UACT + 2 + 2 * a1 + 2))
                    for j in range(3):
                        ch = scan_chunk(a2, 3 * a1 + j)
                        ins = mm(b[:, j * P:(j + 1) * P], KTok[:, a2, j, :], V[:, ch, :], True, True)
                elif kind == "o":
                    if a1 == 0:
                        pe.wait_ge(state_done, h * NSTATE + NSTATE)
                        pe.wait_ge(q_ready, h * NK + NK)
                        pe.wait_ge(use_dve, h * N_UDVE + (N_UDVE + 2 * LEVELS))
                    for cc in range(4):
                        ch = a1 * 4 + cc
                        o = b[:, cc * P:(cc + 1) * P]
                        sl = slice(ch * P, (ch + 1) * P)
                        mm(o, V[:, CT + ch, :], AT[:, sl], True, False)
                        mm(o, S[:, 0, ch, :], Q[:, 1, sl], False, False)
                        ins = mm(o, S[:, 1, XT - 1 - ch, :], Q[:, 0, sl], False, True)
                elif kind == "ssq":
                    pe.wait_ge(sq_ready, h * 2 + 2)
                    for ch in range(XT):
                        ins = mm(b[:, ch:ch + 1], AT[:, ch * P:(ch + 1) * P], ones[:, 0:1], True, True)
                else:
                    if a1 == 0:
                        pe.wait_ge(rs_ready, h + 1)
                    for cc in range(4):
                        ins = mm(b[:, cc * P:(cc + 1) * P], view(hss, XT + a1 * 4 + cc, [(0, P)]), ident[:],
                                 True, True)
                ins.then_inc(use_full, 1)

            pe.wait_ge(xp_free, 2 * NT)
            pe.wait_ge(h_lo, NT)
            for u in range(NUNIT):
                project(0, u)
                if u in MOD_AT:
                    mod_vector(2 + MOD_AT.index(u))
            pe.wait_ge(mod_done, 6)
            with pe.Fori(1, HEADS) as s:
                for u in range(NUNIT):
                    project(s, u)
                    for i in PE_STEPS[u]:
                        use(s - 1, i)
            for i in range(NUSE):
                use(HEADS - 1, i)

            pe.wait_ge(conv_done, HEADS)
            pe.wait_ge(gemm_act, (HEADS + 1) * N_GACT)
            pe.wait_ge(gemm_dve, (HEADS + 1) * N_GDVE)
            for hf in range(2):
                for j in range(4):
                    ins = mm(bank[hf][:], ones[:], cat[:, 4 + j, hf * BANK:(hf + 1) * BANK], j == 0, j == 3)
                ins.then_inc(ln_pe, 1)
            pe.wait_ge(use_dve, (HEADS + 1) * N_UDVE)
            pe.wait_ge(use_act, (HEADS + 1) * N_UACT)
            for hf in range(2):
                for j in range(4):
                    pe.wait_ge(ln_act, hf * 4 + j + 1)
                    ins = mm(bank[2 + hf][:], ones[:], vtmp[:, j % 2, :], j == 0, j == 3)
                    ins.then_inc(ln_pe, 1)

            def gate_rows(i):
                for j in range(KT):
                    ins = mm(bank[4 + j // 4][:, (j % 4) * P:(j % 4 + 1) * P], view(gate, i * KT + j, [(0, P)]),
                             ident[:], True, True)
                ins.then_inc(g_full, 1)

            gate_rows(0)

            def mix(t):
                hf, tt = t // 4, t % 4
                for n in range(2):
                    i = 2 * t + n
                    if i >= 4:
                        pe.wait_ge(mix_done, t - 1)
                    for k in range(KT):
                        if t == 0 and n == 0:
                            pe.wait_ge(cat_lo, 2 * k + 2)
                            pe.wait_ge(o_lo, k + 1)
                            if k == 0:
                                pe.wait_ge(ln_dve, 10)
                        ins = product(bank[i % 4][:], [catS[:, hf, q, k, tt * P:(tt + 1) * P] for q in range(2)],
                                      [wo_part(q, k)[:, n * BANK:(n + 1) * BANK] for q in range(2)],
                                      k == 0, k == KT - 1)
                    ins.then_inc(mix_full, 1)

            def turn2(t):
                pe.wait_ge(x2_ready, t + 1)
                for half in range(2):
                    if t >= 1:
                        pe.wait_ge(h2_free, 2 * t - 1 + half)
                    for k in range(4):
                        ins = pe.transpose(bank[6 + half][:, k * P:(k + 1) * P], x2t[:, half * 4 + k, :], ident[:])
                    ins.then_inc(h2_full, 1)

            for t in range(XT + 2):
                if t < XT:
                    mix(t)
                if t >= 2:
                    turn2(t - 2)
            pe.wait_ge(g_done, 1)
            gate_rows(1)

            def gate_up(n, fi):
                pe.wait_ge(f_lo, gu_no(n, 2 * fi + 1) + 1)
                for hf in range(2):
                    if first(n) and fi == 0:
                        pe.wait_ge(mix_done, XT)
                        pe.wait_ge(h2_lo, 4 * hf + 4)
                    else:
                        pe.wait_ge(gu_free, n * 4 + (2 * fi + hf - 1))
                    for j in range(2):
                        b = bank[2 * hf + j]
                        for k in range(KT):
                            ins = product(b[:], [ffn_part(q, 2 * fi + j)[:, k * P:(k + 1) * P] for q in range(2)],
                                          [h2T[hf][:, q, k, :] for q in range(2)], k == 0, k == KT - 1)
                        ins.then_inc(gu_full, 1)

            def down(n, par):
                pe.wait_ge(f_lo, down_no(n, 1) + 1)
                pe.wait_ge(mid_lo, n * 4 + 4)
                for i in range(2 * XT):
                    t, hf = i // 2, i % 2
                    pe.wait_ge(down_free, n * 16 + (i + 1))
                    for fi in range(2):
                        ins = product(bank[4 + i % 4][:], [mid[:, par, fi, q, t * P:(t + 1) * P] for q in range(2)],
                                      [ffn_part(q, 4 + fi)[:, hf * BANK:(hf + 1) * BANK] for q in range(2)],
                                      fi == 0, fi == 1)
                    ins.then_inc(down_full, 1)

            def pe_round(n, par):
                gate_up(n, 0)
                gate_up(n, 1)
                if first(n):
                    pe.wait_ge(g_done, 2)
                    pe.wait_ge(h2_free, 2 * XT)
                else:
                    down(n - 1, 1 - par)

            ffn_rounds(pe, pe_round)
            down(NGROUP - 1, (NGROUP - 1) % 2)

        @block.scalar
        def _(act):
            step = Steps(act, act_step)

            act.wait_ge(pe_cols, 1)
            act.activation(silt[:], bank[0][:, 0:2 * KT].rearrange("p (a k) -> p a k", a=2),
                           ACT.Sigmoid).then_inc(sil_sig, 1)
            act.wait_ge(cols_done, 1)
            act.activation(lbt[:, 1, :], lbt[:, 0, :], ACT.Exp).then_inc(lb_exp, 1)

            act.wait_ge(cols_done, 2)
            for q, (t0, t1) in enumerate([(0, 2), (2, 5), (5, 8), (8, 10)]):
                act.wait_ge(x_in[q], 16 * (t1 - t0))
                for t in range(t0, t1):
                    if step.n:
                        step.wait()
                    step(act.activation(junk[:], xst[:, t, :], ACT.Square, accum_out=ss[:, 0, t:t + 1]))
                step.wait()
                act.activation(ss[:, 1, t0:t1], ss[:, 0, t0:t1], ACT.Sqrt, bias=eps[:], scale=1.0 / DM).then_inc(x_root, 1)
            act.sem_inc(gemm_act, N_GACT)
            act.sem_inc(use_act, N_UACT)

            def head_hi(s, p):
                act.wait_ge(raw_in[p % RAW], head_fill(s, p) * 16)
                if p >= 2:
                    act.wait_ge(gemm_full, s * NUNIT + (last_unit(p - 2) + 1))
                elif not first(s):
                    act.wait_ge(gemm_full, s * NUNIT + (last_unit(6 - p) + 1 - NUNIT))
                act.activation(split[:, p % 2, 0], raw[:, p % RAW, :], ACT.Copy).then_inc(w_hi, 1)

            for t in range(NT):
                if t in (6, 7):
                    head_hi(0, t - 6)
                act.wait_ge(xp_free, 2 * t + 2)
                act.activation(hT[:, 0, :, t * P:(t + 1) * P], xfull[:, t % 2], ACT.Copy).then_inc(h_hi, 1)

            def evac(s, u):
                p, kind, n = UNITS[u]
                if kind == "a":
                    return
                act.wait_ge(gemm_full, s * NUNIT + (u + 1))
                b = bank[u % GRING]
                sl = slice(n * BANK, (n + 1) * BANK)
                if kind in ("ff", "fb"):
                    w = min(BANK, TOK - n * BANK)
                    if u == 0 and not first(s):
                        act.wait_ge(q_ready, s * NK + (2 - NK))
                    act.activation(F[:, 0 if kind == "ff" else 1, n * BANK:n * BANK + w], b[:, 0:w],
                                   ACT.Sigmoid).then_inc(gemm_act, 1)
                elif kind == "q":
                    act.activation(qraw[:, sl], b[:], ACT.Copy, scale=float(P) ** -0.5).then_inc(gemm_act, 1)
                elif kind == "g":
                    act.activation(cat_tile(s)[:, sl], b[:], ACT.Sigmoid).then_inc(g_sig, 1)
                elif kind == "b":
                    if n == 0 and not first(s):
                        act.wait_ge(conv_done, s)
                    act.activation(U[:, sl], b[:], ACT.Sigmoid).then_inc(gemm_act, 1)
                else:
                    w = min(4, NT - 4 * n)
                    if n == 0 and not first(s):
                        act.wait_ge(use_full, s * NUSE + (USES.index(("o", 1, 0)) + 1 - NUSE))
                    act.activation(V[:, 4 * n:4 * n + w, :], b[:, 0:w * P].rearrange("p (t v) -> p t v", v=P),
                                   ACT.Copy).then_inc(gemm_act, 1)

            def level_keys(h, l):
                bs = 1 << (l - 1)
                act.wait_ge(k_ready, h * NK + l)
                if l > 1:
                    act.wait_ge(use_full, h * NUSE + 2 * l)
                act.activation(view(KC, 0, [(2 * bs, SEQ // (2 * bs)), (bs, 2), (1, bs)]),
                               view(K, CTX, [(2 * bs, SEQ // (2 * bs)), (TOK + bs, 2), (1, bs)]),
                               ACT.Copy).then_inc(kc_ready, 1)

            def act_use(h, i):
                kind, a1, a2 = USES[i]
                b = bank[LBASE + i % LRING]
                if kind == "level" and a1 == 0:
                    act.wait_ge(use_full, h * NUSE + (i + 1))
                    act.activation(AT[:, a2 * BANK:(a2 + 1) * BANK], b[:], ACT.Copy).then_inc(use_act, 1)
                elif kind == "turn":
                    act.wait_ge(use_full, h * NUSE + (i + 1))
                    if a1 > 0:
                        act.wait_ge(use_full, h * NUSE + (USES.index(("outer", a1 - 1, a2)) + 1))
                    act.activation(KTok[:, a2], b[:, 0:3 * P].rearrange("p (j n) -> p j n", n=P),
                                   ACT.Copy).then_inc(use_act, 1)
                elif kind == "o":
                    act.wait_ge(use_full, h * NUSE + (USES.index(("o", 1, 0)) + 1))
                    act.activation(AT[:, a1 * BANK:(a1 + 1) * BANK], b[:], ACT.Square).then_inc(sq_ready, 1)
                elif kind == "ssq":
                    act.wait_ge(use_full, h * NUSE + (i + 1))
                    act.activation(hss[:, 0, :], b[:, 0:XT], ACT.Sqrt, bias=eps[:], scale=1.0 / P).then_inc(use_act, 1)

            def act_body(s, gemm, rec):
                for u in range(NUNIT):
                    if gemm:
                        p, _, n = UNITS[u]
                        if u == 0 and not first(s):
                            head_hi(s, 0)
                            head_hi(s, 1)
                        if u:
                            evac(s, u)
                        if n == 0 and 1 <= p < NTILE - 1:
                            head_hi(s, p + 1)
                    if rec:
                        for i in PE_STEPS[u]:
                            act_use(s - 1, i)
                        if u < LEVELS:
                            level_keys(s - 1, u + 1)
                    if gemm and u == 0:
                        evac(s, u)

            act_body(0, True, False)
            with act.Fori(1, HEADS) as s:
                act_body(s, True, True)
            act_body(HEADS, False, True)

            def cat_parts(j):
                for hf in range(2):
                    act.activation(catS[:, hf, 0, j, :], cat[:, j, hf * BANK:(hf + 1) * BANK],
                                   ACT.Copy).then_inc(cat_hi, 1)

            for n in range(8):
                hf, j = n // 4, n % 4
                act.wait_ge(ln_dve, n + 1)
                if n >= 2:
                    act.wait_ge(ln_pe, n + 1)
                act.activation(vtmp[:, n % 2, :], cat[:, 4 + j, hf * BANK:(hf + 1) * BANK],
                               ACT.Square).then_inc(ln_act, 1)
            for hf in range(2):
                act.wait_ge(ln_pe, 6 + 4 * hf)
                act.activation(rstd[:, hf * BANK:(hf + 1) * BANK], bank[2 + hf][:], ACT.Sqrt, bias=eps[:],
                               scale=1.0 / BANK).then_inc(ln_act, 1)
            act.wait_ge(use_dve, (HEADS + 1) * N_UDVE)
            for j in range(4):
                cat_parts(j)
            for j in range(4):
                act.wait_ge(ln_dve, 11 + j)
                if j >= 2:
                    act.wait_ge(ln_dve, 13 + j)
                act.activation(lnsg[:, j % 2, :], cat[:, 4 + j, :], ACT.Sigmoid, scale=vec[:, R_LNG + j:R_LNG + j + 1],
                               bias=vec[:, R_LNB + j:R_LNB + j + 1]).then_inc(ln_act, 1)

            def wo_hi(i):
                act.wait_ge(raw_in[i % RAW], 16 * late_fill(i))
                act.activation(wo_part(0, i), raw[:, i % RAW, :], ACT.Copy).then_inc(o_hi, 1)

            for i in range(4):
                wo_hi(i)
            for j in range(4, 8):
                act.wait_ge(ln_dve, LN_STEPS - 7 + j)
                cat_parts(j)
                wo_hi(j)

            def mix_roots(t):
                for n in range(2):
                    act.wait_ge(mix_full, 2 * t + n + 1)
                    if t and n == 0:
                        act.wait_ge(mix_done, t)
                    step(act.activation(mixt[:, n * BANK:(n + 1) * BANK], bank[(2 * t + n) % 4][:], ACT.Square,
                                        accum_out=ss[:, n, t:t + 1]))
                step.wait()
                step(act.activation(rr[:, 0, t:t + 1], ss[:, 0, t:t + 1], ACT.Identity, bias=ss[:, 1, t:t + 1]))
                step.wait()
                act.activation(rr[:, 1, t:t + 1], rr[:, 0, t:t + 1], ACT.Sqrt, bias=eps[:],
                               scale=1.0 / DM).then_inc(mix_root, 1)
                act.wait_ge(mix_done, t + 1)
                if t:
                    act.wait_ge(h2_full, 2 * t)
                step(act.activation(x2t[:].rearrange("p k n -> p (k n)"), x1t[:, t % 3, :], ACT.Square,
                                    accum_out=ss[:, 0, t:t + 1]))
                step.wait()
                act.activation(rr[:, 0, t:t + 1], ss[:, 0, t:t + 1], ACT.Sqrt, bias=eps[:],
                               scale=1.0 / DM).then_inc(x1_root, 1)

            def h2_part(t):
                act.wait_ge(h2_free, 2 * t + 2)
                act.activation(h2T[t // 4][:, 0, :, (t % 4) * P:(t % 4 + 1) * P], h2f[:], ACT.Copy).then_inc(h2_hi, 1)

            for t in range(XT + 1):
                if t < XT:
                    mix_roots(t)
                if t >= 1:
                    h2_part(t - 1)

            def gu_hi(n, j):
                if first(n):
                    if j == 0:
                        act.wait_ge(mix_full, 2 * XT)
                        act.wait_ge(x2_ready, XT)
                        for q in range(3):
                            act.wait_ge(x1_store[q], 16 * len(range(q, XT, 3)))
                    act.wait_ge(raw_in[(KT + j) % RAW], 16 * late_fill(KT + j))
                else:
                    act.wait_ge(gu_full, n * 8 + (4 * (j // 2) + 4 - 8))
                    r = (KT + 4 + j) % RAW
                    act.wait_ge(raw_in[r], n * 32 + 16 * (late_fill(KT + 4 + j) - 2))
                act.activation(ffn_part(0, j), raw[:, (KT + j + (0 if first(n) else 4)) % RAW, :],
                               ACT.Copy).then_inc(f_hi, 1)

            def down_hi(n, j):
                if not first(n):
                    act.wait_ge(down_full, n * 16)
                if isinstance(n, int) and n == NGROUP - 1:
                    late = KT + down_no(n, j)
                    r, fills = late % RAW, late_fill(late) * 16
                else:
                    r = (KT + 8 + j) % RAW
                    fills = n * 32 + 16 * late_fill(KT + 8 + j)
                act.wait_ge(raw_in[r], fills)
                act.activation(ffn_part(0, 4 + j), raw[:, r, :], ACT.Copy).then_inc(f_hi, 1)

            def act_tile(n, fi, par):
                for hf in range(2):
                    act.wait_ge(gu_full, n * 8 + (4 * fi + 2 * hf + 1))
                    if not (first(n) and fi == 0):
                        act.wait_ge(gu_free, n * 4 + (2 * fi + hf - 1))
                    act.activation(sgm[:, hf, :], bank[2 * hf][:], ACT.Sigmoid).then_inc(gu_sig, 1)
                for hf in range(2):
                    act.wait_ge(gu_free, n * 4 + (2 * fi + hf + 1))
                    if fi == 0 and hf == 0 and not (isinstance(n, int) and n < 2):
                        act.wait_ge(down_full, n * 16 - 16)
                    act.activation(mid[:, par, fi, 0, hf * BANK:(hf + 1) * BANK], mid32[:, hf, :],
                                   ACT.Copy).then_inc(mid_hi, 1)

            def act_round(n, par):
                if not first(n):
                    down_hi(n - 1, 0)
                    down_hi(n - 1, 1)
                for fi in range(2):
                    act_tile(n, fi, par)
                    if not (isinstance(n, int) and n == NGROUP - 1):
                        gu_hi(n + 1, 2 * fi)
                        gu_hi(n + 1, 2 * fi + 1)

            for j in range(4):
                gu_hi(0, j)
            ffn_rounds(act, act_round)
            down_hi(NGROUP - 1, 0)
            down_hi(NGROUP - 1, 1)

            act.wait_ge(down_full, 16 * NGROUP)
            for t in range(XT):
                act.wait_ge(down_free, 4 + 16 * (NGROUP - 1) + 2 * t + 2)
                step.wait()
                step(act.activation(junk2[:], y[:, t, :], ACT.Square, accum_out=ss[:, 0, t:t + 1]))
                step.wait()
                act.activation(rr[:, 0, t:t + 1], ss[:, 0, t:t + 1], ACT.Sqrt, bias=eps[:],
                               scale=1.0 / DM).then_inc(y_root, 1)

        @block.gpsimd
        def _(pool):
            def lo_part(lo, full, hi):
                return pool.tensor_tensor(lo, full, hi.bitcast(F32), ALU.subtract)

            def head_lo(s, p):
                pool.wait_ge(w_hi, s * NTILE + (p + 1))
                lo_part(split[:, p % 2, 1], raw[:, p % RAW, :], split[:, p % 2, 0]).then_inc(w_lo, 1)

            for t in range(NT):
                if t in (6, 7):
                    head_lo(0, t - 6)
                pool.wait_ge(h_hi, t + 1)
                sl = slice(t * P, (t + 1) * P)
                lo_part(hT[:, 1, :, sl], xfull[:, t % 2], hT[:, 0, :, sl]).then_inc(h_lo, 1)
            for p in range(2, NTILE):
                head_lo(0, p)
            with pool.Fori(1, HEADS) as s:
                for p in range(NTILE):
                    head_lo(s, p)

            for i in range(KT):
                pool.wait_ge(o_hi, i + 1)
                lo_part(wo_part(1, i), raw[:, i % RAW, :], wo_part(0, i)).then_inc(o_lo, 1)
            for t in range(XT):
                pool.wait_ge(h2_hi, t + 1)
                h2, sl = h2T[t // 4], slice((t % 4) * P, (t % 4 + 1) * P)
                lo_part(h2[:, 1, :, sl], h2f[:], h2[:, 0, :, sl]).then_inc(h2_lo, 1)

            def ffn_lo(no, r, j):
                pool.wait_ge(f_hi, no + 1)
                lo_part(ffn_part(1, j), raw[:, r, :], ffn_part(0, j)).then_inc(f_lo, 1)

            for j in range(4):
                ffn_lo(j, (KT + j) % RAW, j)

            def pool_round(n, par):
                if not first(n):
                    for j in range(2):
                        ffn_lo(down_no(n - 1, j), (KT + 2 + j) % RAW, 4 + j)
                if not (isinstance(n, int) and n == NGROUP - 1):
                    for j in range(4):
                        ffn_lo(gu_no(n + 1, j), (KT + 4 + j) % RAW, j)

            ffn_rounds(pool, pool_round)
            for j in range(2):
                no = down_no(NGROUP - 1, j)
                ffn_lo(no, (KT + no) % RAW, 4 + j)

        @block.vector
        def _(dve):
            step = Steps(dve, dve_step)

            step(dve.memset(ones[:], 1.0))
            step(dve.memset(eps[:], EPS))
            dve.sem_inc(gemm_dve, N_GDVE)
            dve.sem_inc(use_dve, N_UDVE)
            dve.sem_inc(down_free, 4)
            dve.wait_ge(pe_cols, 2)
            dve.wait_ge(sil_sig, 1)
            step(dve.tensor_copy(vec[:], bank[0][:, 0:NVEC]))
            step(dve.tensor_copy(masks[:], mask32[:]))
            step(dve.tensor_copy(taps[:], bank[1][:, 0:4 * TAPS].rearrange("p (j t) -> p j t", t=TAPS)))
            step.wait()
            dve.tensor_tensor(lbt[:, 0, :], vec[:, R_LBF:R_LBF + 8], vec[:, R_LBF:R_LBF + 8],
                              ALU.subtract).then_inc(cols_done, 1)
            dve.tensor_tensor(silc[:].rearrange("p k a -> p a k"), silt[:],
                              vec[:, 0:2 * KT].rearrange("p (a k) -> p a k", a=2), ALU.mult).then_inc(cols_done, 1)
            dve.wait_ge(lb_exp, 1)
            step(dve.reciprocal(lbt[:, 2, :], lbt[:, 1, :]))
            step.wait()
            step(dve.tensor_tensor(lbt[:, 0, :], lbt[:, 1, :], lbt[:, 2, :], ALU.mult))
            step.wait()
            step(dve.tensor_tensor(lb[:, 0, :], lbt[:, 0, :], lbt[:, 0, :], ALU.subtract))
            step.wait()
            step(dve.tensor_scalar(lb[:, 1, :], lb[:, 0, :], -1.0, 1.0, ALU.mult, ALU.add))
            step(dve.tensor_scalar(lb[:, 2, :], lb[:, 0, :], 1.0, -1.0, ALU.mult, ALU.add))

            for q, (t0, t1) in enumerate([(0, 2), (2, 5), (5, 8), (8, 10)]):
                dve.wait_ge(x_root, q + 1)
                step(dve.reciprocal(rr[:, 0, t0:t1], ss[:, 1, t0:t1]))
                step.wait()
                for t in range(t0, t1):
                    dve.tensor_scalar(xst[:, t, :], xst[:, t, :], rr[:, 0, t:t + 1], None, ALU.mult).then_inc(xn_ready, 1)

            def mod_take(n):
                m = MODS[n]
                dve.wait_ge(mod_full, KT * (n + 1))
                dve.tensor_tensor(mod[:, m], bank[LBASE + n % 5][:, 0:2 * KT].rearrange("p (k a) -> p k a", a=2),
                                  view(vec, R_BM + m * KT, [(1, KT), (0, 2)]), ALU.add).then_inc(mod_done, 1)
                dve.wait_ge(mod_done, n + 1)
                one = mod[:, m, :, 0]
                if m == 1:
                    step(dve.scalar_tensor_tensor(gain[:], mod[:, m], 1.0, view(vec, R_PREM, [(1, KT), (0, 2)]),
                                                  ALU.add, ALU.mult))
                elif m == 4:
                    step(dve.scalar_tensor_tensor(gain2[:], one, 1.0, vec[:, R_PREF:R_PREF + KT], ALU.add, ALU.mult))
                elif m in (2, 5):
                    g, r0 = (0, R_POSTM) if m == 2 else (1, R_POSTF)
                    step(dve.tensor_tensor(gate[:, g], one, vec[:, r0:r0 + KT], ALU.mult))

            mod_take(0)
            mod_take(1)
            step.wait()
            for t in range(NT):
                a = 1 if t < CT else 0
                for k in range(KT):
                    if k % 4 == 0:
                        dve.wait_ge(xp_full, 2 * t + k // 4 + 1)
                    if k == 0 and t >= 2:
                        dve.wait_ge(h_lo, t - 1)
                    ins = dve.tensor_scalar(xfull[:, t % 2, k, :], bank[(2 * t + k // 4) % 3][:, (k % 4) * P:(k % 4 + 1) * P],
                                            gain[:, k, a:a + 1], mod[:, 0, k, a:a + 1], ALU.mult, ALU.add)
                    if k % 4 == 3:
                        ins.then_inc(xp_free, 1)

            def take(s, u):
                _, kind, n = UNITS[u]
                b = bank[u % GRING]
                sl = slice(n * BANK, (n + 1) * BANK)
                if kind == "g":
                    dve.wait_ge(g_sig, s * 2 + (n + 1))
                    dve.tensor_tensor(cat_tile(s)[:, sl], b[:], cat_tile(s)[:, sl], ALU.mult).then_inc(gemm_dve, 1)
                elif kind == "a":
                    dve.wait_ge(gemm_full, s * NUNIT + (u + 1))
                    dve.wait_ge(gemm_act, s * N_GACT + (N_GACT + 8 + n + 1))
                    dve.tensor_tensor(U[:, sl], b[:], U[:, sl], ALU.mult).then_inc(gemm_dve, 1)

            def conv_view(i, t0, t1):
                return cat[:, bass.ds(i, 1), :].rearrange("p o (r c) -> p (o r) c", c=GRID)[:, :, t0:t1]

            u_rows = U[:].rearrange("p (r c) -> p r c", c=GRID)
            others = [k for k in range(TAPS) if k != PAD]

            def conv(h, n):
                def w(k):
                    return taps[:, bass.ds(h, 1), k:k + 1].rearrange("p o n -> p (o n)")
                if n < 0:
                    dve.wait_ge(gemm_dve, h * N_GDVE + 2 * N_GDVE)
                    step(dve.tensor_scalar(cat_tile(h + 4), U[:], w(PAD), vec[:, bass.ds(h + R_DWB, 1)], ALU.mult, ALU.add))
                    return
                k = others[n]
                d = k - PAD
                t0, t1 = max(0, -d), GRID - max(0, d)
                step.wait(conv_last[0])
                ins = dve.scalar_tensor_tensor(conv_view(h + 4, t0, t1), u_rows[:, :, t0 + d:t1 + d], w(k),
                                               conv_view(h + 4, t0, t1), ALU.mult, ALU.add)
                if n == len(others) - 1:
                    ins.then_inc(conv_done, 1)
                else:
                    conv_last[0] = step(ins)

            conv_last = [0]

            def rec_start(h):
                dve.wait_ge(gemm_act, h * N_GACT + (N_GACT + 8))
                for d in range(2):
                    sc = [lb[:, i, bass.ds(h + 4 * d, 1)] for i in range(3)]
                    ins = dve.tensor_scalar(K[:, d], F[:, d], sc[2], sc[1], ALU.mult, ALU.add)
                ins.then_inc(k_ready, 1)
                for d in range(2):
                    sc = [lb[:, i, bass.ds(h + 4 * d, 1)] for i in range(3)]
                    step(dve.tensor_scalar(F[:, d], F[:, d], sc[1], sc[0], ALU.mult, ALU.add))
                step.wait()
                step(dve.tensor_scalar(F[:], F[:], F_MIN, None, ALU.max))
                step.wait()
                dve.tensor_tensor(Q[:, 0], qraw[:], F[:, 1, CTX:], ALU.mult)
                dve.tensor_tensor(Q[:, 1], qraw[:], F[:, 0, CTX:], ALU.mult).then_inc(q_ready, 1)
                step(dve.tensor_tensor(T[:], view(F, 0, [(TOK, 2), (2, TOK // 2)]),
                                       view(F, 1, [(TOK, 2), (2, TOK // 2)]), ALU.mult))

            def rec_level(h, l):
                bs = 1 << (l - 1)
                half = TOK // 2
                nk, nq = TOK // (2 * bs), SEQ // (2 * bs)
                if l == 1:
                    kt = view(F, 1, [(TOK - 1, 2), (2, nk), (0, 1)])
                    qt = [view(F, TOK + CTX + 1, [(2, nq), (0, 1)]), view(F, CTX, [(2, nq), (0, 1)])]
                else:
                    kt = view(T, bs // 2, [(half - bs // 2, 2), (bs, nk), (0, bs)])
                    qt = [view(T, half + CTX // 2 + bs // 2, [(bs, nq), (0, bs)]),
                          view(T, CTX // 2, [(bs, nq), (0, bs)])]
                dve.wait_ge(kc_ready, h * LEVELS + l)
                if l == 1:
                    dve.wait_ge(use_full, h * NUSE + 2)
                dve.wait_ge(k_ready, h * NK + l)
                step.wait(t_last[0])
                kv = view(K, 0, [(TOK + bs, 2), (2 * bs, nk), (1, bs)])
                dve.tensor_tensor(kv, kv, kt, ALU.mult).then_inc(k_ready, 1)
                if l == 1:
                    dve.wait_ge(use_act, h * N_UACT + (N_UACT + 2))
                dve.wait_ge(use_full, h * NUSE + (2 * l + 2))
                dve.wait_ge(q_ready, h * NK + l)
                for i in range(2):
                    qv = view(Q, i * (SEQ + bs), [(2 * bs, nq), (1, bs)])
                    ins = dve.tensor_tensor(qv, qv, qt[i], ALU.mult)
                ins.then_inc(q_ready, 1)
                if l > 1:
                    dve.wait_ge(k_ready, h * NK + (l + 1))
                    dve.wait_ge(q_ready, h * NK + (l + 1))
                    tv = view(T, 0, [(half, 2), (bs, nk)])
                    t_last[0] = step(dve.tensor_tensor(tv, tv, view(T, bs // 2, [(half, 2), (bs, nk)]), ALU.mult))
                for hf in range(2):
                    dve.copy_predicated(view(AT, hf * BANK, [(P, 4), (1, P)]), view(masks, (l - 1) * P, [(0, 4), (1, P)]),
                                        bank[LBASE + (2 * l + hf) % LRING][:].rearrange("p (c n) -> p c n", n=P)
                                        ).then_inc(use_dve, 1)

            t_last = [0]

            def rec_states(h, g):
                for d in range(2):
                    i = USES.index(("outer", g, d))
                    dve.wait_ge(use_full, h * NUSE + (i + 1))
                    for j in range(3):
                        n = 3 * g + j
                        src = bank[LBASE + i % LRING][:, j * P:(j + 1) * P]
                        dst = S[:, d, n - 1 if n else XT - 1]
                        done = 6 * g + 3 * d + j
                        if n == 0:
                            ins = dve.tensor_copy(dst, src)
                        else:
                            prev = done - 1 if j else done - 4
                            dve.wait_ge(state_done, h * NSTATE + (prev + 1))
                            if n == 1 and d == 0:
                                step.wait(t_last[0])
                            ch = scan_chunk(d, n)
                            ins = dve.scalar_tensor_tensor(dst, S[:, d, n - 2 if n > 1 else XT - 1],
                                                           T[:, d, ch * (P // 2):ch * (P // 2) + 1], src,
                                                           ALU.mult, ALU.add)
                        ins.then_inc(state_done, 1)
                    dve.wait_ge(state_done, h * NSTATE + (6 * g + 3 * d + 3))
                    dve.sem_inc(use_dve, 1)

            def rec_out(h, u):
                if u == 12:
                    for hf in range(2):
                        dve.wait_ge(sq_ready, h * 2 + (hf + 1))
                        dve.wait_ge(gemm_dve, h * N_GDVE + (N_GDVE + 2))
                        i = USES.index(("o", hf, 0))
                        c = cat_tile(h)[:, hf * BANK:(hf + 1) * BANK]
                        dve.scalar_tensor_tensor(c, bank[LBASE + i % LRING][:], vec[:, R_ON:R_ON + 1], c,
                                                 ALU.mult, ALU.mult).then_inc(use_dve, 1)
                elif u == 13:
                    dve.wait_ge(use_act, h * N_UACT + 2 * N_UACT)
                    dve.reciprocal(hss[:, 1, :], hss[:, 0, :]).then_inc(rs_ready, 1)
                elif u == 14:
                    for hf in range(2):
                        i = USES.index(("rb", hf, 0))
                        dve.wait_ge(use_full, h * NUSE + (i + 1))
                        dve.wait_ge(use_dve, h * N_UDVE + (2 * N_UDVE - 3 + hf))
                        c = cat_tile(h)[:, hf * BANK:(hf + 1) * BANK]
                        dve.tensor_tensor(c, bank[LBASE + i % LRING][:], c, ALU.mult).then_inc(use_dve, 1)

            def dve_body(s, gemm, rec):
                tap = 0
                for u in range(NUNIT):
                    if gemm:
                        take(s, u)
                    if rec:
                        h = s - 1
                        if u == 0:
                            rec_start(h)
                            t_last[0] = step.n
                            conv(h, -1)
                            conv_last[0] = step.n
                        elif u <= LEVELS:
                            rec_level(h, u)
                        elif 9 <= u < 9 + SCAN:
                            rec_states(h, u - 9)
                        else:
                            rec_out(h, u)
                        if 1 <= u <= 8:
                            for _ in range(4):
                                if tap < len(others):
                                    conv(h, tap)
                                    tap += 1

            for u in range(NUNIT):
                take(0, u)
                if u in MOD_AT:
                    mod_take(2 + MOD_AT.index(u))
            base = step.n
            with dve.Fori(1, HEADS) as s:
                step.base, step.n = s * BODY_STEPS + (base - BODY_STEPS), 0
                dve_body(s, True, True)
                assert step.n == BODY_STEPS, step.n
            step.base, step.n = base + (HEADS - 1) * BODY_STEPS, 0
            dve_body(HEADS, False, True)
            assert step.n == BODY_STEPS, step.n

            for n in range(8):
                hf, j = n // 4, n % 4
                dve.wait_ge(ln_pe, hf + 1)
                if n == 0:
                    dve.wait_ge(conv_done, HEADS)
                c = cat[:, 4 + j, hf * BANK:(hf + 1) * BANK]
                if j == 3 or hf == 1:
                    dve.wait_ge(ln_pe, 2)
                dve.scalar_tensor_tensor(c, bank[hf][:], -1.0 / BANK, c, ALU.mult, ALU.add).then_inc(ln_dve, 1)

            def cat_part(j):
                for hf in range(2):
                    dve.wait_ge(cat_hi, 2 * j + hf + 1)
                    dve.tensor_tensor(catS[:, hf, 1, j, :], cat[:, j, hf * BANK:(hf + 1) * BANK],
                                      catS[:, hf, 0, j, :].bitcast(F32), ALU.subtract).then_inc(cat_lo, 1)

            dve.wait_ge(g_full, 1)
            for q in range(2):
                step(dve.tensor_copy(Gb[:, q * BANK:(q + 1) * BANK], bank[4 + q][:]))
            step.wait()
            dve.sem_inc(g_done, 1)
            for hf in range(2):
                dve.wait_ge(ln_act, 9 + hf)
                r = rstd[:, hf * BANK:(hf + 1) * BANK]
                dve.reciprocal(r, r).then_inc(ln_dve, 1)
            dve.wait_ge(ln_dve, 10)
            for j in range(4):
                dve.tensor_tensor(cat[:, 4 + j], cat[:, 4 + j], rstd[:], ALU.mult).then_inc(ln_dve, 1)
            for j in range(4):
                cat_part(j)
            for j in range(4):
                dve.wait_ge(ln_act, 11 + j)
                dve.wait_ge(ln_dve, 11 + j)
                step(dve.tensor_scalar(cat[:, 4 + j], cat[:, 4 + j], vec[:, R_LNG + j:R_LNG + j + 1],
                                       vec[:, R_LNB + j:R_LNB + j + 1], ALU.mult, ALU.add))
                step.wait()
                dve.tensor_tensor(cat[:, 4 + j], cat[:, 4 + j], lnsg[:, j % 2, :], ALU.mult).then_inc(ln_dve, 1)
            for j in range(4, 8):
                cat_part(j)

            def x1(t):
                dve.wait_ge(mix_root, t + 1)
                step(dve.reciprocal(rr[:, 1, t:t + 1], rr[:, 1, t:t + 1]))
                step.wait()
                for n in range(2):
                    sl = slice(n * BANK, (n + 1) * BANK)
                    step(dve.scalar_tensor_tensor(mixt[:, sl], bank[(2 * t + n) % 4][:], rr[:, 1, t:t + 1], Gb[:, sl],
                                                  ALU.mult, ALU.mult))
                step.wait()
                dve.wait_ge(x1_in[t % 3], 16 * (t // 3 + 1))
                dve.tensor_tensor(x1t[:, t % 3, :], x1t[:, t % 3, :], mixt[:], ALU.add).then_inc(mix_done, 1)
                dve.wait_ge(x1_root, t + 1)
                step(dve.reciprocal(rr[:, 0, t:t + 1], rr[:, 0, t:t + 1]))
                step.wait()
                dve.tensor_scalar(x2t[:].rearrange("p k n -> p (k n)"), x1t[:, t % 3, :], rr[:, 0, t:t + 1], None,
                                  ALU.mult).then_inc(x2_ready, 1)

            def h2(t):
                for k in range(KT):
                    if k % 4 == 0:
                        dve.wait_ge(h2_full, 2 * t + k // 4 + 1)
                    if k == 0 and t:
                        dve.wait_ge(h2_lo, t)
                    ins = dve.tensor_scalar(h2f[:, k, :], bank[6 + k // 4][:, (k % 4) * P:(k % 4 + 1) * P],
                                            gain2[:, k:k + 1], mod[:, 3, k, 0:1], ALU.mult, ALU.add)
                    if k % 4 == 3:
                        ins.then_inc(h2_free, 1)

            for t in range(XT + 1):
                if t < XT:
                    x1(t)
                if t >= 1:
                    h2(t - 1)
            dve.wait_ge(g_full, 2)
            for q in range(2):
                step(dve.tensor_copy(Gb[:, q * BANK:(q + 1) * BANK], bank[4 + q][:]))
            step.wait()
            dve.sem_inc(g_done, 1)

            def dve_tile(n, fi, par, base):
                for hf in range(2):
                    i = n * 4 + (2 * fi + hf + 1)
                    dve.wait_ge(gu_sig, i)
                    if not (first(n) and fi == 0):
                        dve.wait_ge(mid_lo, i - 2)
                    dve.tensor_tensor(mid32[:, hf, :], bank[2 * hf][:], sgm[:, hf, :], ALU.mult).then_inc(gu_part, 1)
                    dve.wait_ge(gu_part, i)
                    dve.wait_ge(gu_full, n * 8 + (4 * fi + 2 * hf + 2))
                    dve.tensor_tensor(mid32[:, hf, :], bank[2 * hf + 1][:], mid32[:, hf, :], ALU.mult).then_inc(gu_free, 1)
                for hf in range(2):
                    i = n * 4 + (2 * fi + hf + 1)
                    dve.wait_ge(gu_free, i)
                    dve.wait_ge(mid_hi, i)
                    sl = slice(hf * BANK, (hf + 1) * BANK)
                    dve.tensor_tensor(mid[:, par, fi, 1, sl], mid32[:, hf, :], mid[:, par, fi, 0, sl].bitcast(F32),
                                      ALU.subtract).then_inc(mid_lo, 1)

            def dve_down(n):
                for i in range(2 * XT):
                    t, hf = i // 2, i % 2
                    sl = slice(hf * BANK, (hf + 1) * BANK)
                    dve.wait_ge(down_full, n * 16 + (i + 1))
                    if first(n):
                        ins = dve.tensor_copy(y[:, t, sl], bank[4 + i % 4][:])
                    else:
                        dve.wait_ge(down_free, n * 16 + (i + 1 - 12))
                        ins = dve.tensor_tensor(y[:, t, sl], bank[4 + i % 4][:], y[:, t, sl], ALU.add)
                    ins.then_inc(down_free, 1)

            def dve_round(n, par):
                dve_tile(n, 0, par, None)
                dve_tile(n, 1, par, None)
                if not first(n):
                    dve_down(n - 1)

            ffn_rounds(dve, dve_round)
            dve_down(NGROUP - 1)

            for t in range(XT):
                dve.wait_ge(y_root, t + 1)
                step(dve.reciprocal(rr[:, 1, t:t + 1], rr[:, 0, t:t + 1]))
                step.wait()
                step(dve.scalar_tensor_tensor(y[:, t, :], y[:, t, :], rr[:, 1, t:t + 1], Gb[:], ALU.mult, ALU.mult))
                step.wait()
                dve.wait_ge(res_in[t % 2], 16 * (t // 2 + 1))
                dve.tensor_tensor(xres[:, t % 2, :], xres[:, t % 2, :], y[:, t, :], ALU.add).then_inc(y_done, 1)


_INS = ["x", "c", "ctx", "c_ctx", "w_mod", "b_mod", "pre_mix_g", "post_mix_g", "pre_ffn_g", "post_ffn_g",
        "w_in", "w_out", "hgrn_lb_fwd", "hgrn_lb_bwd", "hgrn_onorm_g", "conv_dw_w", "conv_dw_b",
        "conv_ln_g", "conv_ln_b", "ffn_w_gate", "ffn_w_up", "ffn_w_down"]


def shape_constants():
    i = np.arange(P)
    xor = i[:, None] ^ i[None, :]
    masks = np.stack([(xor >= 1 << l) & (xor < 2 << l) for l in range(LEVELS)], 1).astype(np.float32)
    return {"ident": np.eye(P, dtype=np.float32), "masks": masks}


def kernel(**inputs):
    import concourse.bacc as bacc
    from concourse.bass_utils import run_bass_kernel_spmd

    nc = bacc.Bacc("TRN2", target_bir_lowering=False, num_devices=1)
    arrays = {f"in_{n}": np.ascontiguousarray(inputs[n]) for n in _INS}
    arrays.update(shape_constants())
    args = [nc.dram_tensor(n, list(a.shape), mybir.dt.from_np(a.dtype), kind="ExternalInput").ap()
            for n, a in arrays.items()]
    args.append(nc.dram_tensor("out", [1, SEQ, DM], F32, kind="ExternalOutput").ap())
    kernel_program(nc, *args)
    return run_bass_kernel_spmd(nc, [arrays], core_ids=[0]).results[0]["out"]
```

```python
from contextlib import ExitStack

import numpy as np

import concourse.bass as bass
from concourse import mybir

F32 = mybir.dt.float32
F32R = mybir.dt.float32r
U8 = mybir.dt.uint8
ALU = mybir.AluOpType
ACT = mybir.ActivationFunctionType

P = 128
DM = 1024
KT = DM // P
SEQ = 1024
CTX = 256
TOK = CTX + SEQ
XT, CT = SEQ // P, CTX // P
NT = XT + CT
HEADS = 4
GRID = 64
ROWS = SEQ // GRID
TAPS = 31
PAD = TAPS // 2
DFF = 2816
FT = DFF // P
EPS = 1e-6
F_MIN = 1e-30
BANK = 512
LEVELS = 7

R_C, R_CC, R_BM, R_PREM, R_PREF, R_POSTM, R_POSTF, R_LBF, R_LBB, R_DWB, R_LNG, R_LNB, R_ON = (
    0, 8, 16, 64, 72, 80, 88, 96, 100, 104, 108, 112, 116)
NVEC = 117

TILES = [("ff", 512), ("fb", 1024), ("q", 0), ("g", 2048), ("b", 3072), ("a", 2560), ("v", 1536)]
NTILE = len(TILES)
UNITS = [(p, kind, n) for p, (kind, _) in enumerate(TILES)
         for n in range(3 if kind in ("ff", "fb", "v") else 2)]
NUNIT = len(UNITS)
GRING = 3
GEMM_BY = ["dve" if k in ("g", "a") else "act" for _, k, _ in UNITS]

SCAN = 3
USES = [("level", l, hf) for l in range(LEVELS + 1) for hf in range(2)]
_scan = [[("turn", g, d) for d in range(2)] for g in range(SCAN)], [[("outer", g, d) for d in range(2)] for g in range(SCAN)]
USES += _scan[0][0]
for _g in range(SCAN):
    USES += _scan[1][_g]
    if _g + 1 < SCAN:
        USES += _scan[0][_g + 1]
USES += [("o", 0, 0), ("o", 1, 0), ("ssq", 0, 0), ("rb", 0, 0), ("rb", 1, 0)]
NUSE = len(USES)
LRING, LBASE = 5, 3
USE_BY = ["act" if u[0] in ("turn", "ssq") or u[:2] == ("level", 0) else "dve" for u in USES]


def ordinal(by, i):
    return by[:i].count(by[i])


def ring_wait(by, ring, i):
    n = len(by)
    j = i - ring if i >= ring else max(k for k in range(n) if k % ring == i % ring)
    return by[j], ordinal(by, j), 0 if i >= ring else 1


PE_STEPS = [[] for _ in UNITS]
for _i, _u in enumerate(USES):
    _at = {"level": _u[1], "turn": 8 + _u[1], "outer": 9 + _u[1], "o": 12, "ssq": 13, "rb": 14}[_u[0]]
    PE_STEPS[_at].append(_i)

N_GACT, N_GDVE = GEMM_BY.count("act"), GEMM_BY.count("dve")
N_UACT, N_UDVE = USE_BY.count("act"), USE_BY.count("dve")
NK = LEVELS + 1
NSTATE = 2 * 3 * SCAN
LN_STEPS = 18
BODY_STEPS = 40
NGROUP = FT // 2


def scan_chunk(d, n):
    if d == 0:
        return n
    return CT - 1 - n if n < CT else NT - 1 - (n - CT)


def last_unit(p):
    return max(u for u, (q, _, _) in enumerate(UNITS) if q == p)


def kernel_program(nc, x, ctx, w_mod, w_in, w_out, ffn_w_gate, ffn_w_up, ffn_w_down,
                   conv_dw_w, vectors, ident_in, masks_in, out):
    with ExitStack() as es:
        free = [(nc.sbuf_base + 31) // 32 * 32]
        spot = {}

        def sb(name, shape, dt=F32, offset=None):
            if offset is None:
                offset = free[0]
                free[0] += (int(np.prod(shape[1:])) * (1 if dt == U8 else 4) + 31) // 32 * 32
            spot[name] = offset
            return nc.alloc_sbuf_tensor_at(name, shape, dt, offset=offset)

        RAW = 3
        raw = sb("raw", [P, RAW, DM])
        split = sb("split", [P, 2, 2, DM], F32R)
        ident = sb("ident", [P, P])
        masks = sb("masks", [P, LEVELS, P], U8)
        vec = sb("vec", [P, NVEC])
        taps = sb("taps", [P, 4, TAPS])
        mod = sb("mod", [P, 6, KT, 2])
        gain = sb("gain", [P, KT, 2])
        gain2 = sb("gain2", [P, KT])
        gate = sb("gate", [P, 2, KT])
        silc = sb("silc", [P, KT, 2])
        silt = sb("silt", [P, 2, KT])
        lb = sb("lb", [P, 3, 8])
        lbt = sb("lbt", [P, 3, 8])
        ones = sb("ones", [P, P])
        eps = sb("eps", [P, 1])
        ss = sb("ss", [P, 2, NT])
        rr = sb("rr", [P, 2, NT])
        hss = sb("hss", [P, 2, XT])

        hT = sb("hT", [P, 2, KT, TOK], F32R)
        A0 = spot["hT"]
        cat = sb("cat", [P, 8, SEQ])
        W0 = free[0]
        F = sb("F", [P, 2, TOK])
        K = sb("K", [P, 2, TOK])
        Q = sb("Q", [P, 2, SEQ])
        qraw = sb("qraw", [P, SEQ])
        T = sb("T", [P, 2, TOK // 2])
        V = sb("V", [P, NT, P])
        AT = sb("AT", [P, SEQ])
        S = sb("S", [P, 2, XT, P])
        KC = sb("KC", [P, SEQ], offset=spot["S"])
        KTok = sb("KTok", [P, 2, 3, P])
        U = sb("U", [P, SEQ])
        assert free[0] <= nc.sbuf_usable_end, (free[0], nc.sbuf_usable_end)

        xst = sb("xst", [P, NT, DM], offset=W0)
        xfull = sb("xfull", [P, 2, KT, P], offset=W0 + 40960)
        vrow = sb("vrow", [P, P], offset=W0 + 49152)
        trow = sb("trow", [P, 4 * P], offset=W0 + 49152 + 512)
        junk = sb("junk", [P, DM], offset=W0 + 49152 + 2560)
        mask32 = sb("mask32", [P, LEVELS, P], offset=W0 + 49152 + 2560 + 4096)
        mraw = sb("mraw", [P, KT, DM], offset=spot["cat"])
        mrow = sb("mrow", [P, 2, DM], offset=A0 + 32768)
        mraw2 = sb("mraw2", [P, KT, DM], offset=A0)
        XT0 = A0 + 65536
        catS = sb("catS", [P, 2, 2, KT, BANK], F32R, offset=A0)
        Gb = sb("Gb", [P, DM], offset=XT0)
        x1t = sb("x1t", [P, 3, DM], offset=XT0 + 4096)
        rstd = sb("rstd", [P, SEQ], offset=XT0 + 4096)
        lnsg = sb("lnsg", [P, 2, SEQ], offset=XT0 + 8192)
        woA = sb("woA", [P, 6, 2, DM], F32R, offset=W0)
        mixt = sb("mixt", [P, DM], offset=W0 + 49152)
        vtmp = sb("vtmp", [P, 2, BANK], offset=W0 + 49152)
        x2t = sb("x2t", [P, KT, P], offset=W0 + 53248)
        h2f = sb("h2f", [P, KT, P], offset=W0 + 57344)
        h2T = [sb("h2Ta", [P, 2, KT, BANK], F32R, offset=spot["cat"]),
               sb("h2Tb", [P, 2, KT, BANK], F32R, offset=A0)]
        y = sb("y", [P, XT, DM], offset=A0 + 32768)
        sgm = sb("sgm", [P, 2, BANK], offset=XT0 + 4096)
        slotX = sb("slotX", [P, 2, DM], F32R, offset=XT0 + 8192)
        mid = sb("mid", [P, 2, 2, 2, SEQ], F32R, offset=W0)
        more = sb("more", [P, 3, 2, DM], F32R, offset=W0 + 32768)
        mid32 = sb("mid32", [P, 2, BANK], offset=W0 + 57344)
        xres = sb("xres", [P, XT, DM], offset=spot["cat"])
        junk2 = sb("junk2", [P, DM], offset=A0)

        def wo_part(q, k):
            return woA[:, k, q] if k < 6 else split[:, k - 6, q]

        def ffn_part(q, j):
            return split[:, j, q] if j < 2 else (more[:, j - 2, q] if j < 5 else slotX[:, q])

        bank = [es.enter_context(nc.psum_tensor(f"bank{i}", [P, BANK], F32)) for i in range(8)]
        x1_dram = nc.dram_tensor("x1_scratch", [SEQ, DM], F32, kind="Internal").ap()

        def sem(name):
            return es.enter_context(nc.semaphore(name))

        small_in = sem("small_in")
        x_in = [sem(f"x_in{i}") for i in range(NT)]
        mod_in = [sem(f"mod_in{i}") for i in range(8)]
        raw_in = [sem(f"raw_in{i}") for i in range(RAW)]
        x1_in = [sem(f"x1_in{i}") for i in range(3)]
        x1_store = [sem(f"x1_store{i}") for i in range(3)]
        res_in = [sem(f"res_in{i}") for i in range(XT)]
        out_done = [sem(f"out_done{i}") for i in range(XT)]
        pe_cols, cols_done, sil_sig, lb_exp = sem("pe_cols"), sem("cols_done"), sem("sil_sig"), sem("lb_exp")
        mod_full, mod_row, mod_turned, mod_done = (sem("mod_full"), sem("mod_row"), sem("mod_turned"),
                                                   sem("mod_done"))
        x_root, xn_ready, xp_full, xp_free = sem("x_root"), sem("xn_ready"), sem("xp_full"), sem("xp_free")
        h_hi, h_lo = sem("h_hi"), sem("h_lo")
        w_hi, w_lo = sem("w_hi"), sem("w_lo")
        gemm_full, gemm_act, gemm_dve, g_sig = sem("gemm_full"), sem("gemm_act"), sem("gemm_dve"), sem("g_sig")
        use_full, use_act, use_dve = sem("use_full"), sem("use_act"), sem("use_dve")
        k_ready, kc_ready, q_ready = sem("k_ready"), sem("kc_ready"), sem("q_ready")
        state_done, sq_ready, rs_ready, conv_done = sem("state_done"), sem("sq_ready"), sem("rs_ready"), sem("conv_done")
        ln_pe, ln_act, ln_dve = sem("ln_pe"), sem("ln_act"), sem("ln_dve")
        cat_hi, cat_lo, o_hi, o_lo = sem("cat_hi"), sem("cat_lo"), sem("o_hi"), sem("o_lo")
        g_full, g_done = sem("g_full"), sem("g_done")
        mix_full, mix_root, mix_done, x1_root = sem("mix_full"), sem("mix_root"), sem("mix_done"), sem("x1_root")
        x2_ready, h2_full, h2_free, h2_hi, h2_lo = (sem("x2_ready"), sem("h2_full"), sem("h2_free"),
                                                    sem("h2_hi"), sem("h2_lo"))
        f_hi, f_lo = sem("f_hi"), sem("f_lo")
        gu_full, gu_sig, gu_free, mid_hi, mid_lo = (sem("gu_full"), sem("gu_sig"), sem("gu_free"),
                                                    sem("mid_hi"), sem("mid_lo"))
        down_full, down_free, gu_part = sem("down_full"), sem("down_free"), sem("gu_part")
        y_root, y_normed, y_done = sem("y_root"), sem("y_normed"), sem("y_done")
        dve_step, act_step = sem("dve_step"), sem("act_step")

        class Steps:

            def __init__(self, eng, s):
                self.eng, self.s, self.base, self.n = eng, s, 0, 0

            def __call__(self, ins):
                self.n += 1
                ins.then_inc(self.s, 1)
                return self.n

            def wait(self, n=None):
                self.eng.wait_ge(self.s, self.base + (self.n if n is None else n))

        def view(t, offset, dims):
            a = t[:]
            return bass.AP(a.tensor, a.offset + offset, [list(a.ap[0])] + [list(d) for d in dims])

        def first(s):
            return isinstance(s, int) and s == 0

        def cat_tile(i):
            return cat[:, bass.ds(i, 1), :].rearrange("p o n -> p (o n)")

        xf = x.rearrange("b (t p) d -> (b t) p d", p=P)
        cf = ctx.rearrange("b (t p) d -> (b t) p d", p=P)
        outf = out.rearrange("b (t p) d -> (b t) p d", p=P)
        wm = w_mod.rearrange("l (k p) (m n) -> (l m) k p n", p=P, m=6)
        win = w_in.rearrange("l (k p) n -> (l p) k n", p=P)
        wo = w_out.rearrange("l (k p) n -> (l k) p n", p=P)
        wg = ffn_w_gate.rearrange("l (k p) n -> (l p) k n", p=P)
        wu = ffn_w_up.rearrange("l (k p) n -> (l p) k n", p=P)
        wd = ffn_w_down.rearrange("l (k p) n -> (l k) p n", p=P)

        MODS = [1, 0, 2, 3, 4, 5]
        MOD_STEPS = [(2, k) for k in range(KT)]
        for _n in range(3, 6):
            MOD_STEPS += [(_n, 0), (_n, 1), (_n - 1, KT)] + [(_n, k) for k in range(2, KT)]
        MOD_STEPS += [(5, KT)]
        MOD_LAG = 2

        def mod_steps_after(i):
            if i == NUSE - 1:
                return MOD_STEPS[max(0, i - MOD_LAG):]
            return MOD_STEPS[i - MOD_LAG:i - MOD_LAG + 1] if i >= MOD_LAG else []

        SLOT_TILES = [[p for p in range(NTILE) if p % RAW == r] for r in range(RAW)]

        def head_fill(s, p):
            mine = SLOT_TILES[p % RAW]
            return s * len(mine) + (mine.index(p) + 1)

        def late_fill(i):
            return HEADS * len(SLOT_TILES[i % RAW]) + i // RAW + 1

        def ffn_rounds(eng, body):
            body(0, 0)
            body(1, 1)
            with eng.Fori(0, (NGROUP - 3) // 2) as r:
                body(r * 2 + 2, 0)
                body(r * 2 + 3, 1)
            body(NGROUP - 1, (NGROUP - 1) % 2)

        def gu_no(n, j):
            return j if first(n) else n * 6 + (j - 2)

        def down_no(n, j):
            if isinstance(n, int) and n == NGROUP - 1:
                return 6 * NGROUP - 2 + j
            return n * 6 + (8 + j)

        block = es.enter_context(nc.Block())

        @block.sync
        def _(sp):
            sp.dma_start(vrow[0:NVEC, :], vectors).then_inc(small_in, 16)
            sp.dma_start(trow[0:TAPS, :], conv_dw_w.rearrange("l t n -> (l t) n")).then_inc(small_in, 16)
            sp.dma_start(ident[:], ident_in).then_inc(small_in, 16)
            sp.dma_start(mask32[:], masks_in).then_inc(small_in, 16)

            def load_x(t):
                sp.dma_start(xst[:, t, :], cf[t] if t < CT else xf[t - CT]).then_inc(x_in[t], 16)

            def load_mod(n):
                for k in range(KT):
                    if n == 2 and k == 0:
                        sp.wait_ge(gemm_full, HEADS * NUNIT)
                    if n and n != 2:
                        sp.wait_ge(mod_full, (n - 1) * KT + k + 1)
                    sp.dma_start((mraw if n < 2 else mraw2)[:, k, :], wm[MODS[n], k]).then_inc(mod_in[k], 16)

            def load_tile(s, p):
                col = (s - 1) * P + (P + TILES[p][1])
                if p >= RAW:
                    sp.wait_ge(w_lo, s * NTILE + (p - RAW + 1))
                elif not first(s):
                    sp.wait_ge(w_lo, s * NTILE + (SLOT_TILES[p][-1] + 1 - NTILE))
                sp.dma_start(raw[:, p % RAW, :].rearrange("p (k n) -> p k n", k=KT),
                             win[:, :, bass.ds(col, P)]).then_inc(raw_in[p % RAW], 16)

            load_mod(0)
            for t in range(2):
                load_x(t)
                load_tile(0, t)
            load_mod(1)
            for t in range(2, NT):
                load_x(t)
            for p in range(2, NTILE):
                load_tile(0, p)
            with sp.Fori(1, HEADS) as s:
                for p in range(NTILE):
                    load_tile(s, p)

            for i in range(KT):
                if i == RAW:
                    for n in range(2, 6):
                        load_mod(n)
                if i < RAW:
                    sp.wait_ge(w_lo, (HEADS - 1) * NTILE + SLOT_TILES[i][-1] + 1)
                else:
                    sp.wait_ge(o_lo, i - RAW + 1)
                sp.dma_start(raw[:, i % RAW, :], wo[i]).then_inc(raw_in[i % RAW], 16)

            def load_ffn(n, no, r, kind):
                row = n * 2 + int(kind[1])
                at = row if kind[0] == "d" else row * P
                at = at if isinstance(at, int) else sp.snap(at)
                if isinstance(no, int) and no < RAW:
                    sp.wait_ge(o_lo, KT + no - RAW + 1)
                else:
                    sp.wait_ge(f_lo, no - (RAW - 1))
                if kind[0] == "d":
                    sp.dma_start(raw[:, r, :].rearrange("p (o n) -> p o n", o=1),
                                 wd[bass.ds(at, 1)].rearrange("o p n -> p o n")).then_inc(raw_in[r], 16)
                else:
                    w = wg if kind[0] == "g" else wu
                    sp.dma_start(raw[:, r, :].rearrange("p (k n) -> p k n", k=KT),
                                 w[:, :, bass.ds(at, P)]).then_inc(raw_in[r], 16)

            GU = ["g0", "u0", "g1", "u1"]
            for j in range(RAW):
                load_ffn(0, j, (KT + j) % RAW, GU[j])

            for t in range(XT + 2):
                if t < XT:
                    if t == 0:
                        sp.wait_ge(cat_lo, 2 * KT)
                    if t >= 3:
                        sp.wait_ge(x1_store[t % 3], 16 * (t // 3))
                        sp.wait_ge(x2_ready, t - 2)
                    sp.dma_start(x1t[:, t % 3, :], xf[t]).then_inc(x1_in[t % 3], 16)
                if t >= 2:
                    sp.wait_ge(mix_done, t - 1)
                    sp.dma_start(x1_dram[(t - 2) * P:(t - 1) * P, :],
                                 x1t[:, (t - 2) % 3, :]).then_inc(x1_store[(t - 2) % 3], 16)

            load_ffn(0, RAW, (KT + RAW) % RAW, GU[RAW])

            def round_loads(n, par):
                if not first(n):
                    for j in range(2):
                        load_ffn(n - 1, down_no(n - 1, j), (KT + 2 + j) % RAW, f"d{j}")
                if not (isinstance(n, int) and n == NGROUP - 1):
                    for j in range(4):
                        load_ffn(n + 1, gu_no(n + 1, j), (KT + 4 + j) % RAW, GU[j])

            ffn_rounds(sp, round_loads)
            for j in range(2):
                no = down_no(NGROUP - 1, j)
                load_ffn(NGROUP - 1, no, (KT + no) % RAW, f"d{j}")

            for t in range(3):
                sp.wait_ge(x1_store[t], 16 * len(range(t, XT, 3)))
            sp.wait_ge(gu_full, 8 * NGROUP)
            for t in range(XT):
                sp.dma_start(xres[:, t, :], x1_dram[t * P:(t + 1) * P, :]).then_inc(res_in[t], 16)
            for t in range(XT):
                sp.wait_ge(y_done, t + 1)
                sp.dma_start(outf[t], xres[:, t, :]).then_inc(out_done[t], 16)
            for t in range(XT):
                sp.wait_ge(out_done[t], 16)

        @block.tensor
        def _(pe):
            def mm(o, l, r, start, stop):
                return pe.matmul(o, l, r, start=start, stop=stop, skip_group_check=True)

            def product(o, a, b, start, stop):
                mm(o, a[0], b[0], start, False)
                mm(o, a[0], b[1], False, False)
                return mm(o, a[1], b[0], False, stop)

            pe.wait_ge(small_in, 16 * 4)
            pe.transpose(bank[0][:, 0:NVEC], vrow[0:NVEC, :], ident[0:NVEC, 0:NVEC]).then_inc(pe_cols, 1)
            for j in range(4):
                ins = pe.transpose(bank[1][:, j * TAPS:(j + 1) * TAPS], trow[0:TAPS, j * P:(j + 1) * P],
                                   ident[0:TAPS, 0:TAPS])
            ins.then_inc(pe_cols, 1)

            def mod_step(n, k):
                b0, bt = (LBASE + 2 * n, 7) if n < 2 else (0, 2)
                if k < KT:
                    if k == 0 and n > 2:
                        pe.wait_ge(mod_row, n)
                    pe.wait_ge(mod_in[k], 16 * (n + 1))
                    for q in range(2):
                        ins = mm(bank[b0 + q][0:2, :], silc[:, k, :], (mraw if n < 2 else mraw2)[:, k, q * BANK:(q + 1) * BANK],
                                 k == 0, k == KT - 1)
                    ins.then_inc(mod_full, 1)
                else:
                    pe.wait_ge(mod_row, n + 1)
                    if n:
                        pe.wait_ge(mod_done, n)
                    for j in range(KT):
                        c0 = (n % 4) * 2 * KT + 2 * j
                        ins = pe.transpose(bank[bt][:, c0:c0 + 2], mrow[0:2, n % 2, j * P:(j + 1) * P], ident[0:2, 0:2])
                    ins.then_inc(mod_turned, 1)

            pe.wait_ge(cols_done, 2)
            for n in range(2):
                for k in range(KT + 1):
                    mod_step(n, k)

            def turn_x(t):
                pe.wait_ge(xn_ready, t + 1)
                for half in range(2):
                    n = 2 * t + half
                    if n >= 4:
                        pe.wait_ge(xp_free, n - 3)
                    for k in range(4):
                        kk = half * 4 + k
                        ins = pe.transpose(bank[LBASE + n % 4][:, k * P:(k + 1) * P], xst[:, t, kk * P:(kk + 1) * P],
                                           ident[:])
                    ins.then_inc(xp_full, 1)

            def wait_bank(by, ring, i, s, act_sem, dve_sem):
                who, k, ago = ring_wait(by, ring, i)
                n = by.count(who)
                pe.wait_ge(act_sem if who == "act" else dve_sem, s * n + ((1 - ago) * n + k + 1))

            def project(s, u):
                p, kind, n = UNITS[u]
                b = bank[u % GRING]
                if n == 0:
                    pe.wait_ge(w_lo, s * NTILE + (p + 1))
                wait_bank(GEMM_BY, GRING, u, s, gemm_act, gemm_dve)

                def w(k):
                    return [split[:, p % 2, q, k * P:(k + 1) * P] for q in range(2)]

                if kind == "v":
                    for t in range(4 * n, min(4 * n + 4, NT)):
                        for k in range(KT):
                            ins = product(b[:, (t % 4) * P:(t % 4 + 1) * P],
                                          [hT[:, q, k, t * P:(t + 1) * P] for q in range(2)], w(k),
                                          k == 0, k == KT - 1)
                else:
                    t0 = n * BANK if kind in ("ff", "fb") else CTX + n * BANK
                    wd_ = min(BANK, TOK - t0)
                    for k in range(KT):
                        ins = product(b[:, 0:wd_], w(k), [hT[:, q, k, t0:t0 + wd_] for q in range(2)],
                                      k == 0, k == KT - 1)
                ins.then_inc(gemm_full, 1)

            def use(h, i):
                kind, a1, a2 = USES[i]
                b = bank[LBASE + i % LRING]
                wait_bank(USE_BY, LRING, i, h, use_act, use_dve)
                if kind == "level":
                    l, hf = a1, a2
                    if hf == 0 and l == 0:
                        pe.wait_ge(k_ready, h * NK + 1)
                    elif hf == 0:
                        pe.wait_ge(kc_ready, h * LEVELS + l)
                        pe.wait_ge(q_ready, h * NK + l)
                    for cc in range(4):
                        ch = hf * 4 + cc
                        o = b[:, cc * P:(cc + 1) * P]
                        if l == 0:
                            tk = CTX + ch * P
                            mm(o, K[:, 0, tk:tk + P], qraw[:, ch * P:(ch + 1) * P], True, False)
                            ins = mm(o, K[:, 1, tk:tk + P], qraw[:, ch * P:(ch + 1) * P], False, True)
                        else:
                            bs = 1 << (l - 1)
                            q = view(Q, ch * P, [(2 * bs, P // (2 * bs)), (SEQ + bs, 2), (1, bs)])
                            ins = mm(o, KC[:, ch * P:(ch + 1) * P], q, True, True)
                elif kind == "turn":
                    if a1 == 0 and a2 == 0:
                        pe.wait_ge(k_ready, h * NK + NK)
                    for j in range(3):
                        ch = scan_chunk(a2, 3 * a1 + j)
                        ins = pe.transpose(b[:, j * P:(j + 1) * P], K[:, a2, ch * P:(ch + 1) * P], ident[:])
                elif kind == "outer":
                    if a2 == 0:
                        if a1 == 0:
                            pe.wait_ge(gemm_act, h * N_GACT + 2 * N_GACT)
                        pe.wait_ge(use_act, h * N_UACT + (N_UACT + 2 + 2 * a1 + 2))
                    for j in range(3):
                        ch = scan_chunk(a2, 3 * a1 + j)
                        ins = mm(b[:, j * P:(j + 1) * P], KTok[:, a2, j, :], V[:, ch, :], True, True)
                elif kind == "o":
                    if a1 == 0:
                        pe.wait_ge(state_done, h * NSTATE + NSTATE)
                        pe.wait_ge(q_ready, h * NK + NK)
                        pe.wait_ge(use_dve, h * N_UDVE + (N_UDVE + 2 * LEVELS))
                    for cc in range(4):
                        ch = a1 * 4 + cc
                        o = b[:, cc * P:(cc + 1) * P]
                        sl = slice(ch * P, (ch + 1) * P)
                        mm(o, V[:, CT + ch, :], AT[:, sl], True, False)
                        mm(o, S[:, 0, ch, :], Q[:, 1, sl], False, False)
                        ins = mm(o, S[:, 1, XT - 1 - ch, :], Q[:, 0, sl], False, True)
                elif kind == "ssq":
                    pe.wait_ge(sq_ready, h * 2 + 2)
                    for ch in range(XT):
                        ins = mm(b[:, ch:ch + 1], AT[:, ch * P:(ch + 1) * P], ones[:, 0:1], True, True)
                else:
                    if a1 == 0:
                        pe.wait_ge(rs_ready, h + 1)
                    for cc in range(4):
                        ins = mm(b[:, cc * P:(cc + 1) * P], view(hss, XT + a1 * 4 + cc, [(0, P)]), ident[:],
                                 True, True)
                ins.then_inc(use_full, 1)

            for t in range(7):
                turn_x(t)
            pe.wait_ge(h_lo, 4)
            project(0, 0)
            for t in range(7, NT):
                turn_x(t)
            for u in range(1, NUNIT):
                if u <= 2:
                    pe.wait_ge(h_lo, min(4 * u + 4, NT))
                project(0, u)
            pe.wait_ge(xp_free, 2 * NT)
            pe.wait_ge(mod_done, 2)
            with pe.Fori(1, HEADS) as s:
                for u in range(NUNIT):
                    project(s, u)
                    for i in PE_STEPS[u]:
                        use(s - 1, i)
            pe.wait_ge(gemm_act, (HEADS + 1) * N_GACT)
            pe.wait_ge(gemm_dve, (HEADS + 1) * N_GDVE)
            for i in range(NUSE):
                use(HEADS - 1, i)
                for n, k in mod_steps_after(i):
                    mod_step(n, k)

            pe.wait_ge(conv_done, HEADS)
            for hf in range(2):
                for j in range(4):
                    ins = mm(bank[hf][:], ones[:], cat[:, 4 + j, hf * BANK:(hf + 1) * BANK], j == 0, j == 3)
                ins.then_inc(ln_pe, 1)
            pe.wait_ge(use_dve, (HEADS + 1) * N_UDVE)
            pe.wait_ge(use_act, (HEADS + 1) * N_UACT)
            pe.wait_ge(mod_done, 6)
            for hf in range(2):
                for j in range(4):
                    pe.wait_ge(ln_act, hf * 4 + j + 1)
                    ins = mm(bank[2 + hf][:], ones[:], vtmp[:, j % 2, :], j == 0, j == 3)
                    ins.then_inc(ln_pe, 1)

            def gate_rows(i):
                for j in range(KT):
                    ins = mm(bank[4 + j // 4][:, (j % 4) * P:(j % 4 + 1) * P], view(gate, i * KT + j, [(0, P)]),
                             ident[:], True, True)
                ins.then_inc(g_full, 1)

            gate_rows(0)

            def mix(t):
                hf, tt = t // 4, t % 4
                for n in range(2):
                    i = 2 * t + n
                    if i >= 4:
                        pe.wait_ge(mix_done, t - 1)
                    for k in range(KT):
                        if t == 0 and n == 0:
                            pe.wait_ge(cat_lo, 2 * k + 2)
                            pe.wait_ge(o_lo, k + 1)
                            if k == 0:
                                pe.wait_ge(ln_dve, 10)
                        ins = product(bank[i % 4][:], [catS[:, hf, q, k, tt * P:(tt + 1) * P] for q in range(2)],
                                      [wo_part(q, k)[:, n * BANK:(n + 1) * BANK] for q in range(2)],
                                      k == 0, k == KT - 1)
                    ins.then_inc(mix_full, 1)

            def turn2(t):
                pe.wait_ge(x2_ready, t + 1)
                for half in range(2):
                    if t >= 1:
                        pe.wait_ge(h2_free, 2 * t - 1 + half)
                    for k in range(4):
                        ins = pe.transpose(bank[6 + half][:, k * P:(k + 1) * P], x2t[:, half * 4 + k, :], ident[:])
                    ins.then_inc(h2_full, 1)

            for t in range(XT + 2):
                if t < XT:
                    mix(t)
                if t >= 2:
                    turn2(t - 2)
            pe.wait_ge(g_done, 1)
            gate_rows(1)

            def gate_up(n, fi):
                pe.wait_ge(f_lo, gu_no(n, 2 * fi + 1) + 1)
                for hf in range(2):
                    if first(n) and fi == 0:
                        pe.wait_ge(mix_done, XT)
                        pe.wait_ge(h2_lo, 4 * hf + 4)
                    else:
                        pe.wait_ge(gu_free, n * 4 + (2 * fi + hf - 1))
                    for j in range(2):
                        b = bank[2 * hf + j]
                        for k in range(KT):
                            ins = product(b[:], [ffn_part(q, 2 * fi + j)[:, k * P:(k + 1) * P] for q in range(2)],
                                          [h2T[hf][:, q, k, :] for q in range(2)], k == 0, k == KT - 1)
                        ins.then_inc(gu_full, 1)

            def down(n, par):
                pe.wait_ge(f_lo, down_no(n, 1) + 1)
                pe.wait_ge(mid_lo, n * 4 + 4)
                for i in range(2 * XT):
                    t, hf = i // 2, i % 2
                    pe.wait_ge(down_free, n * 16 + (i + 1))
                    for fi in range(2):
                        ins = product(bank[4 + i % 4][:], [mid[:, par, fi, q, t * P:(t + 1) * P] for q in range(2)],
                                      [ffn_part(q, 4 + fi)[:, hf * BANK:(hf + 1) * BANK] for q in range(2)],
                                      fi == 0, fi == 1)
                    ins.then_inc(down_full, 1)

            def pe_round(n, par):
                gate_up(n, 0)
                gate_up(n, 1)
                if first(n):
                    pe.wait_ge(g_done, 2)
                    pe.wait_ge(h2_free, 2 * XT)
                else:
                    down(n - 1, 1 - par)

            ffn_rounds(pe, pe_round)
            down(NGROUP - 1, (NGROUP - 1) % 2)

        @block.scalar
        def _(act):
            step = Steps(act, act_step)

            act.wait_ge(pe_cols, 1)
            act.activation(silt[:], bank[0][:, 0:2 * KT].rearrange("p (a k) -> p a k", a=2),
                           ACT.Sigmoid).then_inc(sil_sig, 1)
            act.wait_ge(cols_done, 1)
            act.activation(lbt[:, 1, :], lbt[:, 0, :], ACT.Exp).then_inc(lb_exp, 1)

            act.wait_ge(cols_done, 2)

            def x_rms(t):
                act.wait_ge(x_in[t], 16)
                if step.n:
                    step.wait()
                step(act.activation(junk[:], xst[:, t, :], ACT.Square, accum_out=ss[:, 0, t:t + 1]))
                step.wait()
                act.activation(ss[:, 1, t:t + 1], ss[:, 0, t:t + 1], ACT.Sqrt, bias=eps[:], scale=1.0 / DM).then_inc(x_root, 1)

            def mod_rows(n):
                b0 = LBASE + 2 * n if n < 2 else 0
                act.wait_ge(mod_full, KT * (n + 1))
                if n >= 2:
                    act.wait_ge(mod_turned, n - 1)
                for q in range(2):
                    ins = act.activation(mrow[0:2, n % 2, q * BANK:(q + 1) * BANK], bank[b0 + q][0:2, :], ACT.Copy)
                ins.then_inc(mod_row, 1)

            act.sem_inc(gemm_act, N_GACT)
            act.sem_inc(use_act, N_UACT)

            def head_hi(s, p):
                act.wait_ge(raw_in[p % RAW], head_fill(s, p) * 16)
                if p >= 2:
                    act.wait_ge(gemm_full, s * NUNIT + (last_unit(p - 2) + 1))
                elif not first(s):
                    act.wait_ge(gemm_full, s * NUNIT + (last_unit(6 - p) + 1 - NUNIT))
                act.activation(split[:, p % 2, 0], raw[:, p % RAW, :], ACT.Copy).then_inc(w_hi, 1)

            mod_rows(0)
            for t in range(2):
                x_rms(t)
                head_hi(0, t)
            mod_rows(1)
            for t in range(NT):
                if t + 2 < NT:
                    x_rms(t + 2)
                act.wait_ge(xp_free, 2 * t + 2)
                act.activation(hT[:, 0, :, t * P:(t + 1) * P], xfull[:, t % 2], ACT.Copy).then_inc(h_hi, 1)

            def evac(s, u):
                p, kind, n = UNITS[u]
                if kind == "a":
                    return
                act.wait_ge(gemm_full, s * NUNIT + (u + 1))
                b = bank[u % GRING]
                sl = slice(n * BANK, (n + 1) * BANK)
                if kind in ("ff", "fb"):
                    w = min(BANK, TOK - n * BANK)
                    if u == 0 and not first(s):
                        act.wait_ge(q_ready, s * NK + (2 - NK))
                    act.activation(F[:, 0 if kind == "ff" else 1, n * BANK:n * BANK + w], b[:, 0:w],
                                   ACT.Sigmoid).then_inc(gemm_act, 1)
                elif kind == "q":
                    act.activation(qraw[:, sl], b[:], ACT.Copy, scale=float(P) ** -0.5).then_inc(gemm_act, 1)
                elif kind == "g":
                    act.activation(cat_tile(s)[:, sl], b[:], ACT.Sigmoid).then_inc(g_sig, 1)
                elif kind == "b":
                    if n == 0 and not first(s):
                        act.wait_ge(conv_done, s)
                    act.activation(U[:, sl], b[:], ACT.Sigmoid).then_inc(gemm_act, 1)
                else:
                    w = min(4, NT - 4 * n)
                    if n == 0 and not first(s):
                        act.wait_ge(use_full, s * NUSE + (USES.index(("o", 1, 0)) + 1 - NUSE))
                    act.activation(V[:, 4 * n:4 * n + w, :], b[:, 0:w * P].rearrange("p (t v) -> p t v", v=P),
                                   ACT.Copy).then_inc(gemm_act, 1)

            def level_keys(h, l):
                bs = 1 << (l - 1)
                act.wait_ge(k_ready, h * NK + l)
                if l > 1:
                    act.wait_ge(use_full, h * NUSE + 2 * l)
                act.activation(view(KC, 0, [(2 * bs, SEQ // (2 * bs)), (bs, 2), (1, bs)]),
                               view(K, CTX, [(2 * bs, SEQ // (2 * bs)), (TOK + bs, 2), (1, bs)]),
                               ACT.Copy).then_inc(kc_ready, 1)

            def act_use(h, i):
                kind, a1, a2 = USES[i]
                b = bank[LBASE + i % LRING]
                if kind == "level" and a1 == 0:
                    act.wait_ge(use_full, h * NUSE + (i + 1))
                    act.activation(AT[:, a2 * BANK:(a2 + 1) * BANK], b[:], ACT.Copy).then_inc(use_act, 1)
                elif kind == "turn":
                    act.wait_ge(use_full, h * NUSE + (i + 1))
                    if a1 > 0:
                        act.wait_ge(use_full, h * NUSE + (USES.index(("outer", a1 - 1, a2)) + 1))
                    act.activation(KTok[:, a2], b[:, 0:3 * P].rearrange("p (j n) -> p j n", n=P),
                                   ACT.Copy).then_inc(use_act, 1)
                elif kind == "o":
                    act.wait_ge(use_full, h * NUSE + (USES.index(("o", 1, 0)) + 1))
                    act.activation(AT[:, a1 * BANK:(a1 + 1) * BANK], b[:], ACT.Square).then_inc(sq_ready, 1)
                elif kind == "ssq":
                    act.wait_ge(use_full, h * NUSE + (i + 1))
                    act.activation(hss[:, 0, :], b[:, 0:XT], ACT.Sqrt, bias=eps[:], scale=1.0 / P).then_inc(use_act, 1)

            def act_body(s, gemm, rec):
                for u in range(NUNIT):
                    if gemm:
                        p, _, n = UNITS[u]
                        if u == 0 and not first(s):
                            head_hi(s, 0)
                            head_hi(s, 1)
                        if u:
                            evac(s, u)
                        if n == 0 and 1 <= p < NTILE - 1:
                            head_hi(s, p + 1)
                    if rec:
                        for i in PE_STEPS[u]:
                            act_use(s - 1, i)
                            if not gemm:
                                for n, k in mod_steps_after(i):
                                    if k == KT - 1:
                                        mod_rows(n)
                        if u < LEVELS:
                            level_keys(s - 1, u + 1)
                    if gemm and u == 0:
                        evac(s, u)

            act_body(0, True, False)
            with act.Fori(1, HEADS) as s:
                act_body(s, True, True)
            act_body(HEADS, False, True)

            def cat_parts(j):
                for hf in range(2):
                    act.activation(catS[:, hf, 0, j, :], cat[:, j, hf * BANK:(hf + 1) * BANK],
                                   ACT.Copy).then_inc(cat_hi, 1)

            for n in range(8):
                hf, j = n // 4, n % 4
                act.wait_ge(ln_dve, n + 1)
                if n >= 2:
                    act.wait_ge(ln_pe, n + 1)
                act.activation(vtmp[:, n % 2, :], cat[:, 4 + j, hf * BANK:(hf + 1) * BANK],
                               ACT.Square).then_inc(ln_act, 1)
            for hf in range(2):
                act.wait_ge(ln_pe, 6 + 4 * hf)
                act.activation(rstd[:, hf * BANK:(hf + 1) * BANK], bank[2 + hf][:], ACT.Sqrt, bias=eps[:],
                               scale=1.0 / BANK).then_inc(ln_act, 1)
            act.wait_ge(use_dve, (HEADS + 1) * N_UDVE)
            act.wait_ge(mod_turned, 6)
            for j in range(4):
                cat_parts(j)
            for j in range(4):
                act.wait_ge(ln_dve, 11 + j)
                if j >= 2:
                    act.wait_ge(ln_dve, 13 + j)
                act.activation(lnsg[:, j % 2, :], cat[:, 4 + j, :], ACT.Sigmoid, scale=vec[:, R_LNG + j:R_LNG + j + 1],
                               bias=vec[:, R_LNB + j:R_LNB + j + 1]).then_inc(ln_act, 1)

            def wo_hi(i):
                act.wait_ge(raw_in[i % RAW], 16 * late_fill(i))
                act.activation(wo_part(0, i), raw[:, i % RAW, :], ACT.Copy).then_inc(o_hi, 1)

            for i in range(4):
                wo_hi(i)
            for j in range(4, 8):
                act.wait_ge(ln_dve, LN_STEPS - 7 + j)
                cat_parts(j)
                wo_hi(j)

            def mix_roots(t):
                for n in range(2):
                    act.wait_ge(mix_full, 2 * t + n + 1)
                    if t and n == 0:
                        act.wait_ge(mix_done, t)
                    step(act.activation(mixt[:, n * BANK:(n + 1) * BANK], bank[(2 * t + n) % 4][:], ACT.Square,
                                        accum_out=ss[:, n, t:t + 1]))
                step.wait()
                step(act.activation(rr[:, 0, t:t + 1], ss[:, 0, t:t + 1], ACT.Identity, bias=ss[:, 1, t:t + 1]))
                step.wait()
                act.activation(rr[:, 1, t:t + 1], rr[:, 0, t:t + 1], ACT.Sqrt, bias=eps[:],
                               scale=1.0 / DM).then_inc(mix_root, 1)
                act.wait_ge(mix_done, t + 1)
                if t:
                    act.wait_ge(h2_full, 2 * t)
                step(act.activation(x2t[:].rearrange("p k n -> p (k n)"), x1t[:, t % 3, :], ACT.Square,
                                    accum_out=ss[:, 0, t:t + 1]))
                step.wait()
                act.activation(rr[:, 0, t:t + 1], ss[:, 0, t:t + 1], ACT.Sqrt, bias=eps[:],
                               scale=1.0 / DM).then_inc(x1_root, 1)

            def h2_part(t):
                act.wait_ge(h2_free, 2 * t + 2)
                act.activation(h2T[t // 4][:, 0, :, (t % 4) * P:(t % 4 + 1) * P], h2f[:], ACT.Copy).then_inc(h2_hi, 1)

            for t in range(XT + 1):
                if t < XT:
                    mix_roots(t)
                if t >= 1:
                    h2_part(t - 1)

            def gu_hi(n, j):
                if first(n):
                    if j == 0:
                        act.wait_ge(mix_full, 2 * XT)
                        act.wait_ge(x2_ready, XT)
                        for q in range(3):
                            act.wait_ge(x1_store[q], 16 * len(range(q, XT, 3)))
                    act.wait_ge(raw_in[(KT + j) % RAW], 16 * late_fill(KT + j))
                else:
                    act.wait_ge(gu_full, n * 8 + (4 * (j // 2) + 4 - 8))
                    r = (KT + 4 + j) % RAW
                    act.wait_ge(raw_in[r], n * 32 + 16 * (late_fill(KT + 4 + j) - 2))
                act.activation(ffn_part(0, j), raw[:, (KT + j + (0 if first(n) else 4)) % RAW, :],
                               ACT.Copy).then_inc(f_hi, 1)

            def down_hi(n, j):
                if not first(n):
                    act.wait_ge(down_full, n * 16)
                if isinstance(n, int) and n == NGROUP - 1:
                    late = KT + down_no(n, j)
                    r, fills = late % RAW, late_fill(late) * 16
                else:
                    r = (KT + 8 + j) % RAW
                    fills = n * 32 + 16 * late_fill(KT + 8 + j)
                act.wait_ge(raw_in[r], fills)
                act.activation(ffn_part(0, 4 + j), raw[:, r, :], ACT.Copy).then_inc(f_hi, 1)

            def act_tile(n, fi, par):
                for hf in range(2):
                    act.wait_ge(gu_full, n * 8 + (4 * fi + 2 * hf + 1))
                    if not (first(n) and fi == 0):
                        act.wait_ge(gu_free, n * 4 + (2 * fi + hf - 1))
                    act.activation(sgm[:, hf, :], bank[2 * hf][:], ACT.Sigmoid).then_inc(gu_sig, 1)
                for hf in range(2):
                    act.wait_ge(gu_free, n * 4 + (2 * fi + hf + 1))
                    if fi == 0 and hf == 0 and not (isinstance(n, int) and n < 2):
                        act.wait_ge(down_full, n * 16 - 16)
                    act.activation(mid[:, par, fi, 0, hf * BANK:(hf + 1) * BANK], mid32[:, hf, :],
                                   ACT.Copy).then_inc(mid_hi, 1)

            def act_round(n, par):
                if not first(n):
                    down_hi(n - 1, 0)
                    down_hi(n - 1, 1)
                for fi in range(2):
                    act_tile(n, fi, par)
                    if not (isinstance(n, int) and n == NGROUP - 1):
                        gu_hi(n + 1, 2 * fi)
                        gu_hi(n + 1, 2 * fi + 1)

            for j in range(4):
                gu_hi(0, j)
            ffn_rounds(act, act_round)
            down_hi(NGROUP - 1, 0)
            down_hi(NGROUP - 1, 1)

            act.wait_ge(gu_full, 8 * NGROUP)
            for t in range(XT):
                act.wait_ge(down_free, 4 + 16 * (NGROUP - 1) + 2 * t + 2)
                step.wait()
                step(act.activation(junk2[:], y[:, t, :], ACT.Square, accum_out=ss[:, 0, t:t + 1]))
                step.wait()
                act.activation(rr[:, 0, t:t + 1], ss[:, 0, t:t + 1], ACT.Sqrt, bias=eps[:],
                               scale=1.0 / DM).then_inc(y_root, 1)

        @block.gpsimd
        def _(pool):
            def lo_part(lo, full, hi):
                return pool.tensor_tensor(lo, full, hi.bitcast(F32), ALU.subtract)

            def head_lo(s, p):
                pool.wait_ge(w_hi, s * NTILE + (p + 1))
                lo_part(split[:, p % 2, 1], raw[:, p % RAW, :], split[:, p % 2, 0]).then_inc(w_lo, 1)

            for p in range(2):
                head_lo(0, p)
            for t in range(NT):
                pool.wait_ge(h_hi, t + 1)
                sl = slice(t * P, (t + 1) * P)
                lo_part(hT[:, 1, :, sl], xfull[:, t % 2], hT[:, 0, :, sl]).then_inc(h_lo, 1)
            for p in range(2, NTILE):
                head_lo(0, p)
            with pool.Fori(1, HEADS) as s:
                for p in range(NTILE):
                    head_lo(s, p)

            for i in range(KT):
                pool.wait_ge(o_hi, i + 1)
                lo_part(wo_part(1, i), raw[:, i % RAW, :], wo_part(0, i)).then_inc(o_lo, 1)
            for t in range(XT):
                pool.wait_ge(h2_hi, t + 1)
                h2, sl = h2T[t // 4], slice((t % 4) * P, (t % 4 + 1) * P)
                lo_part(h2[:, 1, :, sl], h2f[:], h2[:, 0, :, sl]).then_inc(h2_lo, 1)

            def ffn_lo(no, r, j):
                pool.wait_ge(f_hi, no + 1)
                lo_part(ffn_part(1, j), raw[:, r, :], ffn_part(0, j)).then_inc(f_lo, 1)

            for j in range(4):
                ffn_lo(j, (KT + j) % RAW, j)

            def pool_round(n, par):
                if not first(n):
                    for j in range(2):
                        ffn_lo(down_no(n - 1, j), (KT + 2 + j) % RAW, 4 + j)
                if not (isinstance(n, int) and n == NGROUP - 1):
                    for j in range(4):
                        ffn_lo(gu_no(n + 1, j), (KT + 4 + j) % RAW, j)

            ffn_rounds(pool, pool_round)
            for j in range(2):
                no = down_no(NGROUP - 1, j)
                ffn_lo(no, (KT + no) % RAW, 4 + j)

            for t in range(XT):
                pool.wait_ge(y_normed, t + 1)
                pool.wait_ge(res_in[t], 16)
                pool.tensor_tensor(xres[:, t, :], xres[:, t, :], y[:, t, :], ALU.add).then_inc(y_done, 1)

        @block.vector
        def _(dve):
            step = Steps(dve, dve_step)

            step(dve.memset(ones[:], 1.0))
            step(dve.memset(eps[:], EPS))
            dve.sem_inc(gemm_dve, N_GDVE)
            dve.sem_inc(use_dve, N_UDVE)
            dve.sem_inc(down_free, 4)
            dve.wait_ge(pe_cols, 2)
            dve.wait_ge(sil_sig, 1)
            step(dve.tensor_copy(vec[:], bank[0][:, 0:NVEC]))
            step(dve.tensor_copy(masks[:], mask32[:]))
            step(dve.tensor_copy(taps[:], bank[1][:, 0:4 * TAPS].rearrange("p (j t) -> p j t", t=TAPS)))
            step.wait()
            dve.tensor_tensor(lbt[:, 0, :], vec[:, R_LBF:R_LBF + 8], vec[:, R_LBF:R_LBF + 8],
                              ALU.subtract).then_inc(cols_done, 1)
            dve.tensor_tensor(silc[:].rearrange("p k a -> p a k"), silt[:],
                              vec[:, 0:2 * KT].rearrange("p (a k) -> p a k", a=2), ALU.mult).then_inc(cols_done, 1)
            dve.wait_ge(lb_exp, 1)
            step(dve.reciprocal(lbt[:, 2, :], lbt[:, 1, :]))
            step.wait()
            step(dve.tensor_tensor(lbt[:, 0, :], lbt[:, 1, :], lbt[:, 2, :], ALU.mult))
            step.wait()
            step(dve.tensor_tensor(lb[:, 0, :], lbt[:, 0, :], lbt[:, 0, :], ALU.subtract))
            step.wait()
            step(dve.tensor_scalar(lb[:, 1, :], lb[:, 0, :], -1.0, 1.0, ALU.mult, ALU.add))
            step(dve.tensor_scalar(lb[:, 2, :], lb[:, 0, :], 1.0, -1.0, ALU.mult, ALU.add))

            def norm_x(t):
                dve.wait_ge(x_root, t + 1)
                step(dve.reciprocal(rr[:, 0, t:t + 1], ss[:, 1, t:t + 1]))
                step.wait()
                dve.tensor_scalar(xst[:, t, :], xst[:, t, :], rr[:, 0, t:t + 1], None, ALU.mult).then_inc(xn_ready, 1)

            def mod_take(n):
                m = MODS[n]
                dve.wait_ge(mod_turned, n + 1)
                c0 = (n % 4) * 2 * KT
                dve.tensor_tensor(mod[:, m], bank[7 if n < 2 else 2][:, c0:c0 + 2 * KT].rearrange("p (k a) -> p k a", a=2),
                                  view(vec, R_BM + m * KT, [(1, KT), (0, 2)]), ALU.add).then_inc(mod_done, 1)
                dve.wait_ge(mod_done, n + 1)
                one = mod[:, m, :, 0]
                if m == 1:
                    step(dve.scalar_tensor_tensor(gain[:], mod[:, m], 1.0, view(vec, R_PREM, [(1, KT), (0, 2)]),
                                                  ALU.add, ALU.mult))
                elif m == 4:
                    step(dve.scalar_tensor_tensor(gain2[:], one, 1.0, vec[:, R_PREF:R_PREF + KT], ALU.add, ALU.mult))
                elif m in (2, 5):
                    g, r0 = (0, R_POSTM) if m == 2 else (1, R_POSTF)
                    step(dve.tensor_tensor(gate[:, g], one, vec[:, r0:r0 + KT], ALU.mult))

            norm_x(0)
            norm_x(1)
            mod_take(0)
            mod_take(1)
            step.wait()
            for t in range(NT):
                a = 1 if t < CT else 0
                for k in range(KT):
                    if k % 4 == 0:
                        dve.wait_ge(xp_full, 2 * t + k // 4 + 1)
                    if k == 0 and t >= 2:
                        dve.wait_ge(h_lo, t - 1)
                    ins = dve.tensor_scalar(xfull[:, t % 2, k, :],
                                            bank[LBASE + (2 * t + k // 4) % 4][:, (k % 4) * P:(k % 4 + 1) * P],
                                            gain[:, k, a:a + 1], mod[:, 0, k, a:a + 1], ALU.mult, ALU.add)
                    if k % 4 == 3:
                        ins.then_inc(xp_free, 1)
                if t + 2 < NT:
                    norm_x(t + 2)

            def take(s, u):
                _, kind, n = UNITS[u]
                b = bank[u % GRING]
                sl = slice(n * BANK, (n + 1) * BANK)
                if kind == "g":
                    dve.wait_ge(g_sig, s * 2 + (n + 1))
                    dve.tensor_tensor(cat_tile(s)[:, sl], b[:], cat_tile(s)[:, sl], ALU.mult).then_inc(gemm_dve, 1)
                elif kind == "a":
                    dve.wait_ge(gemm_full, s * NUNIT + (u + 1))
                    dve.wait_ge(gemm_act, s * N_GACT + (N_GACT + 8 + n + 1))
                    dve.tensor_tensor(U[:, sl], b[:], U[:, sl], ALU.mult).then_inc(gemm_dve, 1)

            def conv_view(i, t0, t1):
                return cat[:, bass.ds(i, 1), :].rearrange("p o (r c) -> p (o r) c", c=GRID)[:, :, t0:t1]

            u_rows = U[:].rearrange("p (r c) -> p r c", c=GRID)
            others = [k for k in range(TAPS) if k != PAD]

            def conv(h, n):
                def w(k):
                    return taps[:, bass.ds(h, 1), k:k + 1].rearrange("p o n -> p (o n)")
                if n < 0:
                    dve.wait_ge(gemm_dve, h * N_GDVE + 2 * N_GDVE)
                    step(dve.tensor_scalar(cat_tile(h + 4), U[:], w(PAD), vec[:, bass.ds(h + R_DWB, 1)], ALU.mult, ALU.add))
                    return
                k = others[n]
                d = k - PAD
                t0, t1 = max(0, -d), GRID - max(0, d)
                step.wait(conv_last[0])
                ins = dve.scalar_tensor_tensor(conv_view(h + 4, t0, t1), u_rows[:, :, t0 + d:t1 + d], w(k),
                                               conv_view(h + 4, t0, t1), ALU.mult, ALU.add)
                if n == len(others) - 1:
                    ins.then_inc(conv_done, 1)
                else:
                    conv_last[0] = step(ins)

            conv_last = [0]

            def rec_start(h):
                dve.wait_ge(gemm_act, h * N_GACT + (N_GACT + 8))
                for d in range(2):
                    sc = [lb[:, i, bass.ds(h + 4 * d, 1)] for i in range(3)]
                    ins = dve.tensor_scalar(K[:, d], F[:, d], sc[2], sc[1], ALU.mult, ALU.add)
                ins.then_inc(k_ready, 1)
                for d in range(2):
                    sc = [lb[:, i, bass.ds(h + 4 * d, 1)] for i in range(3)]
                    step(dve.tensor_scalar(F[:, d], F[:, d], sc[1], sc[0], ALU.mult, ALU.add))
                step.wait()
                step(dve.tensor_scalar(F[:], F[:], F_MIN, None, ALU.max))
                step.wait()
                dve.tensor_tensor(Q[:, 0], qraw[:], F[:, 1, CTX:], ALU.mult)
                dve.tensor_tensor(Q[:, 1], qraw[:], F[:, 0, CTX:], ALU.mult).then_inc(q_ready, 1)
                step(dve.tensor_tensor(T[:], view(F, 0, [(TOK, 2), (2, TOK // 2)]),
                                       view(F, 1, [(TOK, 2), (2, TOK // 2)]), ALU.mult))

            def rec_level(h, l):
                bs = 1 << (l - 1)
                half = TOK // 2
                nk, nq = TOK // (2 * bs), SEQ // (2 * bs)
                if l == 1:
                    kt = view(F, 1, [(TOK - 1, 2), (2, nk), (0, 1)])
                    qt = [view(F, TOK + CTX + 1, [(2, nq), (0, 1)]), view(F, CTX, [(2, nq), (0, 1)])]
                else:
                    kt = view(T, bs // 2, [(half - bs // 2, 2), (bs, nk), (0, bs)])
                    qt = [view(T, half + CTX // 2 + bs // 2, [(bs, nq), (0, bs)]),
                          view(T, CTX // 2, [(bs, nq), (0, bs)])]
                dve.wait_ge(kc_ready, h * LEVELS + l)
                if l == 1:
                    dve.wait_ge(use_full, h * NUSE + 2)
                dve.wait_ge(k_ready, h * NK + l)
                step.wait(t_last[0])
                kv = view(K, 0, [(TOK + bs, 2), (2 * bs, nk), (1, bs)])
                dve.tensor_tensor(kv, kv, kt, ALU.mult).then_inc(k_ready, 1)
                if l == 1:
                    dve.wait_ge(use_act, h * N_UACT + (N_UACT + 2))
                dve.wait_ge(use_full, h * NUSE + (2 * l + 2))
                dve.wait_ge(q_ready, h * NK + l)
                for i in range(2):
                    qv = view(Q, i * (SEQ + bs), [(2 * bs, nq), (1, bs)])
                    ins = dve.tensor_tensor(qv, qv, qt[i], ALU.mult)
                ins.then_inc(q_ready, 1)
                if l > 1:
                    dve.wait_ge(k_ready, h * NK + (l + 1))
                    dve.wait_ge(q_ready, h * NK + (l + 1))
                    tv = view(T, 0, [(half, 2), (bs, nk)])
                    t_last[0] = step(dve.tensor_tensor(tv, tv, view(T, bs // 2, [(half, 2), (bs, nk)]), ALU.mult))
                for hf in range(2):
                    dve.copy_predicated(view(AT, hf * BANK, [(P, 4), (1, P)]), view(masks, (l - 1) * P, [(0, 4), (1, P)]),
                                        bank[LBASE + (2 * l + hf) % LRING][:].rearrange("p (c n) -> p c n", n=P)
                                        ).then_inc(use_dve, 1)

            t_last = [0]

            def rec_states(h, g):
                for d in range(2):
                    i = USES.index(("outer", g, d))
                    dve.wait_ge(use_full, h * NUSE + (i + 1))
                    for j in range(3):
                        n = 3 * g + j
                        src = bank[LBASE + i % LRING][:, j * P:(j + 1) * P]
                        dst = S[:, d, n - 1 if n else XT - 1]
                        done = 6 * g + 3 * d + j
                        if n == 0:
                            ins = dve.tensor_copy(dst, src)
                        else:
                            prev = done - 1 if j else done - 4
                            dve.wait_ge(state_done, h * NSTATE + (prev + 1))
                            if n == 1 and d == 0:
                                step.wait(t_last[0])
                            ch = scan_chunk(d, n)
                            ins = dve.scalar_tensor_tensor(dst, S[:, d, n - 2 if n > 1 else XT - 1],
                                                           T[:, d, ch * (P // 2):ch * (P // 2) + 1], src,
                                                           ALU.mult, ALU.add)
                        ins.then_inc(state_done, 1)
                    dve.wait_ge(state_done, h * NSTATE + (6 * g + 3 * d + 3))
                    dve.sem_inc(use_dve, 1)

            def rec_out(h, u):
                if u == 12:
                    for hf in range(2):
                        dve.wait_ge(sq_ready, h * 2 + (hf + 1))
                        dve.wait_ge(gemm_dve, h * N_GDVE + (N_GDVE + 2))
                        i = USES.index(("o", hf, 0))
                        c = cat_tile(h)[:, hf * BANK:(hf + 1) * BANK]
                        dve.scalar_tensor_tensor(c, bank[LBASE + i % LRING][:], vec[:, R_ON:R_ON + 1], c,
                                                 ALU.mult, ALU.mult).then_inc(use_dve, 1)
                elif u == 13:
                    dve.wait_ge(use_act, h * N_UACT + 2 * N_UACT)
                    dve.reciprocal(hss[:, 1, :], hss[:, 0, :]).then_inc(rs_ready, 1)
                elif u == 14:
                    for hf in range(2):
                        i = USES.index(("rb", hf, 0))
                        dve.wait_ge(use_full, h * NUSE + (i + 1))
                        dve.wait_ge(use_dve, h * N_UDVE + (2 * N_UDVE - 3 + hf))
                        c = cat_tile(h)[:, hf * BANK:(hf + 1) * BANK]
                        dve.tensor_tensor(c, bank[LBASE + i % LRING][:], c, ALU.mult).then_inc(use_dve, 1)

            MOD_TAKE = {6: 2, 9: 3, 13: 4, 16: 5}

            def dve_body(s, gemm, rec):
                tap = 0
                for u in range(NUNIT):
                    if gemm:
                        take(s, u)
                    if rec:
                        h = s - 1
                        if u == 0:
                            rec_start(h)
                            t_last[0] = step.n
                            conv(h, -1)
                            conv_last[0] = step.n
                        elif u <= LEVELS:
                            rec_level(h, u)
                        elif 9 <= u < 9 + SCAN:
                            rec_states(h, u - 9)
                        else:
                            rec_out(h, u)
                        if 1 <= u <= 8:
                            for _ in range(4):
                                if tap < len(others):
                                    conv(h, tap)
                                    tap += 1
                    if not gemm and u in MOD_TAKE:
                        mod_take(MOD_TAKE[u])

            for u in range(NUNIT):
                take(0, u)
            base = step.n
            with dve.Fori(1, HEADS) as s:
                step.base, step.n = s * BODY_STEPS + (base - BODY_STEPS), 0
                dve_body(s, True, True)
                assert step.n == BODY_STEPS, step.n
            step.base, step.n = base + (HEADS - 1) * BODY_STEPS, 0
            dve_body(HEADS, False, True)

            for n in range(8):
                hf, j = n // 4, n % 4
                dve.wait_ge(ln_pe, hf + 1)
                if n == 0:
                    dve.wait_ge(conv_done, HEADS)
                c = cat[:, 4 + j, hf * BANK:(hf + 1) * BANK]
                if j == 3 or hf == 1:
                    dve.wait_ge(ln_pe, 2)
                dve.scalar_tensor_tensor(c, bank[hf][:], -1.0 / BANK, c, ALU.mult, ALU.add).then_inc(ln_dve, 1)

            def cat_part(j):
                for hf in range(2):
                    dve.wait_ge(cat_hi, 2 * j + hf + 1)
                    dve.tensor_tensor(catS[:, hf, 1, j, :], cat[:, j, hf * BANK:(hf + 1) * BANK],
                                      catS[:, hf, 0, j, :].bitcast(F32), ALU.subtract).then_inc(cat_lo, 1)

            dve.wait_ge(g_full, 1)
            for q in range(2):
                step(dve.tensor_copy(Gb[:, q * BANK:(q + 1) * BANK], bank[4 + q][:]))
            step.wait()
            dve.sem_inc(g_done, 1)
            for hf in range(2):
                dve.wait_ge(ln_act, 9 + hf)
                r = rstd[:, hf * BANK:(hf + 1) * BANK]
                dve.reciprocal(r, r).then_inc(ln_dve, 1)
            dve.wait_ge(ln_dve, 10)
            for j in range(4):
                dve.tensor_tensor(cat[:, 4 + j], cat[:, 4 + j], rstd[:], ALU.mult).then_inc(ln_dve, 1)
            for j in range(4):
                cat_part(j)
            for j in range(4):
                dve.wait_ge(ln_act, 11 + j)
                dve.wait_ge(ln_dve, 11 + j)
                step(dve.tensor_scalar(cat[:, 4 + j], cat[:, 4 + j], vec[:, R_LNG + j:R_LNG + j + 1],
                                       vec[:, R_LNB + j:R_LNB + j + 1], ALU.mult, ALU.add))
                step.wait()
                dve.tensor_tensor(cat[:, 4 + j], cat[:, 4 + j], lnsg[:, j % 2, :], ALU.mult).then_inc(ln_dve, 1)
            for j in range(4, 8):
                cat_part(j)

            def x1(t):
                dve.wait_ge(mix_root, t + 1)
                step(dve.reciprocal(rr[:, 1, t:t + 1], rr[:, 1, t:t + 1]))
                step.wait()
                for n in range(2):
                    sl = slice(n * BANK, (n + 1) * BANK)
                    step(dve.scalar_tensor_tensor(mixt[:, sl], bank[(2 * t + n) % 4][:], rr[:, 1, t:t + 1], Gb[:, sl],
                                                  ALU.mult, ALU.mult))
                step.wait()
                dve.wait_ge(x1_in[t % 3], 16 * (t // 3 + 1))
                dve.tensor_tensor(x1t[:, t % 3, :], x1t[:, t % 3, :], mixt[:], ALU.add).then_inc(mix_done, 1)
                dve.wait_ge(x1_root, t + 1)
                step(dve.reciprocal(rr[:, 0, t:t + 1], rr[:, 0, t:t + 1]))
                step.wait()
                dve.tensor_scalar(x2t[:].rearrange("p k n -> p (k n)"), x1t[:, t % 3, :], rr[:, 0, t:t + 1], None,
                                  ALU.mult).then_inc(x2_ready, 1)

            def h2(t):
                for k in range(KT):
                    if k % 4 == 0:
                        dve.wait_ge(h2_full, 2 * t + k // 4 + 1)
                    if k == 0 and t:
                        dve.wait_ge(h2_lo, t)
                    ins = dve.tensor_scalar(h2f[:, k, :], bank[6 + k // 4][:, (k % 4) * P:(k % 4 + 1) * P],
                                            gain2[:, k:k + 1], mod[:, 3, k, 0:1], ALU.mult, ALU.add)
                    if k % 4 == 3:
                        ins.then_inc(h2_free, 1)

            for t in range(XT + 1):
                if t < XT:
                    x1(t)
                if t >= 1:
                    h2(t - 1)
            dve.wait_ge(g_full, 2)
            for q in range(2):
                step(dve.tensor_copy(Gb[:, q * BANK:(q + 1) * BANK], bank[4 + q][:]))
            step.wait()
            dve.sem_inc(g_done, 1)

            def dve_tile(n, fi, par, base):
                for hf in range(2):
                    i = n * 4 + (2 * fi + hf + 1)
                    dve.wait_ge(gu_sig, i)
                    if not (first(n) and fi == 0):
                        dve.wait_ge(mid_lo, i - 2)
                    dve.tensor_tensor(mid32[:, hf, :], bank[2 * hf][:], sgm[:, hf, :], ALU.mult).then_inc(gu_part, 1)
                    dve.wait_ge(gu_part, i)
                    dve.wait_ge(gu_full, n * 8 + (4 * fi + 2 * hf + 2))
                    dve.tensor_tensor(mid32[:, hf, :], bank[2 * hf + 1][:], mid32[:, hf, :], ALU.mult).then_inc(gu_free, 1)
                for hf in range(2):
                    i = n * 4 + (2 * fi + hf + 1)
                    dve.wait_ge(gu_free, i)
                    dve.wait_ge(mid_hi, i)
                    sl = slice(hf * BANK, (hf + 1) * BANK)
                    dve.tensor_tensor(mid[:, par, fi, 1, sl], mid32[:, hf, :], mid[:, par, fi, 0, sl].bitcast(F32),
                                      ALU.subtract).then_inc(mid_lo, 1)

            def dve_down(n, t):
                for i in (2 * t, 2 * t + 1):
                    hf = i % 2
                    sl = slice(hf * BANK, (hf + 1) * BANK)
                    dve.wait_ge(down_full, n * 16 + (i + 1))
                    if first(n):
                        ins = dve.tensor_copy(y[:, t, sl], bank[4 + i % 4][:])
                    else:
                        dve.wait_ge(down_free, n * 16 + (i + 1 - 12))
                        ins = dve.tensor_tensor(y[:, t, sl], bank[4 + i % 4][:], y[:, t, sl], ALU.add)
                    ins.then_inc(down_free, 1)

            def dve_round(n, par):
                dve_tile(n, 0, par, None)
                dve_tile(n, 1, par, None)
                if not first(n):
                    for t in range(XT):
                        dve_down(n - 1, t)

            ffn_rounds(dve, dve_round)
            for t in range(XT + 1):
                if t < XT:
                    dve_down(NGROUP - 1, t)
                if t:
                    dve.wait_ge(y_root, t)
                    step(dve.reciprocal(rr[:, 1, t - 1:t], rr[:, 0, t - 1:t]))
                    step.wait()
                    dve.scalar_tensor_tensor(y[:, t - 1, :], y[:, t - 1, :], rr[:, 1, t - 1:t], Gb[:], ALU.mult,
                                             ALU.mult).then_inc(y_normed, 1)


MATRICES = ["x", "ctx", "w_mod", "w_in", "w_out", "ffn_w_gate", "ffn_w_up", "ffn_w_down", "conv_dw_w"]
VECTORS = ["c", "c_ctx", "b_mod", "pre_mix_g", "pre_ffn_g", "post_mix_g", "post_ffn_g", "hgrn_lb_fwd",
           "hgrn_lb_bwd", "conv_dw_b", "conv_ln_g", "conv_ln_b", "hgrn_onorm_g"]


def shape_constants():
    i = np.arange(P)
    xor = i[:, None] ^ i[None, :]
    masks = np.stack([(xor >= 1 << l) & (xor < 2 << l) for l in range(LEVELS)], 1).astype(np.float32)
    return {"ident": np.eye(P, dtype=np.float32), "masks": masks}


def lay_out(inputs):
    arrays = {f"in_{n}": np.ascontiguousarray(inputs[n]) for n in MATRICES}
    arrays["vectors"] = np.concatenate([np.reshape(inputs[n], (-1, P)) for n in VECTORS])
    arrays.update(shape_constants())
    return arrays


def kernel(**inputs):
    import concourse.bacc as bacc
    from concourse.bass_utils import run_bass_kernel_spmd

    nc = bacc.Bacc("TRN2", target_bir_lowering=False, num_devices=1)
    arrays = lay_out(inputs)
    args = [nc.dram_tensor(n, list(a.shape), mybir.dt.from_np(a.dtype), kind="ExternalInput").ap()
            for n, a in arrays.items()]
    args.append(nc.dram_tensor("out", [1, SEQ, DM], F32, kind="ExternalOutput").ap())
    kernel_program(nc, *args)
    return run_bass_kernel_spmd(nc, [arrays], core_ids=[0]).results[0]["out"]
```

```python
from contextlib import ExitStack

import numpy as np

import concourse.bass as bass
from concourse import mybir

F32 = mybir.dt.float32
F32R = mybir.dt.float32r
U8 = mybir.dt.uint8
ALU = mybir.AluOpType
ACT = mybir.ActivationFunctionType

P = 128
DM = 1024
KT = DM // P
SEQ = 1024
CTX = 256
TOK = CTX + SEQ
XT, CT = SEQ // P, CTX // P
NT = XT + CT
HEADS = 4
GRID = 64
ROWS = SEQ // GRID
TAPS = 31
PAD = TAPS // 2
DFF = 2816
FT = DFF // P
EPS = 1e-6
F_MIN = 1e-30
BANK = 512
LEVELS = 7

R_C, R_CC, R_BM, R_PREM, R_PREF, R_POSTM, R_POSTF, R_LBF, R_LBB, R_DWB, R_LNG, R_LNB, R_ON = (
    0, 8, 16, 64, 72, 80, 88, 96, 100, 104, 108, 112, 116)
NVEC = 117

TILES = [("ff", 512), ("fb", 1024), ("q", 0), ("g", 2048), ("b", 3072), ("a", 2560), ("v", 1536)]
NTILE = len(TILES)
UNITS = [(p, kind, n) for p, (kind, _) in enumerate(TILES)
         for n in range(3 if kind in ("ff", "fb", "v") else 2)]
UNITS.insert(-1, (NTILE - 1, "vt", 0))
UNITS += [(NTILE - 1, "vt", 1), (NTILE - 1, "vt", 2)]
NUNIT = len(UNITS)
GRING = 3
GEMM_BY = ["dve" if k in ("g", "a") else "act" for _, k, _ in UNITS]

SCAN = 3
USES = [("level", l, hf) for l in range(LEVELS + 1) for hf in range(2)]
_scan = [[("turn", g, d) for d in range(2)] for g in range(SCAN)], [[("outer", g, d) for d in range(2)] for g in range(SCAN)]
USES += _scan[0][0]
for _g in range(SCAN):
    USES += _scan[1][_g]
    if _g + 1 < SCAN:
        USES += _scan[0][_g + 1]
USES += [("o", 0, 0), ("o", 1, 0), ("ssq", 0, 0), ("rb", 0, 0), ("rb", 1, 0)]
NUSE = len(USES)
LRING, LBASE = 5, 3
USE_BY = ["act" if u[0] in ("turn", "ssq") or u[:2] == ("level", 0) else "dve" for u in USES]


def ordinal(by, i):
    return by[:i].count(by[i])


def ring_wait(by, ring, i):
    n = len(by)
    j = i - ring if i >= ring else max(k for k in range(n) if k % ring == i % ring)
    return by[j], ordinal(by, j), 0 if i >= ring else 1


LEVEL_AT = [0, 1, 2, 3, 4, 5, 6, 7]
TURN_AT, OUTER_AT = 8, 9
OUT_AT = 12
PE_STEPS = [[] for _ in UNITS]
for _i, _u in enumerate(USES):
    _at = {"level": LEVEL_AT[_u[1] % 8], "turn": TURN_AT + _u[1], "outer": OUTER_AT + _u[1], "o": OUT_AT,
           "ssq": OUT_AT + 1, "rb": OUT_AT + 2}[_u[0]]
    PE_STEPS[_at].append(_i)
TAPS_AFTER = [0, 0, 1, 1, 1, 1, 1, 1, 3, 3, 3, 3, 3, 3, 3, 3]
DVE_TAPS_AFTER = [0, 0, 1, 1, 1, 1, 1, 1, 1, 1, 1, 1, 1]
ACT_TAPS_AFTER = [2, 2, 2, 2, 2, 2, 2, 1, 1, 1, 1, 1]
assert sum(TAPS_AFTER) == sum(DVE_TAPS_AFTER) + sum(ACT_TAPS_AFTER) == TAPS - 1


def taps_after(after, u):
    return range(sum(after[:u]), sum(after[:u + 1]))

N_GACT, N_GDVE = GEMM_BY.count("act"), GEMM_BY.count("dve")
N_UACT, N_UDVE = USE_BY.count("act"), USE_BY.count("dve")
NK = LEVELS + 1
NSTATE = 2 * 3 * SCAN
BODY_STEPS = 42
NGROUP = FT // 2


def scan_chunk(d, n):
    if d == 0:
        return n
    return CT - 1 - n if n < CT else NT - 1 - (n - CT)


def last_unit(p):
    return max(u for u, (q, kind, _) in enumerate(UNITS) if q == p and kind != "vt")


def kernel_program(nc, x, ctx, w_mod, w_in, w_out, ffn_w_gate, ffn_w_up, ffn_w_down,
                   conv_dw_w, vectors, ident_in, masks_in, out):
    with ExitStack() as es:
        free = [(nc.sbuf_base + 31) // 32 * 32]
        spot = {}

        def sb(name, shape, dt=F32, offset=None):
            if offset is None:
                offset = free[0]
                free[0] += (int(np.prod(shape[1:])) * (1 if dt == U8 else 4) + 31) // 32 * 32
            spot[name] = offset
            return nc.alloc_sbuf_tensor_at(name, shape, dt, offset=offset)

        RAW = 3
        raw = sb("raw", [P, RAW, DM])
        split = sb("split", [P, 2, 2, DM], F32R)
        ring = sb("ring", [P, RAW, 2, DM], F32R, offset=spot["raw"])
        ring_in = sb("ring_in", [P, RAW, 2, DM], offset=spot["raw"])
        ident = sb("ident", [P, P])
        masks = sb("masks", [P, LEVELS, P], U8)
        vec = sb("vec", [P, NVEC])
        taps = sb("taps", [P, 4, TAPS])
        mod = sb("mod", [P, 6, KT, 2])
        gain = sb("gain", [P, KT, 2])
        gain2 = sb("gain2", [P, KT])
        gate = sb("gate", [P, 2, KT])
        silc = sb("silc", [P, KT, 2])
        silt = sb("silt", [P, 2, KT])
        lb = sb("lb", [P, 3, 8])
        lbt = sb("lbt", [P, 3, 8])
        ones = sb("ones", [P, P])
        eps = sb("eps", [P, 1])
        ss = sb("ss", [P, 2, NT])
        rr = sb("rr", [P, 2, NT])
        hss = sb("hss", [P, 2, XT])

        hT = sb("hT", [P, 2, KT, TOK], F32R)
        A0 = spot["hT"]
        cat = sb("cat", [P, 8, SEQ])
        W0 = free[0]
        F = sb("F", [P, 2, TOK])
        K = sb("K", [P, 2, TOK])
        Q = sb("Q", [P, 2, SEQ])
        qraw = sb("qraw", [P, SEQ])
        T = sb("T", [P, 2, TOK // 2])
        V = sb("V", [P, NT, P])
        AT = sb("AT", [P, SEQ])
        S = sb("S", [P, 2, XT, P])
        KC = sb("KC", [P, SEQ], offset=spot["S"])
        KTok = sb("KTok", [P, 2, 3, P])
        conv_sum = sb("conv_sum", [P, SEQ])
        assert free[0] <= nc.sbuf_usable_end, (free[0], nc.sbuf_usable_end)

        xst = sb("xst", [P, NT, DM], offset=W0)
        xfull = sb("xfull", [P, 2, KT, P], offset=W0 + 40960)
        vrow = sb("vrow", [P, P], offset=W0 + 49152)
        trow = sb("trow", [P, 4 * P], offset=W0 + 49152 + 512)
        junk = sb("junk", [P, DM], offset=W0 + 49152 + 2560)
        mask32 = sb("mask32", [P, LEVELS, P], offset=W0 + 49152 + 2560 + 4096)
        mraw = sb("mraw", [P, KT, DM], offset=spot["cat"])
        mrow = sb("mrow", [P, 2, DM], offset=A0 + 32768)
        mraw2 = sb("mraw2", [P, KT, DM], offset=A0)
        vT = sb("vT", [P, 2, BANK], offset=spot["raw"] + RAW * 2 * DM * 4)
        part7 = sb("part7", [P, SEQ], offset=A0 + 40960)
        tap7 = sb("tap7", [P, 2, SEQ], offset=A0 + 45056)
        XT0 = A0 + 65536
        catS = sb("catS", [P, 2, 2, KT, BANK], F32R, offset=A0)
        Gb = sb("Gb", [P, DM], offset=XT0)
        x1t = sb("x1t", [P, 3, DM], offset=XT0 + 4096)
        rstd = sb("rstd", [P, SEQ], offset=XT0 + 4096)
        lnsg = sb("lnsg", [P, 4, BANK], offset=XT0 + 8192)
        woA = sb("woA", [P, 6, 2, DM], F32R, offset=W0)
        mixt = sb("mixt", [P, DM], offset=W0 + 49152)
        vtmp = sb("vtmp", [P, 2, BANK], offset=W0 + 49152)
        x2t = sb("x2t", [P, KT, P], offset=W0 + 53248)
        h2f = sb("h2f", [P, KT, P], offset=W0 + 57344)
        h2T = [sb("h2Ta", [P, 2, KT, BANK], F32R, offset=spot["cat"]),
               sb("h2Tb", [P, 2, KT, BANK], F32R, offset=A0)]
        y = sb("y", [P, XT, DM], offset=A0 + 32768)
        sgm = sb("sgm", [P, 2, BANK], offset=XT0 + 4096)
        slotX = sb("slotX", [P, 2, DM], F32R, offset=XT0 + 8192)
        mid = sb("mid", [P, 2, 2, 2, SEQ], F32R, offset=W0)
        more = sb("more", [P, 3, 2, DM], F32R, offset=W0 + 32768)
        mid32 = sb("mid32", [P, 2, BANK], offset=W0 + 57344)
        xres = sb("xres", [P, XT, DM], offset=spot["cat"])
        junk2 = sb("junk2", [P, DM], offset=A0)

        def wo_part(q, k):
            return split[:, k, q] if k < 2 else woA[:, k - 2, q]

        WO_AT = [2, 3, OUT_AT]

        def last(n):
            return isinstance(n, int) and n == NGROUP - 1

        def down_slot(n, j):
            return j if last(n) else 4 + j

        def ffn_part(q, j):
            return split[:, j, q] if j < 2 else (more[:, j - 2, q] if j < 5 else slotX[:, q])

        bank = [es.enter_context(nc.psum_tensor(f"bank{i}", [P, BANK], F32)) for i in range(8)]
        x1_dram = nc.dram_tensor("x1_scratch", [SEQ, DM], F32, kind="Internal").ap()

        def sem(name):
            return es.enter_context(nc.semaphore(name))

        small_in = sem("small_in")
        x_in = [sem(f"x_in{i}") for i in range(NT)]
        mod_in = [sem(f"mod_in{i}") for i in range(8)]
        raw_in = [sem(f"raw_in{i}") for i in range(RAW)]
        x1_in = [sem(f"x1_in{i}") for i in range(3)]
        x1_store = [sem(f"x1_store{i}") for i in range(3)]
        res_in = [sem(f"res_in{i}") for i in range(XT)]
        out_done = [sem(f"out_done{i}") for i in range(XT)]
        pe_cols, cols_done, sil_sig, lb_exp = sem("pe_cols"), sem("cols_done"), sem("sil_sig"), sem("lb_exp")
        mod_full, mod_row, mod_turned, mod_done = (sem("mod_full"), sem("mod_row"), sem("mod_turned"),
                                                   sem("mod_done"))
        x_root, xn_ready, xp_full, xp_free = sem("x_root"), sem("xn_ready"), sem("xp_full"), sem("xp_free")
        h_hi, h_lo = sem("h_hi"), sem("h_lo")
        w_hi, w_lo = sem("w_hi"), sem("w_lo")
        gemm_full, gemm_act, gemm_dve, g_sig = sem("gemm_full"), sem("gemm_act"), sem("gemm_dve"), sem("g_sig")
        use_full, use_act, use_dve = sem("use_full"), sem("use_act"), sem("use_dve")
        k_ready, kc_ready, q_ready = sem("k_ready"), sem("kc_ready"), sem("q_ready")
        state_done, sq_ready, rs_ready, conv_done = sem("state_done"), sem("sq_ready"), sem("rs_ready"), sem("conv_done")
        conv_pool, tap_ready = sem("conv_pool"), sem("tap_ready")
        ln_sum, ln_centred, ln_square, ln_var = sem("ln_sum"), sem("ln_centred"), sem("ln_square"), sem("ln_var")
        ln_root, ln_rstd, ln_normed, ln_sig, ln_out = (sem("ln_root"), sem("ln_rstd"), sem("ln_normed"),
                                                       sem("ln_sig"), sem("ln_out"))
        cat_hi, cat_lo, o_hi, o_lo = sem("cat_hi"), sem("cat_lo"), sem("o_hi"), sem("o_lo")
        g_full, g_done = sem("g_full"), sem("g_done")
        mix_full, mix_root, mix_done, x1_root = sem("mix_full"), sem("mix_root"), sem("mix_done"), sem("x1_root")
        x2_ready, h2_full, h2_free, h2_hi, h2_lo = (sem("x2_ready"), sem("h2_full"), sem("h2_free"),
                                                    sem("h2_hi"), sem("h2_lo"))
        f_hi, f_lo, split_free = sem("f_hi"), sem("f_lo"), sem("split_free")
        gu_full, gu_sig, gu_free, mid_hi, mid_lo = (sem("gu_full"), sem("gu_sig"), sem("gu_free"),
                                                    sem("mid_hi"), sem("mid_lo"))
        down_full, down_free, gu_part = sem("down_full"), sem("down_free"), sem("gu_part")
        y_root, y_normed, y_done = sem("y_root"), sem("y_normed"), sem("y_done")
        dve_step, act_step = sem("dve_step"), sem("act_step")

        class Steps:

            def __init__(self, eng, s):
                self.eng, self.s, self.base, self.n = eng, s, 0, 0

            def __call__(self, ins):
                self.n += 1
                ins.then_inc(self.s, 1)
                return self.n

            def wait(self, n=None):
                self.eng.wait_ge(self.s, self.base + (self.n if n is None else n))

        def view(t, offset, dims):
            a = t[:]
            return bass.AP(a.tensor, a.offset + offset, [list(a.ap[0])] + [list(d) for d in dims])

        def first(s):
            return isinstance(s, int) and s == 0

        def cat_tile(i):
            return cat[:, bass.ds(i, 1), :].rearrange("p o n -> p (o n)")

        def tap_views(out, h, n):
            k = n + (n >= PAD)
            t0, t1 = max(0, PAD - k), GRID - max(0, k - PAD)
            out = out.rearrange("p (r c) -> p r c", c=GRID)[:, :, t0:t1]
            src = cat_tile(h + 4).rearrange("p (r c) -> p r c", c=GRID)[:, :, t0 + k - PAD:t1 + k - PAD]
            return out, src, tap_weight(h, k)

        def tap_weight(h, k):
            return (taps[:, h, k:k + 1] if isinstance(h, int) else
                    taps[:, bass.ds(h, 1), k:k + 1].rearrange("p o n -> p (o n)"))

        xf = x.rearrange("b (t p) d -> (b t) p d", p=P)
        cf = ctx.rearrange("b (t p) d -> (b t) p d", p=P)
        outf = out.rearrange("b (t p) d -> (b t) p d", p=P)
        wm = w_mod.rearrange("l (k p) (m n) -> (l m) k p n", p=P, m=6)
        win = w_in.rearrange("l (k p) n -> (l p) k n", p=P)
        wo = w_out.rearrange("l (k p) n -> (l k) p n", p=P)
        wg = ffn_w_gate.rearrange("l (k p) n -> (l p) k n", p=P)
        wu = ffn_w_up.rearrange("l (k p) n -> (l p) k n", p=P)
        wd = ffn_w_down.rearrange("l (k p) n -> (l k) p n", p=P)

        MODS = [1, 0, 2, 3, 4, 5]
        MOD_STEPS = [(2, k) for k in range(KT)]
        for _n in range(3, 6):
            MOD_STEPS += [(_n, 0), (_n, 1), (_n - 1, KT)] + [(_n, k) for k in range(2, KT)]
        MOD_STEPS += [(5, KT)]
        MOD_LAG = 2

        def mod_steps_after(i):
            if i == NUSE - 1:
                return MOD_STEPS[max(0, i - MOD_LAG):]
            return MOD_STEPS[i - MOD_LAG:i - MOD_LAG + 1] if i >= MOD_LAG else []

        SLOT = [0, 1, 2, 0, 1, 2, 1]
        SLOT_TILES = [[p for p in range(NTILE) if SLOT[p] == r] for r in range(RAW)]

        def head_fill(s, p):
            mine = SLOT_TILES[SLOT[p]]
            return s * len(mine) + (mine.index(p) + 1)

        def late_fill(i):
            return HEADS * len(SLOT_TILES[i % RAW]) + i // RAW + 1

        def ffn_rounds(eng, body):
            body(0, 0)
            body(1, 1)
            with eng.Fori(0, (NGROUP - 3) // 2) as r:
                body(r * 2 + 2, 0)
                body(r * 2 + 3, 1)
            body(NGROUP - 1, (NGROUP - 1) % 2)

        def gu_no(n, j):
            return j if first(n) else n * 6 + (j - 2)

        def down_no(n, j):
            if last(n):
                return 6 * NGROUP - 2 + j
            return n * 6 + (8 + j)

        block = es.enter_context(nc.Block())

        @block.sync
        def _(sp):
            sp.dma_start(vrow[0:NVEC, :], vectors).then_inc(small_in, 16)
            sp.dma_start(trow[0:TAPS, :], conv_dw_w.rearrange("l t n -> (l t) n")).then_inc(small_in, 16)
            sp.dma_start(ident[:], ident_in).then_inc(small_in, 16)
            sp.dma_start(mask32[:], masks_in).then_inc(small_in, 16)

            def load_x(t):
                sp.dma_start(xst[:, t, :], cf[t] if t < CT else xf[t - CT]).then_inc(x_in[t], 16)

            def load_mod(n):
                for k in range(KT):
                    if n == 2 and k == 0:
                        sp.wait_ge(gemm_full, HEADS * NUNIT)
                    if n and n != 2:
                        sp.wait_ge(mod_full, (n - 1) * KT + k + 1)
                    sp.dma_start((mraw if n < 2 else mraw2)[:, k, :], wm[MODS[n], k]).then_inc(mod_in[k], 16)

            def load_tile(s, p):
                col = (s - 1) * P + (P + TILES[p][1])
                mine = SLOT_TILES[SLOT[p]]
                k = mine.index(p)
                if k:
                    sp.wait_ge(gemm_full, s * NUNIT + (last_unit(mine[k - 1]) + 1))
                elif not first(s):
                    sp.wait_ge(gemm_full, s * NUNIT + (last_unit(mine[-1]) + 1 - NUNIT))
                sp.dma_start(ring_in[:, SLOT[p], 1, :].rearrange("p (k n) -> p k n", k=KT),
                             win[:, :, bass.ds(col, P)]).then_inc(raw_in[SLOT[p]], 16)

            load_mod(0)
            for t in range(2):
                load_x(t)
                load_tile(0, t)
            load_mod(1)
            for t in range(2, NT):
                load_x(t)
            for p in range(2, NTILE):
                load_tile(0, p)
            with sp.Fori(1, HEADS) as s:
                for p in range(NTILE):
                    load_tile(s, p)

            for i in range(KT):
                if i == RAW:
                    for n in range(2, 6):
                        load_mod(n)
                if i < RAW:
                    sp.wait_ge(gemm_full, HEADS * NUNIT)
                else:
                    sp.wait_ge(o_lo, i - RAW + 1)
                sp.dma_start(raw[:, i % RAW, :], wo[i]).then_inc(raw_in[i % RAW], 16)

            def load_ffn(n, no, r, kind):
                row = n * 2 + int(kind[1])
                at = row if kind[0] == "d" else row * P
                at = at if isinstance(at, int) else sp.snap(at)
                if isinstance(no, int) and no < RAW:
                    sp.wait_ge(o_lo, KT + no - RAW + 1)
                else:
                    sp.wait_ge(f_lo, no - (RAW - 1))
                if kind[0] == "d":
                    sp.dma_start(raw[:, r, :].rearrange("p (o n) -> p o n", o=1),
                                 wd[bass.ds(at, 1)].rearrange("o p n -> p o n")).then_inc(raw_in[r], 16)
                else:
                    w = wg if kind[0] == "g" else wu
                    sp.dma_start(raw[:, r, :].rearrange("p (k n) -> p k n", k=KT),
                                 w[:, :, bass.ds(at, P)]).then_inc(raw_in[r], 16)

            GU = ["g0", "u0", "g1", "u1"]
            for j in range(RAW):
                load_ffn(0, j, (KT + j) % RAW, GU[j])

            for t in range(XT + 2):
                if t < XT:
                    if t == 0:
                        sp.wait_ge(cat_lo, 2 * KT)
                    if t >= 3:
                        sp.wait_ge(x1_store[t % 3], 16 * (t // 3))
                        sp.wait_ge(x2_ready, t - 2)
                    sp.dma_start(x1t[:, t % 3, :], xf[t]).then_inc(x1_in[t % 3], 16)
                if t >= 2:
                    sp.wait_ge(mix_done, t - 1)
                    sp.dma_start(x1_dram[(t - 2) * P:(t - 1) * P, :],
                                 x1t[:, (t - 2) % 3, :]).then_inc(x1_store[(t - 2) % 3], 16)

            load_ffn(0, RAW, (KT + RAW) % RAW, GU[RAW])

            def round_loads(n, par):
                if not first(n):
                    for j in range(2):
                        load_ffn(n - 1, down_no(n - 1, j), (KT + 2 + j) % RAW, f"d{j}")
                if not last(n):
                    for j in range(4):
                        load_ffn(n + 1, gu_no(n + 1, j), (KT + 4 + j) % RAW, GU[j])

            ffn_rounds(sp, round_loads)
            for j in range(2):
                no = down_no(NGROUP - 1, j)
                load_ffn(NGROUP - 1, no, (KT + no) % RAW, f"d{j}")

            for t in range(3):
                sp.wait_ge(x1_store[t], 16 * len(range(t, XT, 3)))
            sp.wait_ge(gu_full, 8 * NGROUP)
            for t in range(XT):
                sp.dma_start(xres[:, t, :], x1_dram[t * P:(t + 1) * P, :]).then_inc(res_in[t], 16)
            for t in range(XT):
                sp.wait_ge(y_done, t + 1)
                sp.dma_start(outf[t], xres[:, t, :]).then_inc(out_done[t], 16)
            for t in range(XT):
                sp.wait_ge(out_done[t], 16)

        @block.tensor
        def _(pe):
            def mm(o, l, r, start, stop):
                return pe.matmul(o, l, r, start=start, stop=stop, skip_group_check=True)

            def product(o, a, b, start, stop):
                mm(o, a[0], b[0], start, False)
                mm(o, a[0], b[1], False, False)
                return mm(o, a[1], b[0], False, stop)

            pe.wait_ge(small_in, 16 * 4)
            pe.transpose(bank[0][:, 0:NVEC], vrow[0:NVEC, :], ident[0:NVEC, 0:NVEC]).then_inc(pe_cols, 1)
            for j in range(4):
                ins = pe.transpose(bank[1][:, j * TAPS:(j + 1) * TAPS], trow[0:TAPS, j * P:(j + 1) * P],
                                   ident[0:TAPS, 0:TAPS])
            ins.then_inc(pe_cols, 1)

            def mod_step(n, k):
                b0, bt = (LBASE + 2 * n, 7) if n < 2 else (0, 2)
                if k < KT:
                    if k == 0 and n > 2:
                        pe.wait_ge(mod_row, n)
                    pe.wait_ge(mod_in[k], 16 * (n + 1))
                    for q in range(2):
                        ins = mm(bank[b0 + q][0:2, :], silc[:, k, :], (mraw if n < 2 else mraw2)[:, k, q * BANK:(q + 1) * BANK],
                                 k == 0, k == KT - 1)
                    ins.then_inc(mod_full, 1)
                else:
                    pe.wait_ge(mod_row, n + 1)
                    if n:
                        pe.wait_ge(mod_done, n)
                    for j in range(KT):
                        c0 = (n % 4) * 2 * KT + 2 * j
                        ins = pe.transpose(bank[bt][:, c0:c0 + 2], mrow[0:2, n % 2, j * P:(j + 1) * P], ident[0:2, 0:2])
                    ins.then_inc(mod_turned, 1)

            pe.wait_ge(cols_done, 2)
            for n in range(2):
                for k in range(KT + 1):
                    mod_step(n, k)

            def turn_x(t):
                pe.wait_ge(xn_ready, t + 1)
                for half in range(2):
                    n = 2 * t + half
                    if n >= 4:
                        pe.wait_ge(xp_free, n - 3)
                    for k in range(4):
                        kk = half * 4 + k
                        ins = pe.transpose(bank[LBASE + n % 4][:, k * P:(k + 1) * P], xst[:, t, kk * P:(kk + 1) * P],
                                           ident[:])
                    ins.then_inc(xp_full, 1)

            def wait_bank(by, ring, i, s, act_sem, dve_sem):
                who, k, ago = ring_wait(by, ring, i)
                n = by.count(who)
                pe.wait_ge(act_sem if who == "act" else dve_sem, s * n + ((1 - ago) * n + k + 1))

            def project(s, u):
                p, kind, n = UNITS[u]
                b = bank[u % GRING]
                if n == 0 and kind != "vt":
                    pe.wait_ge(w_lo, s * NTILE + (p + 1))
                wait_bank(GEMM_BY, GRING, u, s, gemm_act, gemm_dve)

                def w(k):
                    return [ring[:, SLOT[p], q, k * P:(k + 1) * P] for q in range(2)]

                if kind == "vt":
                    v = UNITS.index((p, "v", n))
                    pe.wait_ge(gemm_act, s * N_GACT + (N_GACT + ordinal(GEMM_BY, v) + 1))
                    for t in range(min(4, NT - 4 * n)):
                        ins = pe.transpose(b[:, t * P:(t + 1) * P], vT[:, n % 2, t * P:(t + 1) * P], ident[:])
                else:
                    t0 = n * BANK if kind in ("ff", "fb", "v") else CTX + n * BANK
                    wd_ = min(BANK, TOK - t0)
                    for k in range(KT):
                        ins = product(b[:, 0:wd_], w(k), [hT[:, q, k, t0:t0 + wd_] for q in range(2)],
                                      k == 0, k == KT - 1)
                ins.then_inc(gemm_full, 1)

            def use(h, i):
                kind, a1, a2 = USES[i]
                b = bank[LBASE + i % LRING]
                wait_bank(USE_BY, LRING, i, h, use_act, use_dve)
                if kind == "level":
                    l, hf = a1, a2
                    if hf == 0 and l == 0:
                        pe.wait_ge(k_ready, h * NK + 1)
                    elif hf == 0:
                        pe.wait_ge(kc_ready, h * LEVELS + l)
                        pe.wait_ge(q_ready, h * NK + l)
                    for cc in range(4):
                        ch = hf * 4 + cc
                        o = b[:, cc * P:(cc + 1) * P]
                        if l == 0:
                            tk = CTX + ch * P
                            mm(o, K[:, 0, tk:tk + P], qraw[:, ch * P:(ch + 1) * P], True, False)
                            ins = mm(o, K[:, 1, tk:tk + P], qraw[:, ch * P:(ch + 1) * P], False, True)
                        else:
                            bs = 1 << (l - 1)
                            q = view(Q, ch * P, [(2 * bs, P // (2 * bs)), (SEQ + bs, 2), (1, bs)])
                            ins = mm(o, KC[:, ch * P:(ch + 1) * P], q, True, True)
                elif kind == "turn":
                    if a1 == 0 and a2 == 0:
                        pe.wait_ge(k_ready, h * NK + NK)
                    for j in range(3):
                        ch = scan_chunk(a2, 3 * a1 + j)
                        ins = pe.transpose(b[:, j * P:(j + 1) * P], K[:, a2, ch * P:(ch + 1) * P], ident[:])
                elif kind == "outer":
                    if a2 == 0:
                        if a1 == 0:
                            pe.wait_ge(gemm_act, h * N_GACT + 2 * N_GACT)
                        pe.wait_ge(use_act, h * N_UACT + (N_UACT + 2 + 2 * a1 + 2))
                    for j in range(3):
                        ch = scan_chunk(a2, 3 * a1 + j)
                        ins = mm(b[:, j * P:(j + 1) * P], KTok[:, a2, j, :], V[:, ch, :], True, True)
                elif kind == "o":
                    if a1 == 0:
                        pe.wait_ge(state_done, h * NSTATE + NSTATE)
                        pe.wait_ge(q_ready, h * NK + NK)
                        pe.wait_ge(use_dve, h * N_UDVE + (N_UDVE + 2 * LEVELS))
                    for cc in range(4):
                        ch = a1 * 4 + cc
                        o = b[:, cc * P:(cc + 1) * P]
                        sl = slice(ch * P, (ch + 1) * P)
                        mm(o, V[:, CT + ch, :], AT[:, sl], True, False)
                        mm(o, S[:, 0, ch, :], Q[:, 1, sl], False, False)
                        ins = mm(o, S[:, 1, XT - 1 - ch, :], Q[:, 0, sl], False, True)
                elif kind == "ssq":
                    pe.wait_ge(sq_ready, h * 2 + 2)
                    for ch in range(XT):
                        ins = mm(b[:, ch:ch + 1], AT[:, ch * P:(ch + 1) * P], ones[:, 0:1], True, True)
                else:
                    if a1 == 0:
                        pe.wait_ge(rs_ready, h + 1)
                    for cc in range(4):
                        ins = mm(b[:, cc * P:(cc + 1) * P], view(hss, XT + a1 * 4 + cc, [(0, P)]), ident[:],
                                 True, True)
                ins.then_inc(use_full, 1)

            for t in range(7):
                turn_x(t)
            pe.wait_ge(h_lo, 4)
            project(0, 0)
            for t in range(7, NT):
                turn_x(t)
            for u in range(1, NUNIT):
                if u <= 2:
                    pe.wait_ge(h_lo, min(4 * u + 4, NT))
                project(0, u)
            pe.wait_ge(xp_free, 2 * NT)
            pe.wait_ge(mod_done, 2)
            with pe.Fori(1, HEADS) as s:
                for u in range(NUNIT):
                    project(s, u)
                    for i in PE_STEPS[u]:
                        use(s - 1, i)
            pe.wait_ge(gemm_act, (HEADS + 1) * N_GACT)
            pe.wait_ge(gemm_dve, (HEADS + 1) * N_GDVE)
            for i in range(NUSE):
                use(HEADS - 1, i)
                for n, k in mod_steps_after(i):
                    mod_step(n, k)

            pe.wait_ge(conv_done, 1)
            pe.wait_ge(use_dve, (HEADS + 1) * N_UDVE)
            pe.wait_ge(use_act, (HEADS + 1) * N_UACT)
            for hf in range(2):
                for j in range(4):
                    ins = mm(bank[4 + hf][:], ones[:], cat[:, 4 + j, hf * BANK:(hf + 1) * BANK], j == 0, j == 3)
                ins.then_inc(ln_sum, 1)

            def variance(hf):
                for j in range(4):
                    pe.wait_ge(ln_square, hf * 4 + j + 1)
                    mm(bank[6 + hf][:], ones[:], vtmp[:, j % 2, :], j == 0, j == 3).then_inc(ln_var, 1)

            def gate_rows(i):
                for j in range(KT):
                    ins = mm(bank[4 + j // 4][:, (j % 4) * P:(j % 4 + 1) * P], view(gate, i * KT + j, [(0, P)]),
                             ident[:], True, True)
                ins.then_inc(g_full, 1)

            def mix_step(t, n, k):
                hf, tt = t // 4, t % 4
                return product(bank[(2 * t + n) % 4][:], [catS[:, hf, q, k, tt * P:(tt + 1) * P] for q in range(2)],
                               [wo_part(q, k)[:, n * BANK:(n + 1) * BANK] for q in range(2)], k == 0, k == KT - 1)

            pe.wait_ge(mod_done, 6)
            for k in range(KT):
                pe.wait_ge(cat_lo, k + 1)
                pe.wait_ge(o_lo, k + 1)
                for i in range(4):
                    ins = mix_step(i // 2, i % 2, k)
                    if k == KT - 1:
                        ins.then_inc(mix_full, 1)
                if k < 2:
                    variance(k)
                elif k == 3:
                    pe.wait_ge(ln_centred, 8)
                    gate_rows(0)

            def mix(t, n):
                for k in range(KT):
                    ins = mix_step(t, n, k)
                    if t == XT - 1 and n == 1 and k == 1:
                        ins.then_inc(split_free, 1)
                ins.then_inc(mix_full, 1)

            def turn2(t):
                pe.wait_ge(x2_ready, t + 1)
                for half in range(2):
                    if t >= 1:
                        pe.wait_ge(h2_free, 2 * t - 1 + half)
                    for k in range(4):
                        ins = pe.transpose(bank[6 + half][:, k * P:(k + 1) * P], x2t[:, half * 4 + k, :], ident[:])
                    ins.then_inc(h2_full, 1)

            for t in range(2, XT):
                pe.wait_ge(mix_done, t - 1)
                pe.wait_ge(cat_lo, 2 * KT if t >= 4 else KT)
                mix(t, 0)
                turn2(t - 2)
                mix(t, 1)
            turn2(XT - 2)

            def gate_up(n, fi, halves=(0, 1)):
                pe.wait_ge(f_lo, gu_no(n, 2 * fi + 1) + 1)
                for hf in halves:
                    if first(n) and fi == 0:
                        pe.wait_ge(mix_done, XT - 1 + hf)
                        pe.wait_ge(h2_lo, 4 * hf + 4)
                    else:
                        pe.wait_ge(gu_free, n * 4 + (2 * fi + hf - 1))
                    for j in range(2):
                        b = bank[2 * hf + j]
                        for k in range(KT):
                            ins = product(b[:], [ffn_part(q, 2 * fi + j)[:, k * P:(k + 1) * P] for q in range(2)],
                                          [h2T[hf][:, q, k, :] for q in range(2)], k == 0, k == KT - 1)
                        ins.then_inc(gu_full, 1)

            def down(n, par):
                pe.wait_ge(f_lo, down_no(n, 1) + 1)
                pe.wait_ge(mid_lo, n * 4 + 4)
                for i in range(2 * XT):
                    t, hf = i // 2, i % 2
                    pe.wait_ge(down_free, n * 16 + (i + 1))
                    for fi in range(2):
                        ins = product(bank[4 + i % 4][:], [mid[:, par, fi, q, t * P:(t + 1) * P] for q in range(2)],
                                      [ffn_part(q, down_slot(n, fi))[:, hf * BANK:(hf + 1) * BANK] for q in range(2)],
                                      fi == 0, fi == 1)
                    ins.then_inc(down_full, 1)

            def pe_round(n, par):
                gate_up(n, 0, (1,) if first(n) else (0, 1))
                gate_up(n, 1)
                if first(n):
                    pe.wait_ge(g_done, 2)
                    pe.wait_ge(h2_free, 2 * XT)
                else:
                    down(n - 1, 1 - par)

            gate_up(0, 0, (0,))
            turn2(XT - 1)
            pe.wait_ge(g_done, 1)
            gate_rows(1)
            ffn_rounds(pe, pe_round)
            down(NGROUP - 1, (NGROUP - 1) % 2)

        @block.scalar
        def _(act):
            step = Steps(act, act_step)

            act.wait_ge(pe_cols, 1)
            act.activation(silt[:], bank[0][:, 0:2 * KT].rearrange("p (a k) -> p a k", a=2),
                           ACT.Sigmoid).then_inc(sil_sig, 1)
            act.wait_ge(cols_done, 1)
            act.activation(lbt[:, 1, :], lbt[:, 0, :], ACT.Exp).then_inc(lb_exp, 1)

            act.wait_ge(cols_done, 2)

            def x_rms(t):
                act.wait_ge(x_in[t], 16)
                if step.n:
                    step.wait()
                step(act.activation(junk[:], xst[:, t, :], ACT.Square, accum_out=ss[:, 0, t:t + 1]))
                step.wait()
                act.activation(ss[:, 1, t:t + 1], ss[:, 0, t:t + 1], ACT.Sqrt, bias=eps[:], scale=1.0 / DM).then_inc(x_root, 1)

            def mod_rows(n):
                b0 = LBASE + 2 * n if n < 2 else 0
                act.wait_ge(mod_full, KT * (n + 1))
                if n >= 2:
                    act.wait_ge(mod_turned, n - 1)
                for q in range(2):
                    ins = act.activation(mrow[0:2, n % 2, q * BANK:(q + 1) * BANK], bank[b0 + q][0:2, :], ACT.Copy)
                ins.then_inc(mod_row, 1)

            act.sem_inc(gemm_act, N_GACT)
            act.sem_inc(use_act, N_UACT)

            def head_hi(s, p):
                act.wait_ge(raw_in[SLOT[p]], head_fill(s, p) * 16)
                act.activation(ring[:, SLOT[p], 0], ring_in[:, SLOT[p], 1], ACT.Copy).then_inc(w_hi, 1)

            mod_rows(0)
            for t in range(2):
                x_rms(t)
                head_hi(0, t)
            mod_rows(1)
            for t in range(NT):
                if t + 2 < NT:
                    x_rms(t + 2)
                act.wait_ge(xp_free, 2 * t + 2)
                act.activation(hT[:, 0, :, t * P:(t + 1) * P], xfull[:, t % 2], ACT.Copy).then_inc(h_hi, 1)

            def evac(s, u):
                p, kind, n = UNITS[u]
                if kind == "a":
                    return
                act.wait_ge(gemm_full, s * NUNIT + (u + 1))
                b = bank[u % GRING]
                sl = slice(n * BANK, (n + 1) * BANK)
                if kind in ("ff", "fb"):
                    w = min(BANK, TOK - n * BANK)
                    if u == 0 and not first(s):
                        act.wait_ge(q_ready, s * NK + (2 - NK))
                    act.activation(F[:, 0 if kind == "ff" else 1, n * BANK:n * BANK + w], b[:, 0:w],
                                   ACT.Sigmoid).then_inc(gemm_act, 1)
                elif kind == "q":
                    act.activation(qraw[:, sl], b[:], ACT.Copy, scale=float(P) ** -0.5).then_inc(gemm_act, 1)
                elif kind == "g":
                    act.activation(cat_tile(s)[:, sl], b[:], ACT.Sigmoid).then_inc(g_sig, 1)
                elif kind == "b":
                    act.activation(cat_tile(s + 4)[:, sl], b[:], ACT.Sigmoid).then_inc(gemm_act, 1)
                elif kind == "v":
                    w = min(BANK, TOK - n * BANK)
                    act.activation(vT[:, n % 2, 0:w], b[:, 0:w], ACT.Copy).then_inc(gemm_act, 1)
                else:
                    w = min(4, NT - 4 * n)
                    if n == 0 and not first(s):
                        act.wait_ge(use_full, s * NUSE + (USES.index(("o", 1, 0)) + 1 - NUSE))
                    act.activation(V[:, 4 * n:4 * n + w, :], b[:, 0:w * P].rearrange("p (t v) -> p t v", v=P),
                                   ACT.Copy).then_inc(gemm_act, 1)

            def level_keys(h, l):
                bs = 1 << (l - 1)
                act.wait_ge(k_ready, h * NK + l)
                if l > 1:
                    act.wait_ge(use_full, h * NUSE + 2 * l)
                act.activation(view(KC, 0, [(2 * bs, SEQ // (2 * bs)), (bs, 2), (1, bs)]),
                               view(K, CTX, [(2 * bs, SEQ // (2 * bs)), (TOK + bs, 2), (1, bs)]),
                               ACT.Copy).then_inc(kc_ready, 1)

            def act_use(h, i):
                kind, a1, a2 = USES[i]
                b = bank[LBASE + i % LRING]
                if kind == "level" and a1 == 0:
                    act.wait_ge(use_full, h * NUSE + (i + 1))
                    act.activation(AT[:, a2 * BANK:(a2 + 1) * BANK], b[:], ACT.Copy).then_inc(use_act, 1)
                elif kind == "turn":
                    act.wait_ge(use_full, h * NUSE + (i + 1))
                    if a1 > 0:
                        act.wait_ge(use_full, h * NUSE + (USES.index(("outer", a1 - 1, a2)) + 1))
                    act.activation(KTok[:, a2], b[:, 0:3 * P].rearrange("p (j n) -> p j n", n=P),
                                   ACT.Copy).then_inc(use_act, 1)
                elif kind == "o":
                    act.wait_ge(use_full, h * NUSE + (USES.index(("o", 1, 0)) + 1))
                    act.activation(AT[:, a1 * BANK:(a1 + 1) * BANK], b[:], ACT.Square).then_inc(sq_ready, 1)
                elif kind == "ssq":
                    act.wait_ge(use_full, h * NUSE + (i + 1))
                    act.activation(hss[:, 0, :], b[:, 0:XT], ACT.Sqrt, bias=eps[:], scale=1.0 / P).then_inc(use_act, 1)

            def tap_product(n):
                if n == 0:
                    act.wait_ge(gemm_full, HEADS * NUNIT)
                    act.wait_ge(gemm_dve, (HEADS + 1) * N_GDVE)
                else:
                    act.wait_ge(conv_pool, n)
                out, src, w = tap_views(tap7[:, n % 2], HEADS - 1, n)
                act.activation(out, src, ACT.Copy, scale=w).then_inc(tap_ready, 1)

            def wo_hi(i):
                act.wait_ge(raw_in[i % RAW], 16 * late_fill(i))
                act.activation(wo_part(0, i), raw[:, i % RAW, :], ACT.Copy).then_inc(o_hi, 1)

            def act_body(s, gemm, rec, more):
                for u in range(NUNIT):
                    if gemm:
                        p, _, n = UNITS[u]
                        if u:
                            evac(s, u)
                        if u == 1 and not first(s):
                            head_hi(s, 1)
                        if u == last_unit(NTILE - 2) + 2 and more:
                            head_hi(s + 1, 0)
                        if n == 0 and 1 <= p < NTILE - 1 and p != NTILE - 2:
                            head_hi(s, p + 1)
                        if u == last_unit(NTILE - 2):
                            head_hi(s, NTILE - 1)
                    if rec:
                        for i in PE_STEPS[u]:
                            act_use(s - 1, i)
                            if not gemm:
                                for n, k in mod_steps_after(i):
                                    if k == KT - 1:
                                        mod_rows(n)
                        if u in LEVEL_AT[:-1]:
                            level_keys(s - 1, LEVEL_AT.index(u) + 1)
                        if not gemm:
                            for n in taps_after(ACT_TAPS_AFTER, u):
                                tap_product(n)
                            if u in WO_AT:
                                wo_hi(WO_AT.index(u))
                    if gemm and u == 0:
                        evac(s, u)

            act_body(0, True, False, True)
            with act.Fori(1, HEADS - 1) as s:
                act_body(s, True, True, True)
            act_body(HEADS - 1, True, True, False)
            act_body(HEADS, False, True, False)

            def cat_parts(j, hf):
                act.activation(catS[:, hf, 0, j, :], cat[:, j, hf * BANK:(hf + 1) * BANK], ACT.Copy).then_inc(cat_hi, 1)

            def squares(hf):
                for j in range(4):
                    n = 4 * hf + j
                    act.wait_ge(ln_centred, n + 1)
                    if n >= 2:
                        act.wait_ge(ln_var, n - 1)
                    act.activation(vtmp[:, j % 2, :], cat[:, 4 + j, hf * BANK:(hf + 1) * BANK],
                                   ACT.Square).then_inc(ln_square, 1)

            def ln_roots(hf):
                act.wait_ge(ln_var, 4 * hf + 4)
                act.activation(rstd[:, hf * BANK:(hf + 1) * BANK], bank[6 + hf][:], ACT.Sqrt, bias=eps[:],
                               scale=1.0 / BANK).then_inc(ln_root, 1)

            def swish_sig(hf):
                for j in range(4):
                    act.wait_ge(ln_normed, 4 * hf + j + 1)
                    if hf:
                        act.wait_ge(ln_out, j + 1)
                    act.activation(lnsg[:, j, :], cat[:, 4 + j, hf * BANK:(hf + 1) * BANK], ACT.Sigmoid,
                                   scale=vec[:, R_LNG + j:R_LNG + j + 1],
                                   bias=vec[:, R_LNB + j:R_LNB + j + 1]).then_inc(ln_sig, 1)

            act.wait_ge(use_dve, (HEADS + 1) * N_UDVE)
            act.wait_ge(mod_turned, 6)
            for j in range(4):
                cat_parts(j, 0)
            squares(0)
            wo_hi(3)
            ln_roots(0)
            squares(1)
            wo_hi(4)
            ln_roots(1)
            wo_hi(5)
            swish_sig(0)
            wo_hi(6)
            for j in range(4, 8):
                act.wait_ge(ln_out, j - 3)
                cat_parts(j, 0)
            wo_hi(7)
            swish_sig(1)
            for j in range(4):
                cat_parts(j, 1)
            for j in range(4, 8):
                act.wait_ge(ln_out, j + 1)
                cat_parts(j, 1)

            def mix_roots(t):
                for n in range(2):
                    act.wait_ge(mix_full, 2 * t + n + 1)
                    if t and n == 0:
                        act.wait_ge(mix_done, t)
                    step(act.activation(mixt[:, n * BANK:(n + 1) * BANK], bank[(2 * t + n) % 4][:], ACT.Square,
                                        accum_out=ss[:, n, t:t + 1]))
                step.wait()
                step(act.activation(rr[:, 0, t:t + 1], ss[:, 0, t:t + 1], ACT.Identity, bias=ss[:, 1, t:t + 1]))
                step.wait()
                act.activation(rr[:, 1, t:t + 1], rr[:, 0, t:t + 1], ACT.Sqrt, bias=eps[:],
                               scale=1.0 / DM).then_inc(mix_root, 1)
                act.wait_ge(mix_done, t + 1)
                if t:
                    act.wait_ge(h2_full, 2 * t)
                step(act.activation(x2t[:].rearrange("p k n -> p (k n)"), x1t[:, t % 3, :], ACT.Square,
                                    accum_out=ss[:, 0, t:t + 1]))
                step.wait()
                act.activation(rr[:, 0, t:t + 1], ss[:, 0, t:t + 1], ACT.Sqrt, bias=eps[:],
                               scale=1.0 / DM).then_inc(x1_root, 1)

            def h2_part(t):
                act.wait_ge(h2_free, 2 * t + 2)
                act.activation(h2T[t // 4][:, 0, :, (t % 4) * P:(t % 4 + 1) * P], h2f[:], ACT.Copy).then_inc(h2_hi, 1)

            def gu_hi(n, j):
                if first(n):
                    act.wait_ge(raw_in[(KT + j) % RAW], 16 * late_fill(KT + j))
                else:
                    act.wait_ge(gu_full, n * 8 + (4 * (j // 2) + 4 - 8))
                    r = (KT + 4 + j) % RAW
                    act.wait_ge(raw_in[r], n * 32 + 16 * (late_fill(KT + 4 + j) - 2))
                act.activation(ffn_part(0, j), raw[:, (KT + j + (0 if first(n) else 4)) % RAW, :],
                               ACT.Copy).then_inc(f_hi, 1)

            def down_hi(n, j):
                if last(n):
                    act.wait_ge(gu_full, n * 8 + 4)
                elif not first(n):
                    act.wait_ge(down_full, n * 16)
                if last(n):
                    late = KT + down_no(n, j)
                    r, fills = late % RAW, late_fill(late) * 16
                else:
                    r = (KT + 8 + j) % RAW
                    fills = n * 32 + 16 * late_fill(KT + 8 + j)
                act.wait_ge(raw_in[r], fills)
                act.activation(ffn_part(0, down_slot(n, j)), raw[:, r, :], ACT.Copy).then_inc(f_hi, 1)

            def act_tile(n, fi, par):
                for hf in range(2):
                    act.wait_ge(gu_full, n * 8 + (4 * fi + 2 * hf + 1))
                    if not (first(n) and fi == 0):
                        act.wait_ge(gu_free, n * 4 + (2 * fi + hf - 1))
                    act.activation(sgm[:, hf, :], bank[2 * hf][:], ACT.Sigmoid).then_inc(gu_sig, 1)
                for hf in range(2):
                    act.wait_ge(gu_free, n * 4 + (2 * fi + hf + 1))
                    if fi == 0 and hf == 0 and not (isinstance(n, int) and n < 2):
                        act.wait_ge(down_full, n * 16 - 16)
                    act.activation(mid[:, par, fi, 0, hf * BANK:(hf + 1) * BANK], mid32[:, hf, :],
                                   ACT.Copy).then_inc(mid_hi, 1)

            def act_round(n, par):
                if not first(n):
                    down_hi(n - 1, 0)
                    down_hi(n - 1, 1)
                for fi in range(2):
                    act_tile(n, fi, par)
                    if not last(n):
                        gu_hi(n + 1, 2 * fi)
                        gu_hi(n + 1, 2 * fi + 1)

            for t in range(XT + 1):
                if t < XT:
                    mix_roots(t)
                if t == XT - 2:
                    act.wait_ge(split_free, 1)
                    gu_hi(0, 0)
                    gu_hi(0, 1)
                if t >= 1:
                    h2_part(t - 1)
            gu_hi(0, 2)
            gu_hi(0, 3)
            act.wait_ge(x2_ready, XT)
            for q in range(3):
                act.wait_ge(x1_store[q], 16 * len(range(q, XT, 3)))
            ffn_rounds(act, act_round)
            down_hi(NGROUP - 1, 0)
            down_hi(NGROUP - 1, 1)

            act.wait_ge(gu_full, 8 * NGROUP)
            for t in range(XT):
                act.wait_ge(down_free, 4 + 16 * (NGROUP - 1) + 2 * t + 2)
                step.wait()
                step(act.activation(junk2[:], y[:, t, :], ACT.Square, accum_out=ss[:, 0, t:t + 1]))
                step.wait()
                act.activation(rr[:, 0, t:t + 1], ss[:, 0, t:t + 1], ACT.Sqrt, bias=eps[:],
                               scale=1.0 / DM).then_inc(y_root, 1)

        @block.gpsimd
        def _(pool):
            def lo_part(lo, full, hi):
                return pool.tensor_tensor(lo, full, hi.bitcast(F32), ALU.subtract)

            def head_lo(s, p):
                pool.wait_ge(w_hi, s * NTILE + (p + 1))
                lo_part(ring[:, SLOT[p], 1], ring_in[:, SLOT[p], 1], ring[:, SLOT[p], 0]).then_inc(w_lo, 1)

            for p in range(2):
                head_lo(0, p)
            for t in range(NT):
                pool.wait_ge(h_hi, t + 1)
                sl = slice(t * P, (t + 1) * P)
                lo_part(hT[:, 1, :, sl], xfull[:, t % 2], hT[:, 0, :, sl]).then_inc(h_lo, 1)
            for p in range(2, NTILE):
                head_lo(0, p)
            with pool.Fori(1, HEADS) as s:
                for p in range(NTILE):
                    head_lo(s, p)

            def wo_lo(i):
                pool.wait_ge(o_hi, i + 1)
                lo_part(wo_part(1, i), raw[:, i % RAW, :], wo_part(0, i)).then_inc(o_lo, 1)

            for n in range(sum(ACT_TAPS_AFTER)):
                out, _, _ = tap_views(conv_sum[:], HEADS - 1, n)
                product, _, _ = tap_views(tap7[:, n % 2], HEADS - 1, n)
                pool.wait_ge(conv_pool, n + 1)
                pool.wait_ge(tap_ready, n + 1)
                pool.tensor_tensor(out, out, product, ALU.add).then_inc(conv_pool, 1)
                for i in range(2):
                    if n + 1 == sum(ACT_TAPS_AFTER[:WO_AT[i] + 1]):
                        wo_lo(i)
            for i in range(2, KT):
                wo_lo(i)
            def ffn_lo(no, r, j):
                pool.wait_ge(f_hi, no + 1)
                lo_part(ffn_part(1, j), raw[:, r, :], ffn_part(0, j)).then_inc(f_lo, 1)

            for t in range(XT):
                if t == XT - 3:
                    ffn_lo(0, KT % RAW, 0)
                    ffn_lo(1, (KT + 1) % RAW, 1)
                pool.wait_ge(h2_hi, t + 1)
                h2, sl = h2T[t // 4], slice((t % 4) * P, (t % 4 + 1) * P)
                lo_part(h2[:, 1, :, sl], h2f[:], h2[:, 0, :, sl]).then_inc(h2_lo, 1)

            for j in range(2, 4):
                ffn_lo(j, (KT + j) % RAW, j)

            def pool_round(n, par):
                if not first(n):
                    for j in range(2):
                        ffn_lo(down_no(n - 1, j), (KT + 2 + j) % RAW, 4 + j)
                if not last(n):
                    for j in range(4):
                        ffn_lo(gu_no(n + 1, j), (KT + 4 + j) % RAW, j)

            ffn_rounds(pool, pool_round)
            for j in range(2):
                no = down_no(NGROUP - 1, j)
                ffn_lo(no, (KT + no) % RAW, down_slot(NGROUP - 1, j))

            for t in range(XT):
                pool.wait_ge(y_normed, t + 1)
                pool.wait_ge(res_in[t], 16)
                pool.tensor_tensor(xres[:, t, :], xres[:, t, :], y[:, t, :], ALU.add).then_inc(y_done, 1)

        @block.vector
        def _(dve):
            step = Steps(dve, dve_step)

            step(dve.memset(ones[:], 1.0))
            step(dve.memset(eps[:], EPS))
            dve.sem_inc(gemm_dve, N_GDVE)
            dve.sem_inc(use_dve, N_UDVE)
            dve.sem_inc(down_free, 4)
            dve.wait_ge(pe_cols, 2)
            dve.wait_ge(sil_sig, 1)
            step(dve.tensor_copy(vec[:], bank[0][:, 0:NVEC]))
            step(dve.tensor_copy(masks[:], mask32[:]))
            step(dve.tensor_copy(taps[:], bank[1][:, 0:4 * TAPS].rearrange("p (j t) -> p j t", t=TAPS)))
            step.wait()
            dve.tensor_tensor(lbt[:, 0, :], vec[:, R_LBF:R_LBF + 8], vec[:, R_LBF:R_LBF + 8],
                              ALU.subtract).then_inc(cols_done, 1)
            dve.tensor_tensor(silc[:].rearrange("p k a -> p a k"), silt[:],
                              vec[:, 0:2 * KT].rearrange("p (a k) -> p a k", a=2), ALU.mult).then_inc(cols_done, 1)
            dve.wait_ge(lb_exp, 1)
            step(dve.reciprocal(lbt[:, 2, :], lbt[:, 1, :]))
            step.wait()
            step(dve.tensor_tensor(lbt[:, 0, :], lbt[:, 1, :], lbt[:, 2, :], ALU.mult))
            step.wait()
            step(dve.tensor_tensor(lb[:, 0, :], lbt[:, 0, :], lbt[:, 0, :], ALU.subtract))
            step.wait()
            step(dve.tensor_scalar(lb[:, 1, :], lb[:, 0, :], -1.0, 1.0, ALU.mult, ALU.add))
            step(dve.tensor_scalar(lb[:, 2, :], lb[:, 0, :], 1.0, -1.0, ALU.mult, ALU.add))

            def norm_x(t):
                dve.wait_ge(x_root, t + 1)
                step(dve.reciprocal(rr[:, 0, t:t + 1], ss[:, 1, t:t + 1]))
                step.wait()
                dve.tensor_scalar(xst[:, t, :], xst[:, t, :], rr[:, 0, t:t + 1], None, ALU.mult).then_inc(xn_ready, 1)

            def mod_take(n):
                m = MODS[n]
                dve.wait_ge(mod_turned, n + 1)
                c0 = (n % 4) * 2 * KT
                dve.tensor_tensor(mod[:, m], bank[7 if n < 2 else 2][:, c0:c0 + 2 * KT].rearrange("p (k a) -> p k a", a=2),
                                  view(vec, R_BM + m * KT, [(1, KT), (0, 2)]), ALU.add).then_inc(mod_done, 1)
                dve.wait_ge(mod_done, n + 1)
                one = mod[:, m, :, 0]
                if m == 1:
                    step(dve.scalar_tensor_tensor(gain[:], mod[:, m], 1.0, view(vec, R_PREM, [(1, KT), (0, 2)]),
                                                  ALU.add, ALU.mult))
                elif m == 4:
                    step(dve.scalar_tensor_tensor(gain2[:], one, 1.0, vec[:, R_PREF:R_PREF + KT], ALU.add, ALU.mult))
                elif m in (2, 5):
                    g, r0 = (0, R_POSTM) if m == 2 else (1, R_POSTF)
                    step(dve.tensor_tensor(gate[:, g], one, vec[:, r0:r0 + KT], ALU.mult))

            norm_x(0)
            norm_x(1)
            mod_take(0)
            mod_take(1)
            step.wait()
            for t in range(NT):
                a = 1 if t < CT else 0
                for k in range(KT):
                    if k % 4 == 0:
                        dve.wait_ge(xp_full, 2 * t + k // 4 + 1)
                    if k == 0 and t >= 2:
                        dve.wait_ge(h_lo, t - 1)
                    ins = dve.tensor_scalar(xfull[:, t % 2, k, :],
                                            bank[LBASE + (2 * t + k // 4) % 4][:, (k % 4) * P:(k % 4 + 1) * P],
                                            gain[:, k, a:a + 1], mod[:, 0, k, a:a + 1], ALU.mult, ALU.add)
                    if k % 4 == 3:
                        ins.then_inc(xp_free, 1)
                if t + 2 < NT:
                    norm_x(t + 2)

            def take(s, u):
                _, kind, n = UNITS[u]
                b = bank[u % GRING]
                sl = slice(n * BANK, (n + 1) * BANK)
                if kind == "g":
                    dve.wait_ge(g_sig, s * 2 + (n + 1))
                    dve.tensor_tensor(cat_tile(s)[:, sl], b[:], cat_tile(s)[:, sl], ALU.mult).then_inc(gemm_dve, 1)
                elif kind == "a":
                    dve.wait_ge(gemm_full, s * NUNIT + (u + 1))
                    dve.wait_ge(gemm_act, s * N_GACT + (N_GACT + 8 + n + 1))
                    c = cat_tile(s + 4)[:, sl]
                    dve.tensor_tensor(c, b[:], c, ALU.mult).then_inc(gemm_dve, 1)

            def conv_start(h):
                dve.wait_ge(gemm_dve, h * N_GDVE + 2 * N_GDVE)
                step.wait(0)
                bias = vec[:, bass.ds(h + R_DWB, 1)]
                conv_last[0] = step(dve.tensor_copy(conv_sum[:], bass.AP(bias.tensor, bias.offset,
                                                                         [list(bias.ap[0]), [0, SEQ]])))

            def conv_tap(h, n):
                out, src, w = tap_views(conv_sum[:], h, n)
                step.wait(conv_last[0])
                conv_last[0] = step(dve.scalar_tensor_tensor(out, src, w, out, ALU.mult, ALU.add))

            def conv_end(h):
                step.wait(conv_last[0])
                c = cat_tile(h + 4)
                step(dve.scalar_tensor_tensor(c, c, tap_weight(h, PAD), conv_sum[:], ALU.mult, ALU.add))

            def part_start():
                dve.wait_ge(gemm_full, HEADS * NUNIT)
                step.wait(0)
                dve.memset(conv_sum[:], 0.0).then_inc(conv_pool, 1)
                dve.wait_ge(gemm_dve, (HEADS + 1) * N_GDVE)
                conv_last[0] = step(dve.tensor_scalar(part7[:], cat[:, 7], tap_weight(3, PAD), vec[:, R_DWB + 3:R_DWB + 4],
                                                      ALU.mult, ALU.add))

            def part_tap(n):
                out, src, w = tap_views(part7[:], HEADS - 1, sum(ACT_TAPS_AFTER) + n)
                step.wait(conv_last[0])
                conv_last[0] = step(dve.scalar_tensor_tensor(out, src, w, out, ALU.mult, ALU.add))

            conv_last = [0]

            def rec_start(h):
                dve.wait_ge(gemm_act, h * N_GACT + (N_GACT + 8))
                for d in range(2):
                    sc = [lb[:, i, bass.ds(h + 4 * d, 1)] for i in range(3)]
                    ins = dve.tensor_scalar(K[:, d], F[:, d], sc[2], sc[1], ALU.mult, ALU.add)
                ins.then_inc(k_ready, 1)
                for d in range(2):
                    sc = [lb[:, i, bass.ds(h + 4 * d, 1)] for i in range(3)]
                    step(dve.tensor_scalar(F[:, d], F[:, d], sc[1], sc[0], ALU.mult, ALU.add))
                step.wait()
                step(dve.tensor_scalar(F[:], F[:], F_MIN, None, ALU.max))
                step.wait()
                dve.tensor_tensor(Q[:, 0], qraw[:], F[:, 1, CTX:], ALU.mult)
                dve.tensor_tensor(Q[:, 1], qraw[:], F[:, 0, CTX:], ALU.mult).then_inc(q_ready, 1)
                step(dve.tensor_tensor(T[:], view(F, 0, [(TOK, 2), (2, TOK // 2)]),
                                       view(F, 1, [(TOK, 2), (2, TOK // 2)]), ALU.mult))

            def rec_level(h, l, part):
                bs = 1 << (l - 1)
                half = TOK // 2
                nk, nq = TOK // (2 * bs), SEQ // (2 * bs)
                if l == 1:
                    kt = view(F, 1, [(TOK - 1, 2), (2, nk), (0, 1)])
                    qt = [view(F, TOK + CTX + 1, [(2, nq), (0, 1)]), view(F, CTX, [(2, nq), (0, 1)])]
                else:
                    kt = view(T, bs // 2, [(half - bs // 2, 2), (bs, nk), (0, bs)])
                    qt = [view(T, half + CTX // 2 + bs // 2, [(bs, nq), (0, bs)]),
                          view(T, CTX // 2, [(bs, nq), (0, bs)])]
                if part == 0:
                    dve.wait_ge(kc_ready, h * LEVELS + l)
                    if l == 1:
                        dve.wait_ge(use_full, h * NUSE + 2)
                    dve.wait_ge(k_ready, h * NK + l)
                    step.wait(t_last[0])
                    kv = view(K, 0, [(TOK + bs, 2), (2 * bs, nk), (1, bs)])
                    dve.tensor_tensor(kv, kv, kt, ALU.mult).then_inc(k_ready, 1)
                    return
                if l == 1:
                    dve.wait_ge(use_act, h * N_UACT + (N_UACT + 2))
                dve.wait_ge(use_full, h * NUSE + (2 * l + 2))
                dve.wait_ge(q_ready, h * NK + l)
                for i in range(2):
                    qv = view(Q, i * (SEQ + bs), [(2 * bs, nq), (1, bs)])
                    ins = dve.tensor_tensor(qv, qv, qt[i], ALU.mult)
                ins.then_inc(q_ready, 1)
                if l > 1:
                    dve.wait_ge(k_ready, h * NK + (l + 1))
                    dve.wait_ge(q_ready, h * NK + (l + 1))
                    tv = view(T, 0, [(half, 2), (bs, nk)])
                    t_last[0] = step(dve.tensor_tensor(tv, tv, view(T, bs // 2, [(half, 2), (bs, nk)]), ALU.mult))
                for hf in range(2):
                    dve.copy_predicated(view(AT, hf * BANK, [(P, 4), (1, P)]), view(masks, (l - 1) * P, [(0, 4), (1, P)]),
                                        bank[LBASE + (2 * l + hf) % LRING][:].rearrange("p (c n) -> p c n", n=P)
                                        ).then_inc(use_dve, 1)

            t_last = [0]

            def rec_states(h, g):
                for d in range(2):
                    i = USES.index(("outer", g, d))
                    dve.wait_ge(use_full, h * NUSE + (i + 1))
                    for j in range(3):
                        n = 3 * g + j
                        src = bank[LBASE + i % LRING][:, j * P:(j + 1) * P]
                        dst = S[:, d, n - 1 if n else XT - 1]
                        done = 6 * g + 3 * d + j
                        if n == 0:
                            ins = dve.tensor_copy(dst, src)
                        else:
                            prev = done - 1 if j else done - 4
                            dve.wait_ge(state_done, h * NSTATE + (prev + 1))
                            if n == 1 and d == 0:
                                step.wait(t_last[0])
                            ch = scan_chunk(d, n)
                            ins = dve.scalar_tensor_tensor(dst, S[:, d, n - 2 if n > 1 else XT - 1],
                                                           T[:, d, ch * (P // 2):ch * (P // 2) + 1], src,
                                                           ALU.mult, ALU.add)
                        ins.then_inc(state_done, 1)
                    dve.wait_ge(state_done, h * NSTATE + (6 * g + 3 * d + 3))
                    dve.sem_inc(use_dve, 1)

            def rec_out(h, u):
                if u == OUT_AT:
                    for hf in range(2):
                        dve.wait_ge(sq_ready, h * 2 + (hf + 1))
                        dve.wait_ge(gemm_dve, h * N_GDVE + (N_GDVE + 2))
                        i = USES.index(("o", hf, 0))
                        c = cat_tile(h)[:, hf * BANK:(hf + 1) * BANK]
                        dve.scalar_tensor_tensor(c, bank[LBASE + i % LRING][:], vec[:, R_ON:R_ON + 1], c,
                                                 ALU.mult, ALU.mult).then_inc(use_dve, 1)
                elif u == OUT_AT + 1:
                    dve.wait_ge(use_act, h * N_UACT + 2 * N_UACT)
                    dve.reciprocal(hss[:, 1, :], hss[:, 0, :]).then_inc(rs_ready, 1)
                elif u == OUT_AT + 2:
                    for hf in range(2):
                        i = USES.index(("rb", hf, 0))
                        dve.wait_ge(use_full, h * NUSE + (i + 1))
                        dve.wait_ge(use_dve, h * N_UDVE + (2 * N_UDVE - 3 + hf))
                        c = cat_tile(h)[:, hf * BANK:(hf + 1) * BANK]
                        dve.tensor_tensor(c, bank[LBASE + i % LRING][:], c, ALU.mult).then_inc(use_dve, 1)

            MOD_TAKE = {6: 2, 9: 3, 13: 4, 14: 5}

            def dve_body(s, gemm, rec):
                h = s - 1
                for u in range(NUNIT):
                    if gemm:
                        take(s, u)
                    level = LEVEL_AT.index(u) if u in LEVEL_AT else 0
                    if u == 0:
                        rec_start(h)
                        t_last[0] = step.n
                        if gemm:
                            conv_start(h)
                    elif level:
                        rec_level(h, level, 0)
                    if u == 1 and not gemm:
                        part_start()
                    for n in taps_after(TAPS_AFTER if gemm else DVE_TAPS_AFTER, u):
                        if gemm:
                            conv_tap(h, n)
                        else:
                            part_tap(n)
                    if level:
                        rec_level(h, level, 1)
                    elif OUTER_AT <= u < OUTER_AT + SCAN:
                        rec_states(h, u - OUTER_AT)
                    else:
                        rec_out(h, u)
                    if not gemm and u in MOD_TAKE:
                        mod_take(MOD_TAKE[u])
                    if gemm and u == len(TAPS_AFTER) - 1:
                        conv_end(h)

            for u in range(NUNIT):
                take(0, u)
            base = step.n
            with dve.Fori(1, HEADS) as s:
                step.base, step.n = s * BODY_STEPS + (base - BODY_STEPS), 0
                dve_body(s, True, True)
                assert step.n == BODY_STEPS, step.n
            step.base, step.n = base + (HEADS - 1) * BODY_STEPS, 0
            dve_body(HEADS, False, True)

            dve.wait_ge(conv_pool, sum(ACT_TAPS_AFTER) + 1)
            step.wait()
            dve.tensor_tensor(cat[:, 7], conv_sum[:], part7[:], ALU.add).then_inc(conv_done, 1)

            def centre(hf):
                dve.wait_ge(ln_sum, 2)
                for j in range(4):
                    c = cat[:, 4 + j, hf * BANK:(hf + 1) * BANK]
                    dve.scalar_tensor_tensor(c, bank[4 + hf][:], -1.0 / BANK, c, ALU.mult, ALU.add).then_inc(ln_centred, 1)

            def cat_part(j, hf):
                dve.wait_ge(cat_hi, hf * KT + j + 1)
                dve.tensor_tensor(catS[:, hf, 1, j, :], cat[:, j, hf * BANK:(hf + 1) * BANK],
                                  catS[:, hf, 0, j, :].bitcast(F32), ALU.subtract).then_inc(cat_lo, 1)

            def rstds(hf):
                dve.wait_ge(ln_root, hf + 1)
                r = rstd[:, hf * BANK:(hf + 1) * BANK]
                dve.reciprocal(r, r).then_inc(ln_rstd, 1)

            def normed(hf):
                dve.wait_ge(ln_rstd, hf + 1)
                for j in range(4):
                    c = cat[:, 4 + j, hf * BANK:(hf + 1) * BANK]
                    dve.tensor_tensor(c, c, rstd[:, hf * BANK:(hf + 1) * BANK], ALU.mult).then_inc(ln_normed, 1)

            def swish(hf):
                for j in range(4):
                    c = cat[:, 4 + j, hf * BANK:(hf + 1) * BANK]
                    dve.wait_ge(ln_sig, 4 * hf + j + 1)
                    dve.wait_ge(ln_normed, 4 * hf + j + 1)
                    step(dve.tensor_scalar(c, c, vec[:, R_LNG + j:R_LNG + j + 1], vec[:, R_LNB + j:R_LNB + j + 1],
                                           ALU.mult, ALU.add))
                    step.wait()
                    dve.tensor_tensor(c, c, lnsg[:, j, :], ALU.mult).then_inc(ln_out, 1)

            centre(0)
            for j in range(4):
                cat_part(j, 0)
            centre(1)
            rstds(0)
            normed(0)
            rstds(1)
            swish(0)
            for j in range(4, 8):
                cat_part(j, 0)
            normed(1)
            swish(1)
            for j in range(8):
                cat_part(j, 1)
            dve.wait_ge(g_full, 1)
            for q in range(2):
                step(dve.tensor_copy(Gb[:, q * BANK:(q + 1) * BANK], bank[4 + q][:]))
            step.wait()
            dve.sem_inc(g_done, 1)

            def x1(t):
                dve.wait_ge(mix_root, t + 1)
                step(dve.reciprocal(rr[:, 1, t:t + 1], rr[:, 1, t:t + 1]))
                step.wait()
                for n in range(2):
                    sl = slice(n * BANK, (n + 1) * BANK)
                    step(dve.scalar_tensor_tensor(mixt[:, sl], bank[(2 * t + n) % 4][:], rr[:, 1, t:t + 1], Gb[:, sl],
                                                  ALU.mult, ALU.mult))
                step.wait()
                dve.wait_ge(x1_in[t % 3], 16 * (t // 3 + 1))
                dve.tensor_tensor(x1t[:, t % 3, :], x1t[:, t % 3, :], mixt[:], ALU.add).then_inc(mix_done, 1)
                dve.wait_ge(x1_root, t + 1)
                step(dve.reciprocal(rr[:, 0, t:t + 1], rr[:, 0, t:t + 1]))
                step.wait()
                dve.tensor_scalar(x2t[:].rearrange("p k n -> p (k n)"), x1t[:, t % 3, :], rr[:, 0, t:t + 1], None,
                                  ALU.mult).then_inc(x2_ready, 1)

            def h2(t):
                for k in range(KT):
                    if k % 4 == 0:
                        dve.wait_ge(h2_full, 2 * t + k // 4 + 1)
                    if k == 0 and t:
                        dve.wait_ge(h2_lo, t)
                    ins = dve.tensor_scalar(h2f[:, k, :], bank[6 + k // 4][:, (k % 4) * P:(k % 4 + 1) * P],
                                            gain2[:, k:k + 1], mod[:, 3, k, 0:1], ALU.mult, ALU.add)
                    if k % 4 == 3:
                        ins.then_inc(h2_free, 1)

            for t in range(XT + 1):
                if t < XT:
                    x1(t)
                if t >= 1:
                    h2(t - 1)
            dve.wait_ge(g_full, 2)
            for q in range(2):
                step(dve.tensor_copy(Gb[:, q * BANK:(q + 1) * BANK], bank[4 + q][:]))
            step.wait()
            dve.sem_inc(g_done, 1)

            def dve_tile(n, fi, par):
                for hf in range(2):
                    i = n * 4 + (2 * fi + hf + 1)
                    dve.wait_ge(gu_sig, i)
                    if not (first(n) and fi == 0):
                        dve.wait_ge(mid_lo, i - 2)
                    dve.tensor_tensor(mid32[:, hf, :], bank[2 * hf][:], sgm[:, hf, :], ALU.mult).then_inc(gu_part, 1)
                    dve.wait_ge(gu_part, i)
                    dve.wait_ge(gu_full, n * 8 + (4 * fi + 2 * hf + 2))
                    dve.tensor_tensor(mid32[:, hf, :], bank[2 * hf + 1][:], mid32[:, hf, :], ALU.mult).then_inc(gu_free, 1)
                for hf in range(2):
                    i = n * 4 + (2 * fi + hf + 1)
                    dve.wait_ge(gu_free, i)
                    dve.wait_ge(mid_hi, i)
                    sl = slice(hf * BANK, (hf + 1) * BANK)
                    dve.tensor_tensor(mid[:, par, fi, 1, sl], mid32[:, hf, :], mid[:, par, fi, 0, sl].bitcast(F32),
                                      ALU.subtract).then_inc(mid_lo, 1)

            def dve_down(n, t):
                for i in (2 * t, 2 * t + 1):
                    hf = i % 2
                    sl = slice(hf * BANK, (hf + 1) * BANK)
                    dve.wait_ge(down_full, n * 16 + (i + 1))
                    if first(n):
                        ins = dve.tensor_copy(y[:, t, sl], bank[4 + i % 4][:])
                    else:
                        dve.wait_ge(down_free, n * 16 + (i + 1 - 12))
                        ins = dve.tensor_tensor(y[:, t, sl], bank[4 + i % 4][:], y[:, t, sl], ALU.add)
                    ins.then_inc(down_free, 1)

            def dve_round(n, par):
                dve_tile(n, 0, par)
                dve_tile(n, 1, par)
                if not first(n):
                    for t in range(XT):
                        dve_down(n - 1, t)

            dve.wait_ge(h2_lo, XT)
            ffn_rounds(dve, dve_round)
            for t in range(XT + 1):
                if t < XT:
                    dve_down(NGROUP - 1, t)
                if t:
                    dve.wait_ge(y_root, t)
                    step(dve.reciprocal(rr[:, 1, t - 1:t], rr[:, 0, t - 1:t]))
                    step.wait()
                    dve.scalar_tensor_tensor(y[:, t - 1, :], y[:, t - 1, :], rr[:, 1, t - 1:t], Gb[:], ALU.mult,
                                             ALU.mult).then_inc(y_normed, 1)


MATRICES = ["x", "ctx", "w_mod", "w_in", "w_out", "ffn_w_gate", "ffn_w_up", "ffn_w_down", "conv_dw_w"]
VECTORS = ["c", "c_ctx", "b_mod", "pre_mix_g", "pre_ffn_g", "post_mix_g", "post_ffn_g", "hgrn_lb_fwd",
           "hgrn_lb_bwd", "conv_dw_b", "conv_ln_g", "conv_ln_b", "hgrn_onorm_g"]


def shape_constants():
    i = np.arange(P)
    xor = i[:, None] ^ i[None, :]
    masks = np.stack([(xor >= 1 << l) & (xor < 2 << l) for l in range(LEVELS)], 1).astype(np.float32)
    return {"ident": np.eye(P, dtype=np.float32), "masks": masks}


def lay_out(inputs):
    arrays = {f"in_{n}": np.ascontiguousarray(inputs[n]) for n in MATRICES}
    arrays["vectors"] = np.concatenate([np.reshape(inputs[n], (-1, P)) for n in VECTORS])
    arrays.update(shape_constants())
    return arrays


def kernel(**inputs):
    import concourse.bacc as bacc
    from concourse.bass_utils import run_bass_kernel_spmd

    nc = bacc.Bacc("TRN2", target_bir_lowering=False, num_devices=1)
    arrays = lay_out(inputs)
    args = [nc.dram_tensor(n, list(a.shape), mybir.dt.from_np(a.dtype), kind="ExternalInput").ap()
            for n, a in arrays.items()]
    args.append(nc.dram_tensor("out", [1, SEQ, DM], F32, kind="ExternalOutput").ap())
    kernel_program(nc, *args)
    return run_bass_kernel_spmd(nc, [arrays], core_ids=[0]).results[0]["out"]
```
